# Optimizing a Trainium2 kernel written in Bass

```python
import math
import jax, jax.numpy as jnp
from jax import lax
import numpy as np

D_MODEL = 1024
BATCH = 1
SEQ = 512
DEPTH = 2
DEC_BATCH = 8
DEC_SEQ = 8
PAST_LEN = 512
PAGE_SIZE = 128

HEAD_DIM = 64
ML_HEADS = 4
RW_HEADS = 4
NSA_HEADS = 8
NSA_KV_HEADS = 2
NSA_GROUP = NSA_HEADS // NSA_KV_HEADS
ML_WIDTH = ML_HEADS * HEAD_DIM
RW_WIDTH = RW_HEADS * HEAD_DIM
NSA_WIDTH = NSA_HEADS * HEAD_DIM
KV_WIDTH = NSA_KV_HEADS * HEAD_DIM
MIX_WIDTH = ML_WIDTH + RW_WIDTH + NSA_WIDTH
ML_CHUNK = 64
ML_CONV = 4
ML_NORM_EPS = 1e-6
RW_LORA_W = 64
RW_LORA_A = 64
RW_LORA_G = 128
RW_GN_EPS = 64e-5
CMP_LEN = 32
CMP_STRIDE = 16
CMP_HID = 128
SEL_BLOCK = 64
SEL_TOPN = 8
WINDOW = 512
Q_BLOCK = 64
ROPE_THETA = 10000.0
D_FF = 2816
N_EXPERTS = 8
TOP_K = 2
D_EXP = 1408
RMS_EPS = 1e-6
NEG = -1e30
SEL_NEG = -1e9
FORCE_BONUS = 1e3
ML_COLS = 4 * ML_WIDTH + 2 * ML_HEADS
RW_COLS = 3 * RW_WIDTH + RW_LORA_W + RW_LORA_A + RW_LORA_G
NSA_COLS = NSA_WIDTH + 6 * KV_WIDTH + 3 * NSA_HEADS
N_IN = ML_COLS + RW_COLS + NSA_COLS

kernel_name = 'hybrid_mlstm_rwkv7_nsa_step'

def split_cols(a, sizes):
    out, s = [], 0
    for n in sizes:
        out.append(a[..., s:s + n])
        s += n
    return out

def heads(a, h):
    return a.reshape(a.shape[:2] + (h, HEAD_DIM))

def rmsnorm(x, w):
    xf = x.astype(jnp.float32)
    y = xf * lax.rsqrt(jnp.mean(xf * xf, axis=-1, keepdims=True) + RMS_EPS)
    return (y * w.astype(jnp.float32)).astype(x.dtype)

def head_norm(h, w, eps):
    hf = h.astype(jnp.float32)
    mu = jnp.mean(hf, -1, keepdims=True)
    var = jnp.mean(jnp.square(hf - mu), -1, keepdims=True)
    y = ((hf - mu) * lax.rsqrt(var + eps)).reshape(h.shape[:2] + (-1,))
    return y * w.astype(jnp.float32)

def rope(x, pos):
    half = HEAD_DIM // 2
    inv = ROPE_THETA ** (-jnp.arange(half, dtype=jnp.float32) / half)
    ang = pos.astype(jnp.float32)[:, None] * inv[None, :]
    cos = jnp.cos(ang)[None, :, None, :]
    sin = jnp.sin(ang)[None, :, None, :]
    x1 = x[..., :half].astype(jnp.float32)
    x2 = x[..., half:].astype(jnp.float32)
    return jnp.concatenate([x1 * cos - x2 * sin, x2 * cos + x1 * sin], -1).astype(x.dtype)

def masked_softmax(s, mask):
    s = jnp.where(mask, s.astype(jnp.float32), NEG)
    m = jnp.max(s, axis=-1, keepdims=True)
    p = jnp.exp(s - m) * mask
    return p / jnp.maximum(jnp.sum(p, -1, keepdims=True), 1e-30)

def last_rows(a, n):
    length = a.shape[1]
    if length >= n:
        return a[:, length - n:]
    return jnp.pad(a, ((0, 0), (n - length, 0)) + ((0, 0),) * (a.ndim - 2))

def causal_conv(x, buf, w, b):
    t = x.shape[1]
    xp = jnp.concatenate([buf.astype(x.dtype), x], 1)
    y = b
    for j in range(ML_CONV):
        y = y + xp[:, j:j + t] * w[j]
    return y, xp[:, -(ML_CONV - 1):]

def mlstm_chunkwise(q, k, v, ig, fg, C0, n0, m0):
    f32 = jnp.float32
    B, T, H, Dh = q.shape
    L = math.gcd(T, ML_CHUNK)
    NC = T // L

    def chunks(a):
        a = a.astype(f32).reshape((B, NC, L, H) + a.shape[3:])
        return jnp.moveaxis(a, (1, 3), (0, 2))

    xs = (chunks(q), chunks(k), chunks(v), chunks(ig), jax.nn.log_sigmoid(chunks(fg)))
    causal = jnp.tril(jnp.ones((L, L), bool))

    def step(carry, inp):
        C, n, m = carry
        qb, kb, vb, ib, lf = inp
        b = jnp.cumsum(lf, axis=-1)
        a = ib - b
        m_t = jnp.maximum(b + m[..., None], b + lax.cummax(a, axis=2))
        logd = jnp.where(causal, b[..., :, None] + a[..., None, :] - m_t[..., :, None], -jnp.inf)
        S = jnp.einsum('bhtd,bhsd->bhts', qb, kb) * jnp.exp(logd)
        inter = jnp.exp(b + m[..., None] - m_t)
        num = inter[..., None] * jnp.einsum('bhvd,bhtd->bhtv', C, qb) + jnp.einsum('bhts,bhsv->bhtv', S, vb)
        den = inter * jnp.einsum('bhd,bhtd->bht', n, qb) + jnp.sum(S, -1)
        h = num / jnp.maximum(jnp.abs(den), jnp.exp(-m_t))[..., None]
        m_new = m_t[..., -1]
        wgt = jnp.exp(b[..., -1:] + a - m_new[..., None])
        dec = jnp.exp(b[..., -1] + m - m_new)
        C_new = dec[..., None, None] * C + jnp.einsum('bhs,bhsv,bhsd->bhvd', wgt, vb, kb)
        n_new = dec[..., None] * n + jnp.einsum('bhs,bhsd->bhd', wgt, kb)
        return (C_new, n_new, m_new), h

    (C, n, m), hs = lax.scan(step, (C0.astype(f32), n0.astype(f32), m0.astype(f32)), xs)
    h = jnp.moveaxis(hs, (0, 2), (1, 3)).reshape(B, T, H, Dh)
    return h, C, n, m

def rwkv7_scan(r, w, k, v, kk, a, S0):
    def step(S, inp):
        rt, wt, kt, vt, kkt, at = inp
        sa = jnp.einsum('bhvk,bhk->bhv', S, kkt)
        S = S * wt[:, :, None, :] - sa[..., None] * (at * kkt)[:, :, None, :] + vt[..., None] * kt[:, :, None, :]
        return S, jnp.einsum('bhvk,bhk->bhv', S, rt)

    xs = tuple(jnp.moveaxis(t.astype(jnp.float32), 1, 0) for t in (r, w, k, v, kk, a))
    S, ys = lax.scan(step, S0.astype(jnp.float32), xs)
    return jnp.moveaxis(ys, 0, 1), S

def nsa_attend(q, q_rot, gates, kv_full, win_kv, offset, cmp_pos, cmp_w1, cmp_w2):
    B, T = q.shape[:2]
    P = kv_full.shape[1]
    Lbuf = win_kv.shape[1] - T
    dt = q.dtype
    scale = HEAD_DIM ** -0.5
    KVH, G = NSA_KV_HEADS, NSA_GROUP
    NC = (P - CMP_LEN) // CMP_STRIDE + 1
    cidx = np.arange(NC)[:, None] * CMP_STRIDE + np.arange(CMP_LEN)[None, :]
    blocks = kv_full[:, cidx, :2]
    blocks = blocks + jnp.transpose(cmp_pos, (1, 0, 2))[None, None, :, :, None, :]
    blocks = jnp.moveaxis(blocks, 2, 4).reshape(B, NC, 2, KVH, CMP_LEN * HEAD_DIM)
    hid = jax.nn.silu(jnp.einsum('bcjgf,jfe->bcjge', blocks, cmp_w1))
    ckv = jnp.einsum('bcjge,jed->bcjgd', hid, cmp_w2)
    ck, cv = ckv[:, :, 0], ckv[:, :, 1]
    cmp_end = jnp.asarray(np.arange(NC) * CMP_STRIDE + CMP_LEN - 1)
    NS = -(-P // SEL_BLOCK)
    cs = np.arange(NC) * CMP_STRIDE
    ss = np.arange(NS) * SEL_BLOCK
    ov = np.clip(np.minimum(cs[:, None] + CMP_LEN, ss[None, :] + SEL_BLOCK) - np.maximum(cs[:, None], ss[None, :]), 0, None) / CMP_LEN
    ov = jnp.asarray(ov, jnp.float32)
    slc = jnp.pad(kv_full[:, :, 2:], ((0, 0), (0, NS * SEL_BLOCK - P), (0, 0), (0, 0), (0, 0)))
    slc = slc.reshape(B, NS, SEL_BLOCK, 2, KVH, HEAD_DIM).transpose(0, 4, 1, 2, 3, 5)
    K_SEL = min(SEL_TOPN, NS)
    wpad = jnp.pad(win_kv, ((0, 0), (WINDOW, 0), (0, 0), (0, 0), (0, 0)))
    QB = math.gcd(T, Q_BLOCK)
    NB = T // QB
    qg = q.reshape(B, T, KVH, G, HEAD_DIM)
    qrg = q_rot.reshape(B, T, KVH, G, HEAD_DIM)
    gg = gates.reshape(B, T, KVH, G, 3)
    bi = jnp.arange(B)[:, None, None, None]
    gi = jnp.arange(KVH)[None, None, :, None]
    blk = jnp.arange(NS)

    def block(nb):
        qs = nb * QB
        tpos = offset + qs + jnp.arange(QB)
        qb = lax.dynamic_slice_in_dim(qg, qs, QB, 1)
        qrb = lax.dynamic_slice_in_dim(qrg, qs, QB, 1)
        s_c = jnp.einsum('bqghd,bcgd->bqghc', qb, ck) * scale
        p_c = masked_softmax(s_c, (cmp_end[None, :] <= tpos[:, None])[None, :, None, None, :])
        o_c = jnp.einsum('bqghc,bcgd->bqghd', p_c.astype(dt), cv)
        imp = jnp.einsum('bqghc,cs->bqgs', p_c, ov)
        cur = tpos // SEL_BLOCK
        avail = (blk[None, :] * SEL_BLOCK <= tpos[:, None])[None, :, None, :]
        forced = ((blk[None, :] == 0) | (blk[None, :] == cur[:, None]) | (blk[None, :] == cur[:, None] - 1))[None, :, None, :]
        score = jnp.where(avail, imp + jnp.where(forced, FORCE_BONUS, 0.0), SEL_NEG)
        top_v, top_i = lax.top_k(score, K_SEL)
        valid = top_v > 0.5 * SEL_NEG
        sk = slc[bi, gi, top_i]
        kpos = top_i[..., None] * SEL_BLOCK + jnp.arange(SEL_BLOCK)
        mask_s = valid[..., None] & (kpos <= tpos[None, :, None, None, None])
        s_s = jnp.einsum('bqghd,bqgksd->bqghks', qrb, sk[..., 0, :]) * scale
        p_s = masked_softmax(s_s.reshape(B, QB, KVH, G, K_SEL * SEL_BLOCK),
                             mask_s.reshape(B, QB, KVH, 1, K_SEL * SEL_BLOCK)).reshape(s_s.shape)
        o_s = jnp.einsum('bqghks,bqgksd->bqghd', p_s.astype(dt), sk[..., 1, :])
        wk = lax.dynamic_slice_in_dim(wpad, qs + Lbuf, WINDOW + QB, 1)
        ridx = qs + Lbuf + jnp.arange(WINDOW + QB)
        wpos = offset - Lbuf - WINDOW + ridx
        dlt = tpos[:, None] - wpos[None, :]
        mask_w = (ridx >= WINDOW)[None, :] & (dlt >= 0) & (dlt < WINDOW)
        s_w = jnp.einsum('bqghd,bjgd->bqghj', qrb, wk[:, :, 0]) * scale
        p_w = masked_softmax(s_w, mask_w[None, :, None, None, :])
        o_w = jnp.einsum('bqghj,bjgd->bqghd', p_w.astype(dt), wk[:, :, 1])
        gb = lax.dynamic_slice_in_dim(gg, qs, QB, 1)
        return gb[..., 0:1] * o_c + gb[..., 1:2] * o_s + gb[..., 2:3] * o_w

    out = lax.map(block, jnp.arange(NB))
    return jnp.moveaxis(out, 0, 1).reshape(B, T, NSA_WIDTH)

def swiglu(x, w1, w3, w2):
    return (jax.nn.silu(x @ w1) * (x @ w3)) @ w2

def setup_inputs(seed: int = 0) -> dict:
    key = jax.random.key(seed)
    ks = iter(jax.random.split(key, 64))
    f32 = jnp.float32

    def nrm(shape, scale=1.0):
        return jax.random.normal(next(ks), shape, f32) * scale

    def uni(shape, lo, hi):
        return jax.random.uniform(next(ks), shape, f32, lo, hi)

    n_pages = PAST_LEN // PAGE_SIZE
    n_pool = (DEC_BATCH * n_pages * 5) // 4
    wbuf = min(WINDOW, PAST_LEN)
    n_dense = (DEPTH + 1) // 2
    n_moe = DEPTH // 2
    page_table = jax.random.permutation(next(ks), n_pool)[:DEC_BATCH * n_pages].reshape(DEC_BATCH, n_pages).astype(jnp.int32)
    return {
        'x_prompt': nrm((BATCH, SEQ, D_MODEL)),
        'x_sample': nrm((DEC_BATCH, DEC_SEQ, D_MODEL)),
        'cache_nsa_kv': nrm((DEPTH, n_pool, PAGE_SIZE, 4, NSA_KV_HEADS, HEAD_DIM)),
        'cache_win_kv': nrm((DEPTH, DEC_BATCH, wbuf, 2, NSA_KV_HEADS, HEAD_DIM)),
        'state_mlstm_C': nrm((DEPTH, DEC_BATCH, ML_HEADS, HEAD_DIM, HEAD_DIM), 0.3),
        'state_mlstm_n': nrm((DEPTH, DEC_BATCH, ML_HEADS, HEAD_DIM), 0.3),
        'state_mlstm_m': nrm((DEPTH, DEC_BATCH, ML_HEADS), 0.5),
        'state_mlstm_conv': nrm((DEPTH, DEC_BATCH, ML_CONV - 1, 2 * ML_WIDTH)),
        'state_rwkv_S': nrm((DEPTH, DEC_BATCH, RW_HEADS, HEAD_DIM, HEAD_DIM), 0.3),
        'state_rwkv_shift': nrm((DEPTH, DEC_BATCH, RW_COLS)),
        'page_table': page_table,
        'norm_mix_w': 1.0 + nrm((DEPTH, D_MODEL), 0.1),
        'w_in': nrm((DEPTH, D_MODEL, N_IN), D_MODEL ** -0.5),
        'ml_conv_w': nrm((DEPTH, ML_CONV, 2 * ML_WIDTH), ML_CONV ** -0.5),
        'ml_conv_b': nrm((DEPTH, 2 * ML_WIDTH), 0.02),
        'ml_b_i': nrm((DEPTH, ML_HEADS), 0.1),
        'ml_b_f': jnp.linspace(3.0, 6.0, ML_HEADS, dtype=f32)[None, :] + nrm((DEPTH, ML_HEADS), 0.1),
        'ml_norm_w': 1.0 + nrm((DEPTH, ML_WIDTH), 0.1),
        'rw_mu': uni((DEPTH, RW_COLS), 0.0, 1.0),
        'rw_w0': uni((DEPTH, RW_WIDTH), -6.0, 1.0),
        'rw_w2': nrm((DEPTH, RW_LORA_W, RW_WIDTH), 0.5 * RW_LORA_W ** -0.5),
        'rw_a0': nrm((DEPTH, RW_WIDTH), 0.1),
        'rw_a2': nrm((DEPTH, RW_LORA_A, RW_WIDTH), 0.5 * RW_LORA_A ** -0.5),
        'rw_g2': nrm((DEPTH, RW_LORA_G, RW_WIDTH), RW_LORA_G ** -0.5),
        'rw_k_k': 0.85 + nrm((DEPTH, RW_WIDTH), 0.05),
        'rw_k_a': 1.0 + nrm((DEPTH, RW_WIDTH), 0.05),
        'rw_r_k': nrm((DEPTH, RW_HEADS, HEAD_DIM), 0.1),
        'rw_ln_w': 1.0 + nrm((DEPTH, RW_WIDTH), 0.1),
        'rw_ln_b': nrm((DEPTH, RW_WIDTH), 0.02),
        'nsa_cmp_pos': nrm((DEPTH, 2, CMP_LEN, HEAD_DIM), 0.1),
        'nsa_cmp_w1': nrm((DEPTH, 2, CMP_LEN * HEAD_DIM, CMP_HID), (CMP_LEN * HEAD_DIM) ** -0.5),
        'nsa_cmp_w2': nrm((DEPTH, 2, CMP_HID, HEAD_DIM), CMP_HID ** -0.5),
        'w_out': nrm((DEPTH, MIX_WIDTH, D_MODEL), MIX_WIDTH ** -0.5),
        'norm_ffn_w': 1.0 + nrm((DEPTH, D_MODEL), 0.1),
        'ffn_w1': nrm((n_dense, D_MODEL, D_FF), D_MODEL ** -0.5),
        'ffn_w3': nrm((n_dense, D_MODEL, D_FF), D_MODEL ** -0.5),
        'ffn_w2': nrm((n_dense, D_FF, D_MODEL), D_FF ** -0.5),
        'moe_router': nrm((n_moe, D_MODEL, N_EXPERTS), D_MODEL ** -0.5),
        'moe_w1': nrm((n_moe, N_EXPERTS, D_MODEL, D_EXP), D_MODEL ** -0.5),
        'moe_w3': nrm((n_moe, N_EXPERTS, D_MODEL, D_EXP), D_MODEL ** -0.5),
        'moe_w2': nrm((n_moe, N_EXPERTS, D_EXP, D_MODEL), D_EXP ** -0.5),
        'norm_final_w': 1.0 + nrm((D_MODEL,), 0.1),
    }

def reference(x_prompt, x_sample, cache_nsa_kv, cache_win_kv, state_mlstm_C, state_mlstm_n, state_mlstm_m,
              state_mlstm_conv, state_rwkv_S, state_rwkv_shift, page_table, norm_mix_w, w_in, ml_conv_w,
              ml_conv_b, ml_b_i, ml_b_f, ml_norm_w, rw_mu, rw_w0, rw_w2, rw_a0, rw_a2, rw_g2, rw_k_k, rw_k_a,
              rw_r_k, rw_ln_w, rw_ln_b, nsa_cmp_pos, nsa_cmp_w1, nsa_cmp_w2, w_out, norm_ffn_w, ffn_w1, ffn_w3,
              ffn_w2, moe_router, moe_w1, moe_w3, moe_w2, norm_final_w):
    f32 = jnp.float32
    wbuf = min(WINDOW, PAST_LEN)

    def moe(x, e_layer):
        B, T, D = x.shape
        xf = x.reshape(B * T, D)
        logits = (xf @ moe_router[e_layer]).astype(f32)
        top_v, top_i = lax.top_k(logits, TOP_K)
        gw = jax.nn.softmax(top_v, axis=-1)
        comb = jnp.sum(jax.nn.one_hot(top_i, N_EXPERTS, dtype=f32) * gw[..., None], axis=1)
        y = jnp.zeros_like(xf)
        for e in range(N_EXPERTS):
            y = y + comb[:, e:e + 1].astype(x.dtype) * swiglu(xf, moe_w1[e_layer, e], moe_w3[e_layer, e], moe_w2[e_layer, e])
        return y.reshape(B, T, D)

    def layer(l, x, offset, st):
        C0, n0, m0, conv0, S0, shift0, past_kv, win0 = st
        B, T, _ = x.shape
        dt = x.dtype
        pos = offset + jnp.arange(T)
        xn = rmsnorm(x, norm_mix_w[l])
        cols = xn @ w_in[l]
        ml_c, rw_c, ns_c = split_cols(cols, (ML_COLS, RW_COLS, NSA_COLS))
        qk_pre, ml_v, ml_o, ml_i, ml_f = split_cols(ml_c, (2 * ML_WIDTH, ML_WIDTH, ML_WIDTH, ML_HEADS, ML_HEADS))
        qk, conv_new = causal_conv(qk_pre, conv0, ml_conv_w[l], ml_conv_b[l])
        qk = jax.nn.silu(qk)
        h_ml, C, n, m = mlstm_chunkwise(heads(qk[..., :ML_WIDTH], ML_HEADS),
                                        heads(qk[..., ML_WIDTH:], ML_HEADS) * HEAD_DIM ** -0.5,
                                        heads(ml_v, ML_HEADS), ml_i + ml_b_i[l], ml_f + ml_b_f[l], C0, n0, m0)
        h_ml = head_norm(h_ml, ml_norm_w[l], ML_NORM_EPS) * jax.nn.sigmoid(ml_o.astype(f32))
        prev = jnp.concatenate([shift0[:, None].astype(rw_c.dtype), rw_c[:, :-1]], 1)
        xm = rw_c + (prev - rw_c) * rw_mu[l]
        shift_new = rw_c[:, -1]
        r, wl, k, v, al, gl = split_cols(xm, (RW_WIDTH, RW_LORA_W, RW_WIDTH, RW_WIDTH, RW_LORA_A, RW_LORA_G))
        wpre = (rw_w0[l] + jnp.tanh(wl) @ rw_w2[l]).astype(f32)
        decay = jnp.exp(-jnp.exp(-jax.nn.softplus(-wpre) - 0.5))
        a = jax.nn.sigmoid((rw_a0[l] + al @ rw_a2[l]).astype(f32))
        g = jax.nn.sigmoid(gl) @ rw_g2[l]
        kk = heads((k * rw_k_k[l]).astype(f32), RW_HEADS)
        kk = kk / jnp.maximum(jnp.sqrt(jnp.sum(kk * kk, -1, keepdims=True)), 1e-12)
        k2 = k.astype(f32) * (1.0 + (a - 1.0) * rw_k_a[l])
        rh, kh, vh = heads(r.astype(f32), RW_HEADS), heads(k2, RW_HEADS), heads(v.astype(f32), RW_HEADS)
        out, S = rwkv7_scan(rh, heads(decay, RW_HEADS), kh, vh, kk, heads(a, RW_HEADS), S0)
        bonus = jnp.sum(rh * kh * rw_r_k[l], -1, keepdims=True) * vh
        h_rw = (head_norm(out, rw_ln_w[l], RW_GN_EPS) + rw_ln_b[l] + bonus.reshape(B, T, RW_WIDTH)) * g
        nq, nkv, nwkv, ngate = split_cols(ns_c, (NSA_WIDTH, 4 * KV_WIDTH, 2 * KV_WIDTH, 3 * NSA_HEADS))
        q_raw = heads(nq, NSA_HEADS)
        q_rot = rope(q_raw, pos)
        kv4 = nkv.reshape(B, T, 4, NSA_KV_HEADS, HEAD_DIM)
        kv4 = jnp.stack([kv4[:, :, 0], kv4[:, :, 1], rope(kv4[:, :, 2], pos), kv4[:, :, 3]], 2)
        wkv = nwkv.reshape(B, T, 2, NSA_KV_HEADS, HEAD_DIM)
        wkv = jnp.stack([rope(wkv[:, :, 0], pos), wkv[:, :, 1]], 2)
        gates = jax.nn.sigmoid(ngate.reshape(B, T, NSA_HEADS, 3))
        kv_full = jnp.concatenate([past_kv.astype(dt), kv4], 1)
        win_all = jnp.concatenate([win0.astype(dt), wkv], 1)
        h_ns = nsa_attend(q_raw, q_rot, gates, kv_full, win_all, offset, nsa_cmp_pos[l], nsa_cmp_w1[l], nsa_cmp_w2[l])
        win_new = last_rows(win_all, wbuf)
        x = x + jnp.concatenate([h_ml, h_rw, h_ns], -1).astype(dt) @ w_out[l]
        xn2 = rmsnorm(x, norm_ffn_w[l])
        if l % 2 == 0:
            ff = swiglu(xn2, ffn_w1[l // 2], ffn_w3[l // 2], ffn_w2[l // 2])
        else:
            ff = moe(xn2, l // 2)
        x = x + ff
        return x, (kv4, win_new, C, n, m, conv_new, S, shift_new)

    def run(x, offset, get_state):
        news = []
        for l in range(DEPTH):
            x, nw = layer(l, x, offset, get_state(l))
            news.append(nw)
        y = rmsnorm(x, norm_final_w)
        return y, [jnp.stack([nw[i] for nw in news]) for i in range(8)]

    Bp = x_prompt.shape[0]
    dtp = x_prompt.dtype

    def prompt_state(l):
        return (jnp.zeros((Bp, ML_HEADS, HEAD_DIM, HEAD_DIM), f32), jnp.zeros((Bp, ML_HEADS, HEAD_DIM), f32),
                jnp.zeros((Bp, ML_HEADS), f32), jnp.zeros((Bp, ML_CONV - 1, 2 * ML_WIDTH), dtp),
                jnp.zeros((Bp, RW_HEADS, HEAD_DIM, HEAD_DIM), f32), jnp.zeros((Bp, RW_COLS), dtp),
                jnp.zeros((Bp, 0, 4, NSA_KV_HEADS, HEAD_DIM), dtp), jnp.zeros((Bp, 0, 2, NSA_KV_HEADS, HEAD_DIM), dtp))

    Bs = x_sample.shape[0]
    past_len = page_table.shape[1] * PAGE_SIZE

    def sample_state(l):
        past = cache_nsa_kv[l][page_table].reshape(Bs, past_len, 4, NSA_KV_HEADS, HEAD_DIM)
        return (state_mlstm_C[l], state_mlstm_n[l], state_mlstm_m[l], state_mlstm_conv[l],
                state_rwkv_S[l], state_rwkv_shift[l], past, cache_win_kv[l])

    y_prompt, pst = run(x_prompt, 0, prompt_state)
    y_sample, sst = run(x_sample, past_len, sample_state)
    p_kv, p_win, p_C, p_n, p_m, p_conv, p_S, p_shift = pst
    s_kv, s_win, s_C, s_n, s_m, s_conv, s_S, s_shift = sst
    return (y_prompt, y_sample, p_kv, s_kv, p_win, s_win, p_C, s_C, p_n, s_n, p_m, s_m,
            p_conv, s_conv, p_S, s_S, p_shift, s_shift)


_drawn_inputs = setup_inputs


def setup_inputs(seed=0):
    import zlib

    import numpy as np

    out = dict(_drawn_inputs(seed))
    spreads = {}
    factors = {}
    for name, (base, spread) in spreads.items():
        noise = np.random.default_rng([zlib.crc32(name.encode()), seed]).standard_normal(out[name].shape)
        drawn = base * np.exp(spread * noise) if base else spread * noise
        out[name] = __import__('jax').numpy.asarray(drawn.astype(out[name].dtype))
    for name, factor in factors.items():
        out[name] = (out[name] * factor).astype(out[name].dtype)
    return out
```

```python
from contextlib import ExitStack

import numpy as np
import concourse.bass as bass
from concourse import mybir

F32 = mybir.dt.float32
I32 = mybir.dt.int32
ALU = mybir.AluOpType
ACT = mybir.ActivationFunctionType
AX = mybir.AxisListType

P = 128
D = 1024
KD = D // P
SEQ = 512
NB = 8
TS = 8
NS_TOK = NB * TS
T = SEQ + NS_TOK
PT = SEQ // P
TILES = [(i * P, P) for i in range(PT)] + [(SEQ, NS_TOK)]
DEPTH = 2
PAST = 512
PAGES = PAST // P
HD = 64
CMP = 31
STRIDE = 16
CLEN = 32
NBLK = 9
FC = 11
NEG = -1e30
SCALE = HD ** -0.5

CQ, CK, CV, CO = 0, 2, 4, 6
CR, CWA, CRK, CRV, CG = 8, 10, 11, 13, 15
CNQ, CCK, CCV, CSK, CSV, CWK, CWV, CGATE = 16, 20, 21, 22, 23, 24, 25, 26
NCH = 27

_v = {}
_n = 0
for _name, _w in (("nmix", 8), ("nffn", 8), ("convw", 16), ("convb", 4), ("mu", 8), ("w0", 2), ("a0", 2),
                  ("kk", 2), ("ka", 2), ("rk", 2), ("lnw", 2), ("lnb", 2), ("mlw", 2), ("gb", 1), ("flag", 1),
                  ("cpos", 64)):
    _v[_name] = _n
    _n += _w
NV = _n
VEC = dict(_v)


def tables():
    c = {}
    i = np.arange(P)
    c["ident"] = np.eye(P)
    c["ones"] = np.ones((P, P))
    c["onesbd"] = (i[:, None] // HD == i[None, :] // HD) * 1.0
    rot = np.zeros((P, P))
    for o in (0, HD):
        for d in range(HD // 2):
            rot[o + d + HD // 2, o + d] = -1.0
            rot[o + d, o + d + HD // 2] = 1.0
    c["rot"] = rot
    pos = np.concatenate([np.arange(SEQ), np.tile(PAST + np.arange(TS), NB)]).astype(np.float32)
    half = HD // 2
    inv = (np.float32(10000.0) ** (-np.arange(half, dtype=np.float32) / np.float32(half))).astype(np.float32)
    ang = (pos[None, :] * inv[:, None]).astype(np.float32)
    c["cos"] = np.tile(np.cos(ang), (4, 1))
    c["sin"] = np.tile(np.sin(ang), (4, 1))
    up = i[:, None] <= i[None, :]
    seg = i[:, None] // TS == i[None, :] // TS
    c["tri"] = np.where(i[None, :] <= i[:, None], 0.0, NEG)
    c["mlp"] = np.where(up, 0.0, NEG)
    c["mls"] = np.where(up & seg, 0.0, NEG)
    st = i[:, None] < i[None, :]
    c["rwp"] = np.concatenate([st, up], 1) * 1.0
    c["rws"] = np.concatenate([(st & seg)[:, :64], (up & seg)[:, :64]], 1) * 1.0
    lev = []
    for k in range(7):
        b = 1 << k
        lev.append((i[:, None] // (2 * b) == i[None, :] // (2 * b)) & (i[:, None] // b % 2 == 0)
                   & (i[None, :] // b % 2 == 1))
    c["lev"] = np.concatenate(lev, 1) * 1.0
    c["bd"] = np.tile(c["onesbd"], (1, 2))
    b65 = np.repeat(np.arange(2), 65)
    c["bd65"] = np.tile((i[:, None] // HD == b65[None, :]) * 1.0, (1, 2))
    t64 = np.arange(64)
    c["segbt"] = np.tile((np.arange(NB)[:, None] == t64[None, :] // TS).reshape(1, -1), (P, 1)) * 1.0
    c["segsb"] = (i[:, None] // TS == np.arange(NB)[None, :]) * 1.0
    cm = (np.arange(CMP) * STRIDE + CLEN - 1)[None, None, :] <= (np.arange(PT)[None, :, None] * P + i[:, None, None])
    c["cm1"] = cm.reshape(P, -1) * 1.0
    c["cma"] = np.where(cm, 0.0, NEG).reshape(P, -1)
    r = i
    rb, rt = r // 32, r % TS
    col = np.arange(64)
    new = [((col[None, :] // TS == rb[:, None] + 4 * q) & (col[None, :] % TS <= rt[:, None])) for q in range(2)]
    c["newm"] = np.where(np.concatenate(new, 1), 0.0, NEG)
    c["winm"] = np.where(np.arange(8)[None, :] > rt[:, None], 0.0, NEG)
    c["same"] = ((rb[:, None] == rb[None, :]) & (rt[:, None] == rt[None, :])) * 1.0
    cs, ss = np.arange(CMP) * STRIDE, np.arange(NBLK) * HD
    ov = np.clip(np.minimum(cs[:, None] + CLEN, ss[None, :] + HD) - np.maximum(cs[:, None], ss[None, :]), 0, None)
    c["ov"] = ov / CLEN
    c["rowi"] = np.tile((np.arange(4)[None, :, None] == (r // TS % 4)[:, None, None]) * np.ones((1, 1, 3)), (1, 2, 1)).reshape(P, 24)
    c["rank"] = np.tile(np.arange(1, 10)[None, :], (P, 1))
    c["rrank"] = np.tile(np.arange(8, 0, -1)[None, :], (P, 5))
    for j in range(2):
        s = np.zeros((4, P))
        s[2 * j, :HD] = 1.0
        s[2 * j + 1, HD:] = 1.0
        c[f"pair{j}"] = s
    tt = np.arange(T)
    first = (tt % P == 0) | ((tt >= SEQ) & (tt % TS == 0))
    c["reset"] = np.tile(np.where(first, 0.0, 1.0)[None, :], (P, 1))
    c["kill"] = np.tile(np.where((tt >= SEQ) & (tt % TS == 0), NEG, 0.0)[None, :], (4, 1))
    return {k: np.asarray(v, np.float32) for k, v in c.items()}


def table_layout():
    at, col = {}, 0
    for k, v in tables().items():
        at[k] = (col, v.shape[0], v.shape[1])
        col += v.shape[1]
    return at, col


TAB, TAB_W = table_layout()

ST_CONV, ST_SHIFT, ST_W = 0, 4 * NB * 3, 4 * NB * 3 + 8 * NB
OUT_CP, OUT_CS, OUT_SP, OUT_SS = 0, 12, 12 + 96, 12 + 96 + 8
OUT_W = OUT_SS + 64


class Chain:

    def __init__(self, eng, sem):
        self.eng, self.sem, self.n = eng, sem, 0

    def __call__(self, ins, *signals):
        self.n += 1
        ins.then_inc(self.sem, 1)
        self.eng.wait_ge(self.sem, self.n)
        for s in signals:
            self.eng.sem_inc(s, 1)


class Space:

    def __init__(self, buf, start, end):
        self.buf, self.at, self.end = buf, start, end

    def take(self, *dims):
        n = int(np.prod(dims))
        assert self.at + n <= self.end, (self.at, n, self.end)
        v = self.buf[:, self.at:self.at + n]
        self.at += n
        if len(dims) == 2:
            v = v.rearrange("p (a b) -> p a b", b=dims[1])
        elif len(dims) == 3:
            v = v.rearrange("p (a b c) -> p a b c", b=dims[1], c=dims[2])
        elif len(dims) == 4:
            v = v.rearrange("p (a b c d) -> p a b c d", b=dims[1], c=dims[2], d=dims[3])
        return v


def build(nc, A):
    with ExitStack() as ctx:
        sems = {}

        FIRST = ("mix_norm", "proj_", "w_in_", "conv_", "shift_", "f_", "exp_args", "m_rows", "rows_", "m_out", "ml_",
                 "rw_", "hn_")
        SECOND = ("cmp_", "rope_", "at_", "sa_", "cw", "pages_", "qpages_", "qwin", "wo_", "w_out_", "ffn_norm", "rt_")
        shared, used = [], {True: 0, False: 0}

        def S(name):
            if name not in sems:
                part = name.startswith(FIRST)
                if part or name.startswith(SECOND):
                    if used[part] == len(shared):
                        shared.append(ctx.enter_context(nc.semaphore(f"part_{len(shared)}")))
                    sems[name] = shared[used[part]]
                    used[part] += 1
                else:
                    sems[name] = ctx.enter_context(nc.semaphore(name))
            return sems[name]

        def sb(name, cols):
            return ctx.enter_context(nc.sbuf_tensor(name, [P, cols], F32))

        tab = sb("tab", TAB_W)
        x_buf = sb("x_buf", KD * T)
        n_buf = sb("n_buf", KD * T)
        cols_buf = sb("cols_buf", NCH * T)
        small = sb("small", 1400)
        h_buf = sb("h_buf", 5 * 2 * 256)
        ARENA = 21000
        arena = sb("arena", ARENA)
        page_buf = ctx.enter_context(nc.sbuf_tensor("page_buf", [1, NB * PAGES], I32))
        ps_buf = ctx.enter_context(nc.psum_tensor("ps_buf", [P, 8, 512], F32))

        def tb(name, rows=None, lo=0):
            c, r, w = TAB[name]
            return tab[lo:(rows or r), c:c + w]

        ident = tb("ident")
        x = x_buf[:, :].rearrange("p (k t) -> p k t", t=T)
        xn = n_buf[:, :].rearrange("p (k t) -> p k t", t=T)
        hmix = xn
        cols = cols_buf[:, :].rearrange("p (k t) -> p k t", t=T)
        HB = h_buf[:, :].rearrange("p (m i c) -> p m i c", m=2, i=5)
        sm = Space(small, 0, 1400)
        vec = sm.take(NV)
        state_in = sm.take(ST_W)
        state_out = sm.take(OUT_W)
        m0_in = sm.take(NB)
        nfin = sm.take(8)
        n64 = sm.take(40)
        n64b = sm.take(40)
        decb = sm.take(2, 12)
        posb = sm.take(4)
        omka = sm.take(2)
        router = sm.take(8, 8)
        prod = sm.take(2, 12)
        midp = sm.take(2, 4)
        gates = sm.take(5, 24)
        sgate = sm.take(2, 2, 3)
        stat = sm.take(4, 4)
        impz = sm.take(9)
        imps = sm.take(9)
        kbias = sm.take(8)
        iw = sm.take(8)
        sg24 = sm.take(24)
        ups = sm.take(2, 4)

        def V(name, k=0, lo=0, hi=P):
            c = VEC[name] + k
            return vec[lo:hi, c:c + 1]

        def bank(i, n=512, rows=P):
            return ps_buf[0:rows, i, 0:n]

        sync = nc.sync

        WR = 4
        sp1 = Space(arena, 0, ARENA)
        wring = sp1.take(WR, KD, P)
        qkpad = sp1.take(4, 3 + SEQ + NB * 11)
        rwpad = sp1.take(8, 1 + SEQ + NB * 9)
        rstd = sp1.take(T)

        def pad_p(pad, c, h, j, n=SEQ):
            return pad[:, c, j:j + n]

        def pad_s(pad, c, h, j, n=TS):
            return pad[:, c, h + SEQ:].rearrange("p (b t) -> p b t", t=h + TS)[:, :, j:j + n]

        sp2 = Space(arena, 0, ARENA)
        R = sp2.take(12, T)
        G = sp2.take(T)
        GT = sp2.take(5, P)
        qs = sp2.take(2, T)
        qmask = sp2.take(NB, NS_TOK)
        v1 = sp2.take(5, 260)
        wk = sp2.take(5, 256)
        DT = sp2.take(512)
        STb = sp2.take(512)
        Cp = sp2.take(260)
        Cs = sp2.take(2, NB, 130)
        vm = sp2.take(NB, 130)
        seg12 = sp2.take(4, 12)
        den = sp2.take(8)

        sp3 = Space(arena, 0, ARENA)
        rw_w = sp3.take(2, 256)
        ra = sp3.take(2, T)
        rg = sp3.take(2, T)
        rcum = sp3.take(2, T)
        rcumx = sp3.take(2, T)
        rkk = sp3.take(2, T)
        rk2 = sp3.take(2, T)
        KR = sp3.take(2, 2 * T)
        nbt = sp3.take(2, T)
        kht = sp3.take(2, T)
        e3 = sp3.take(2, T)
        tk_flat = sp3.take(5 * 3 * 256)
        TK = tk_flat.rearrange("p (i c) -> p i c", i=5)
        XU = sp3.take(2, 256)
        S0 = sp3.take(256)
        mid = sp3.take(2, 4)
        M1 = cols_buf[:, 0:1024].rearrange("p (h c) -> p h c", h=4)
        M2 = cols_buf[:, 1024:2048].rearrange("p (h c) -> p h c", h=4)
        Dm = cols_buf[:, 2048:2560]
        Dt = cols_buf[:, 2560:3072]
        S0s = sp3.take(2, NB, P)
        Nb = sp3.take(512)
        Yb = sp3.take(512)
        kmask = cols_buf[:, 2048:2560].rearrange("p (b t) -> p b t", b=NB)
        rmask = Nb.rearrange("p (b t) -> p b t", b=NB)
        umask = cols_buf[:, 0:1024].rearrange("p (b c) -> p b c", b=NB)
        vmask = cols_buf[:, 1024:2048].rearrange("p (b c) -> p b c", b=NB)
        hsq = tk_flat[:, 0:2560].rearrange("p (g d) -> p g d", d=HD)

        def kr(j, i, which, n, lo=0, hi=P):
            o = 2 * TILES[i][0] + which * n
            return KR[lo:hi, j, o:o + n]

        sp4 = Space(arena, 0, ARENA)
        ckb = sp4.take(9, 2, 512)
        cw1 = sp4.take(CLEN, P)
        hid = sp4.take(4, 9 * CMP)
        ckT = sp4.take(9 * CMP)
        cvt = sp4.take(9, 2, HD)
        cw2 = sp4.take(2, HD)
        qrs = sp4.take(2, NB * 32)
        svt = sp4.take(5, P)
        wvt = sp4.take(5, P)
        rtmp = sp4.take(T)
        osamp = sp4.take(2, P)
        sp5 = Space(arena, 0, 9 * 1024 + 4096)
        skq = sp5.take(4, 512)
        wkq = sp5.take(4, 512)
        svq = sp5.take(4, PAGES, P)
        wvq = sp5.take(4, 4, P)
        Sb = sp5.take(2, T)
        PTb = sp5.take(2, 5, P)
        oacc = sp5.take(4, 4, P)
        qrot = Space(cols_buf, 0, 4 * T).take(4, T)
        sp6 = Space(arena, 0, ARENA)
        w13 = sp6.take(2, 2, KD, P)
        w2r = sp6.take(3, FC, P)
        comb = sp6.take(8, T)
        sg = sp6.take(2, T)
        lg = sp6.take(5, 8)
        lw = sp6.take(8, 40)
        cT = sp6.take(T)
        rstd2 = sp6.take(T)
        woring = Space(arena, 0, ARENA).take(2, KD, P)
        hff = Space(cols_buf, 0, FC * T).take(FC, T)

        meets = {"pe": 0, "act": 0, "dve": 0}

        def meet(eng, who):
            eng.drain().then_inc(S("phase_ended"), 1)
            meets[who] += 1
            eng.wait_ge(S("phase_ended"), 3 * meets[who])

        def norm_act(a, tag, rs):
            for k in range(KD):
                a(nc.scalar.activation(xn[:, k, :], x[:, k, :], ACT.Square), S(tag + "_squares"))
            nc.scalar.wait_ge(S(tag + "_mean"), 1)
            a(nc.scalar.activation(rs, rs, ACT.Sqrt), S(tag + "_root"))

        def norm_pe(tag):
            for k in range(KD):
                nc.tensor.wait_ge(S(tag + "_squares"), k + 1)
                nc.tensor.matmul(bank(0), tb("ones"), xn[:, k, 0:SEQ], start=k == 0, stop=k == KD - 1)
                last = nc.tensor.matmul(bank(1, 64), tb("ones"), xn[:, k, SEQ:T], start=k == 0, stop=k == KD - 1)
            last.then_inc(S(tag + "_sum"), 1)

        def norm_dve(v, tag, rs, w):
            nc.vector.wait_ge(S(tag + "_sum"), 1)
            v(nc.vector.tensor_scalar(rs[:, 0:SEQ], bank(0), 1.0 / D, 1e-6, ALU.mult, ALU.add))
            v(nc.vector.tensor_scalar(rs[:, SEQ:T], bank(1, 64), 1.0 / D, 1e-6, ALU.mult, ALU.add), S(tag + "_mean"))
            nc.vector.wait_ge(S(tag + "_root"), 1)
            v(nc.vector.reciprocal(rs, rs))
            for k in range(KD):
                v(nc.vector.scalar_tensor_tensor(xn[:, k, :], x[:, k, :], w(k), rs, ALU.mult, ALU.mult),
                  S(tag + "_done"))

        def proj_sp(l):
            for c in range(NCH):
                if c >= WR:
                    sync.wait_ge(S("proj_done"), c - WR + 1)
                sync.dma_start(wring[:, c % WR], A["w_in"][l * NCH + c]).then_inc(S(f"w_in_{c % WR}"), 16)

        def proj_pe():
            for c in range(NCH):
                if c == 0:
                    nc.tensor.wait_ge(S("mix_norm_done"), KD)
                nc.tensor.wait_ge(S(f"w_in_{c % WR}"), 16 * (c // WR + 1))
                if c >= 3:
                    nc.tensor.wait_ge(S("proj_out"), c - 2)
                b = 2 + 2 * (c % 3)
                for k in range(KD):
                    nc.tensor.matmul(bank(b), wring[:, c % WR, k, :], xn[:, k, 0:SEQ], start=k == 0, stop=k == KD - 1)
                    last = nc.tensor.matmul(bank(b + 1, 64), wring[:, c % WR, k, :], xn[:, k, SEQ:T],
                                            start=k == 0, stop=k == KD - 1)
                last.then_inc(S("proj_done"), 1)

        def proj_act(a):
            for c in range(NCH):
                nc.scalar.wait_ge(S("proj_done"), c + 1)
                b = 2 + 2 * (c % 3)
                s64 = bank(b + 1, 64).rearrange("p (b t) -> p b t", t=TS)
                if c < 4:
                    a(nc.scalar.copy(pad_p(qkpad, c, 3, 3), bank(b)))
                    a(nc.scalar.copy(pad_s(qkpad, c, 3, 3), s64), S("proj_out"))
                elif 8 <= c < 16:
                    a(nc.scalar.copy(pad_p(rwpad, c - 8, 1, 1), bank(b)))
                    a(nc.scalar.copy(pad_s(rwpad, c - 8, 1, 1), s64), S("proj_out"))
                elif c == CGATE:
                    a(nc.scalar.activation(cols[:, c, 0:SEQ], bank(b), ACT.Identity, bias=V("gb")))
                    a(nc.scalar.activation(cols[:, c, SEQ:T], bank(b + 1, 64), ACT.Identity, bias=V("gb")), S("proj_out"))
                else:
                    a(nc.scalar.copy(cols[:, c, 0:SEQ], bank(b)))
                    a(nc.scalar.copy(cols[:, c, SEQ:T], bank(b + 1, 64)), S("proj_out"))
            nc.scalar.wait_ge(S("conv_done"), 4)
            for c in range(4):
                a(nc.scalar.activation(cols[:, c, :], cols[:, c, :], ACT.Silu))
                if c >= 2:
                    a(nc.scalar.mul(cols[:, c, :], cols[:, c, :], SCALE))

        def proj_dve(v):
            ve = nc.vector
            v(ve.memset(qkpad[:, :, 0:3], 0.0))
            v(ve.memset(rwpad[:, :, 0:1], 0.0))
            for c in range(4):
                v(ve.tensor_copy(pad_s(qkpad, c, 3, 0, 3),
                                 state_in[:, ST_CONV + 24 * c:ST_CONV + 24 * c + 24].rearrange("p (b j) -> p b j", j=3)))
            for c in range(8):
                v(ve.tensor_copy(pad_s(rwpad, c, 1, 0, 1),
                                 state_in[:, ST_SHIFT + 8 * c:ST_SHIFT + 8 * c + 8].rearrange("p (b j) -> p b j", j=1)))

            def both(c):
                yield cols[:, c, 0:SEQ], pad_p
                yield cols[:, c, SEQ:T].rearrange("p (b t) -> p b t", t=TS), pad_s

            for c in range(4):
                ve.wait_ge(S("proj_out"), c + 1)
                for y, pad in both(c):
                    n = SEQ if pad is pad_p else TS
                    v(ve.tensor_scalar(y, pad(qkpad, c, 3, 0, n), V("convw", c), V("convb", c), ALU.mult, ALU.add))
                    for j in range(1, 4):
                        v(ve.scalar_tensor_tensor(y, pad(qkpad, c, 3, j, n), V("convw", 4 * j + c), y, ALU.mult, ALU.add))
                v(ve.tensor_copy(state_out[:, OUT_CP + 3 * c:OUT_CP + 3 * c + 3], qkpad[:, c, SEQ:SEQ + 3]))
                v(ve.tensor_copy(state_out[:, OUT_CS + 24 * c:OUT_CS + 24 * c + 24].rearrange("p (b j) -> p b j", j=3),
                                 pad_s(qkpad, c, 3, TS, 3)), S("conv_done"))
            for c in range(8):
                ve.wait_ge(S("proj_out"), 8 + c + 1)
                for y, pad in both(8 + c):
                    n = SEQ if pad is pad_p else TS
                    now = pad(rwpad, c, 1, 1, n)
                    v(ve.tensor_tensor(y, pad(rwpad, c, 1, 0, n), now, ALU.subtract))
                    v(ve.scalar_tensor_tensor(y, y, V("mu", c), now, ALU.mult, ALU.add))
                v(ve.tensor_copy(state_out[:, OUT_SP + c:OUT_SP + c + 1], rwpad[:, c, SEQ:SEQ + 1]))
                v(ve.tensor_copy(state_out[:, OUT_SS + 8 * c:OUT_SS + 8 * c + 8].rearrange("p (b j) -> p b j", j=1),
                                 pad_s(rwpad, c, 1, TS, 1)), S("shift_done"))

        def onehot(h, n):
            return ident[0:4, h:h + 1].to_broadcast([4, n])

        def pairsel(j):
            return tb(f"pair{j}")

        RF, RL, RB, RM, RP, RU, RI, RD1, RD0, RT = range(10)

        def rows_dve(v):
            ve = nc.vector

            def r(k, a=0, b=T, s=1):
                return R[0:4, k, a:b:s] if s > 1 else R[0:4, k, a:b]

            def seg(k):
                return R[0:4, k, SEQ:T].rearrange("p (b t) -> p b t", t=TS)

            def til(k, a=0, b=SEQ):
                return R[0:4, k, a:b].rearrange("p (c t) -> p c t", t=P)

            ig = cols[0:4, CGATE, :]
            v(ve.memset(G, 0.0))
            v(ve.memset(seg12, 0.0), S("rows_start"))
            v(ve.tensor_copy(r(RF), cols[32:36, CGATE, :]))
            v(ve.scalar_tensor_tensor(r(RT), r(RF), -1.0, r(RF), ALU.mult, ALU.max), S("f_abs"))
            ve.wait_ge(S("f_exp"), 1)
            v(ve.tensor_scalar(r(RL), r(RL), 1.0, None, ALU.add), S("f_one"))
            ve.wait_ge(S("f_ln"), 1)
            v(ve.scalar_tensor_tensor(r(RL), r(RF), 0.0, r(RL), ALU.min, ALU.subtract))
            v(ve.tensor_tensor_scan(r(RB), tb("reset", 4), r(RL), 0.0, ALU.mult, ALU.add))
            v(ve.tensor_copy(r(RD1), ig))
            v(ve.tensor_tensor(seg12[0:4, 3, 0:8], R[0:4, RL, SEQ:T:TS], m0_in[0:4, :], ALU.add))
            v(ve.tensor_tensor(R[0:4, RD1, SEQ:T:TS], R[0:4, RD1, SEQ:T:TS], seg12[0:4, 3, 0:8], ALU.max))
            v(ve.tensor_tensor(r(RD0), r(RL), tb("kill", 4), ALU.add))
            v(ve.tensor_tensor_scan(r(RM), r(RD0), r(RD1), 0.0, ALU.add, ALU.max), S("m_rows"))
            v(ve.memset(r(RP, 0, P), 0.0))
            v(ve.tensor_copy(til(RP, P, SEQ), R[0:4, RM, P - 1:SEQ - P:P].unsqueeze(2).to_broadcast([4, PT - 1, P])))
            v(ve.tensor_copy(seg(RP), m0_in[0:4, :].unsqueeze(2).to_broadcast([4, NB, TS])))
            v(ve.tensor_tensor(r(RU), r(RB), r(RM), ALU.subtract))
            v(ve.tensor_tensor(r(RI), r(RU), r(RP), ALU.add))
            v(ve.tensor_tensor(G[0:4, :], ig, r(RB), ALU.subtract))
            v(ve.tensor_copy(seg12[0:4, 0, 0:4], R[0:4, RU, P - 1:SEQ:P]))
            v(ve.tensor_copy(seg12[0:4, 0, 4:12], R[0:4, RU, SEQ + TS - 1:T:TS]))
            v(ve.tensor_tensor(seg12[0:4, 1, 0:4], seg12[0:4, 0, 0:4], R[0:4, RP, 0:SEQ:P], ALU.add))
            v(ve.tensor_tensor(seg12[0:4, 1, 4:12], seg12[0:4, 0, 4:12], m0_in[0:4, :], ALU.add))
            v(ve.tensor_tensor(til(RT), G[0:4, 0:SEQ].rearrange("p (c t) -> p c t", t=P),
                               seg12[0:4, 0, 0:4].unsqueeze(2).to_broadcast([4, 4, P]), ALU.add))
            v(ve.tensor_tensor(seg(RT), G[0:4, SEQ:T].rearrange("p (b t) -> p b t", t=TS),
                               seg12[0:4, 0, 4:12].unsqueeze(2).to_broadcast([4, NB, TS]), ALU.add), S("exp_args"))
            v(ve.tensor_copy(seg12[0:4, 2, 0:4], R[0:4, RM, P - 1:SEQ:P]))
            v(ve.tensor_copy(seg12[0:4, 2, 4:12], R[0:4, RM, SEQ + TS - 1:T:TS]), S("m_out"))

        def rows_act(a):
            ac = nc.scalar
            ac.wait_ge(S("rows_start"), 1)
            a(ac.activation(G[96:120, :], cols[64:88, CGATE, :], ACT.Sigmoid))
            ac.wait_ge(S("f_abs"), 1)
            a(ac.activation(R[0:4, RL, :], R[0:4, RT, :], ACT.Exp, scale=-1.0), S("f_exp"))
            ac.wait_ge(S("f_one"), 1)
            a(ac.activation(R[0:4, RL, :], R[0:4, RL, :], ACT.Ln), S("f_ln"))
            ac.wait_ge(S("exp_args"), 1)
            a(ac.activation(G[64:68, :], R[0:4, RM, :], ACT.Exp, scale=-1.0))
            a(ac.activation(R[0:4, RI, :], R[0:4, RI, :], ACT.Exp))
            a(ac.activation(seg12[0:4, 1, :], seg12[0:4, 1, :], ACT.Exp))
            a(ac.activation(G[32:36, :], R[0:4, RT, :], ACT.Exp), S("rows_done"))

        def ml_pe():
            pe = nc.tensor
            pe.wait_ge(S("rows_done"), 1)
            for i, (t0, n) in enumerate(TILES):
                last = pe.transpose(ps_buf[0:n, i // 4, (i % 4) * P:(i % 4) * P + P], G[:, t0:t0 + n], ident)
            last.then_inc(S("ml_cols"), 1)
            for j in range(2):
                pe.matmul(bank(2 + 2 * j), pairsel(j), R[0:4, RI, 0:SEQ], start=True, stop=True)
                pe.matmul(bank(3 + 2 * j, 64), pairsel(j), R[0:4, RI, SEQ:T], start=True, stop=True)
                last = pe.matmul(ps_buf[:, 6, 12 * j:12 * j + 12], pairsel(j), seg12[0:4, 1, :], start=True, stop=True)
            last.then_inc(S("ml_spread"), 1)
            for i, (t0, n) in enumerate(TILES):
                pe.wait_ge(S("ml_spread_out") if i == 0 else S("ml_kv_out"), 1 if i == 0 else i)
                for c in range(4):
                    last = pe.transpose(ps_buf[0:n, 7, c * P:c * P + P], cols[:, CK + c, t0:t0 + n], ident)
                last.then_inc(S("ml_kv"), 1)
            for i, (t0, n) in enumerate(TILES):
                mask = tb("mlp" if n == P else "mls", n)[:, 0:n]
                if i == 0:
                    pe.wait_ge(S("ml_kv_out"), 5)
                for h in range(4):
                    o = ps_buf[0:n, 0, h * n:h * n + n]
                    pe.matmul(o, onehot(h, n), R[0:4, RU, t0:t0 + n], start=True, stop=False)
                    last = pe.matmul(o, ident[0:n, 0:n], mask, start=False, stop=True)
                last.then_inc(S("ml_logd"), 1)
                for h in range(4):
                    j, f = h // 2, h % 2
                    last = pe.matmul(ps_buf[0:n, 1 + f, j * n:j * n + n], cols[64 * f:64 * f + 64, CK + j, t0:t0 + n],
                                     cols[64 * f:64 * f + 64, CQ + j, t0:t0 + n], start=True, stop=True)
                last.then_inc(S("ml_kq"), 1)
                if i == 4:
                    pe.wait_ge(S("ml_state_in"), 32)
                else:
                    pe.wait_ge(S("ml_state"), i + 1)
                for j in range(2):
                    o = ps_buf[0:n, 3, j * 130:j * 130 + 130]
                    if i < 4:
                        pe.matmul(o, qs[:, j, t0:t0 + n], Cp[:, j * 130:j * 130 + 130], start=True, stop=False)
                    else:
                        pe.wait_ge(S("ml_qmask"), j + 1)
                        for b in range(NB):
                            last = pe.matmul(o, qmask[:, b, :], Cs[:, j, b, :], start=b == 0, stop=False)
                        last.then_inc(S("ml_qmask_used"), 1)
                    if j == 0:
                        pe.wait_ge(S("ml_S"), i + 1)
                    for f in range(2):
                        last = pe.matmul(ps_buf[0:n, 3, j * 130 + 65 * f:j * 130 + 65 * f + 65],
                                         STb[0:n, (2 * f + j) * n:(2 * f + j) * n + n],
                                         v1[0:n, i, (2 * j + f) * 65:(2 * j + f) * 65 + 65], start=False, stop=f == 1)
                last.then_inc(S("ml_num"), 1)
                if i < 4:
                    for j in range(2):
                        last = pe.matmul(ps_buf[:, 4, j * 130:j * 130 + 130], wk[:, i, 128 * j:128 * j + 128],
                                         v1[:, i, 130 * j:130 * j + 130], start=True, stop=True)
                    last.then_inc(S("ml_add"), 1)
                else:
                    for j in range(2):
                        pe.wait_ge(S("ml_vm"), j + 1)
                        for g in range(3):
                            nb = min(3, NB - 3 * g)
                            last = pe.matmul(ps_buf[:, 4 + g, 0:nb * 130], wk[0:64, 4, 128 * j:128 * j + 128],
                                             vm[0:64, 3 * g:3 * g + nb, :], start=True, stop=True)
                        last.then_inc(S("ml_add"), 1)
                if i < 4:
                    pe.wait_ge(S("ml_h"), i + 1)

        def ml_act(a):
            ac = nc.scalar
            for i, (t0, n) in enumerate(TILES):
                ac.wait_ge(S("ml_logd"), i + 1)
                ac.wait_ge(S("ml_kv_out"), 5)
                for h in range(4):
                    idx = (h % 2) * 2 + h // 2
                    a(ac.activation(DT[0:n, idx * n:idx * n + n], ps_buf[0:n, 0, h * n:h * n + n], ACT.Exp,
                                    bias=GT[0:n, i, h:h + 1]))
                ac.sem_inc(S("ml_D"), 1)
                if i < 4:
                    ac.wait_ge(S("ml_h"), i + 1)

        def ml_dve(v):
            ve = nc.vector
            v(ve.memset(Cp, 0.0))
            v(ve.memset(v1, 1.0))
            v(ve.memset(h_buf[:, :], 0.0), S("ml_state"))
            ve.wait_ge(S("ml_cols"), 1)
            v(ve.tensor_copy(GT[:, 0:4, :], bank(0).rearrange("p (i c) -> p i c", c=P)))
            v(ve.tensor_copy(GT[0:64, 4, :], ps_buf[0:64, 1, 0:P]))
            v(ve.tensor_copy(gates[:, 0:4, :], GT[:, 0:4, 96:120]))
            ve.wait_ge(S("ml_spread"), 1)
            for j in range(2):
                v(ve.tensor_tensor(qs[:, j, 0:SEQ], cols[:, CQ + j, 0:SEQ], bank(2 + 2 * j), ALU.mult))
                v(ve.tensor_tensor(qs[:, j, SEQ:T], cols[:, CQ + j, SEQ:T], bank(3 + 2 * j, 64), ALU.mult))
            v(ve.tensor_copy(decb, ps_buf[:, 6, 0:24].rearrange("p (j c) -> p j c", j=2)), S("ml_spread_out"))
            for i, (t0, n) in enumerate(TILES):
                ve.wait_ge(S("ml_kv"), i + 1)
                v(ve.tensor_tensor(wk[0:n, i, :].rearrange("p (h d) -> p h d", h=4),
                                   ps_buf[0:n, 7, 0:256].rearrange("p (h d) -> p h d", h=4),
                                   GT[0:n, i, 32:36].unsqueeze(2).to_broadcast([n, 4, HD]), ALU.mult))
                v(ve.tensor_copy(v1[0:n, i, :].rearrange("p (h d) -> p h d", h=4)[:, :, 0:HD],
                                 ps_buf[0:n, 7, 256:512].rearrange("p (h d) -> p h d", h=4)), S("ml_kv_out"))
            for i, (t0, n) in enumerate(TILES):
                if i == 4:
                    v(ve.tensor_tensor(qmask, qs[:, 0, SEQ:T].unsqueeze(1).to_broadcast([P, NB, NS_TOK]),
                                       tb("segbt").rearrange("p (b t) -> p b t", b=NB), ALU.mult), S("ml_qmask"))
                ve.wait_ge(S("ml_kq"), i + 1)
                ve.wait_ge(S("ml_D"), i + 1)
                for f in range(2):
                    v(ve.tensor_tensor(STb[0:n, 2 * f * n:2 * f * n + 2 * n], ps_buf[0:n, 1 + f, 0:2 * n],
                                       DT[0:n, 2 * f * n:2 * f * n + 2 * n], ALU.mult), *([S("ml_S")] if f else []))
                if i == 4:
                    ve.wait_ge(S("ml_qmask_used"), 1)
                    v(ve.tensor_tensor(qmask, qs[:, 1, SEQ:T].unsqueeze(1).to_broadcast([P, NB, NS_TOK]),
                                       tb("segbt").rearrange("p (b t) -> p b t", b=NB), ALU.mult), S("ml_qmask"))
                ve.wait_ge(S("ml_num"), i + 1)
                num = ps_buf[0:n, 3, 0:260].rearrange("p (h d) -> p h d", h=4)
                v(ve.tensor_copy(den[0:n, 4:8], num[:, :, HD]))
                v(ve.scalar_tensor_tensor(den[0:n, 0:4], den[0:n, 4:8], -1.0, den[0:n, 4:8], ALU.mult, ALU.max))
                v(ve.tensor_tensor(den[0:n, 0:4], den[0:n, 0:4], GT[0:n, i, 64:68], ALU.max))
                v(ve.reciprocal(den[0:n, 4:8], den[0:n, 0:4]))
                v(ve.tensor_tensor(HB[0:n, 0, i, :].rearrange("p (h d) -> p h d", h=4), num[:, :, 0:HD],
                                   den[0:n, 4:8].unsqueeze(2).to_broadcast([n, 4, HD]), ALU.mult))
                if i < 4:
                    ve.wait_ge(S("ml_add"), i + 1)
                    for j in range(2):
                        c = Cp[:, 130 * j:130 * j + 130]
                        v(ve.scalar_tensor_tensor(c, c, decb[:, j, i:i + 1], ps_buf[:, 4, 130 * j:130 * j + 130],
                                                  ALU.mult, ALU.add))
                    v(ve.tensor_tensor(Cp, Cp, tb("bd65"), ALU.mult), S("ml_state"), S("ml_h"))
                else:
                    for j in range(2):
                        v(ve.tensor_tensor(vm[0:64], v1[0:64, 4, 130 * j:130 * j + 130].unsqueeze(1).to_broadcast([64, NB, 130]),
                                           tb("segsb", 64).unsqueeze(2).to_broadcast([64, NB, 130]), ALU.mult), S("ml_vm"))
                        ve.wait_ge(S("ml_add"), 5 + j)
                        v(ve.tensor_tensor(Cs[:, j], Cs[:, j], decb[:, j, 4:12].unsqueeze(2).to_broadcast([P, NB, 130]), ALU.mult))
                        for g in range(3):
                            nb = min(3, NB - 3 * g)
                            v(ve.tensor_tensor(Cs[:, j, 3 * g:3 * g + nb, :], Cs[:, j, 3 * g:3 * g + nb, :],
                                               ps_buf[:, 4 + g, 0:nb * 130].rearrange("p (b c) -> p b c", b=nb), ALU.add))
                    ve.sem_inc(S("ml_final"), 1)

        def rwprep_pe():
            pe = nc.tensor
            pe.wait_ge(S("rw_w_in"), 32)
            pe.wait_ge(S("rw_lora_in"), 1)
            for j in range(2):
                for a0, b0 in ((0, SEQ), (SEQ, T)):
                    last = pe.matmul(bank(2 * j + (a0 > 0), b0 - a0), rw_w[0:64, 0, P * j:P * j + P],
                                     cols[0:64, CWA, a0:b0], start=True, stop=True)
            last.then_inc(S("rw_w_pre"), 1)
            for j in range(2):
                for a0, b0 in ((0, SEQ), (SEQ, T)):
                    last = pe.matmul(bank(4 + 2 * j + (a0 > 0), b0 - a0), rw_w[64:128, 0, P * j:P * j + P],
                                     cols[64:128, CWA, a0:b0], start=True, stop=True)
            last.then_inc(S("rw_a_pre"), 1)
            pe.wait_ge(S("rw_decay"), 1)
            for j in range(2):
                for a0, b0 in ((0, SEQ), (SEQ, T)):
                    last = pe.matmul(bank(2 * j + (a0 > 0), b0 - a0), rw_w[:, 1, P * j:P * j + P],
                                     cols[:, CG, a0:b0], start=True, stop=True)
            last.then_inc(S("rw_g"), 1)
            pe.wait_ge(S("rw_a"), 1)
            pe.wait_ge(S("rw_kk_sq"), 1)
            for j in range(2):
                for a0, b0 in ((0, SEQ), (SEQ, T)):
                    last = pe.matmul(bank(4 + 2 * j + (a0 > 0), b0 - a0), tb("onesbd"), e3[:, j, a0:b0],
                                     start=True, stop=True)
            last.then_inc(S("rw_kk_sum"), 1)
            pe.wait_ge(S("rw_rk"), 1)
            for j in range(2):
                for a0, b0 in ((0, SEQ), (SEQ, T)):
                    last = pe.matmul(bank(2 * j + (a0 > 0), b0 - a0), tb("onesbd"), Yb2[:, j, a0:b0],
                                     start=True, stop=True)
            last.then_inc(S("rw_rk_sum"), 1)
            pe.wait_ge(S("rw_ready"), 1)
            for i, (t0, n) in enumerate(TILES):
                if i:
                    pe.wait_ge(S("rw_rows_out"), i)
                for j in range(2):
                    pe.transpose(ps_buf[0:n, 6, P * j:P * j + P], nbt[:, j, t0:t0 + n], ident)
                    pe.transpose(ps_buf[0:n, 6, 256 + P * j:256 + P * j + P], kht[:, j, t0:t0 + n], ident)
                    last = pe.transpose(ps_buf[0:n, 7, P * j:P * j + P], cols[:, CRV + j, t0:t0 + n], ident)
                last.then_inc(S("rw_rows"), 1)

        def rwprep_act(a):
            ac = nc.scalar
            a(ac.activation(cols[0:64, CWA, :], cols[0:64, CWA, :], ACT.Tanh), S("rw_lora_in"))
            a(ac.activation(cols[:, CG, :], cols[:, CG, :], ACT.Sigmoid))
            ac.wait_ge(S("rw_w_pre"), 1)
            for j in range(2):
                a(ac.activation(rcumx[:, j, 0:SEQ], bank(2 * j), ACT.Sigmoid, bias=V("w0", j)))
                a(ac.activation(rcumx[:, j, SEQ:T], bank(2 * j + 1, 64), ACT.Sigmoid, bias=V("w0", j)),
                  *([S("rw_decay")] if j else []))
            ac.wait_ge(S("rw_a_pre"), 1)
            for j in range(2):
                a(ac.activation(ra[:, j, 0:SEQ], bank(4 + 2 * j), ACT.Sigmoid, bias=V("a0", j)))
                a(ac.activation(ra[:, j, SEQ:T], bank(5 + 2 * j, 64), ACT.Sigmoid, bias=V("a0", j)),
                  *([S("rw_a")] if j else []))
            ac.wait_ge(S("rw_g"), 1)
            for j in range(2):
                a(ac.copy(rg[:, j, 0:SEQ], bank(2 * j)))
                a(ac.copy(rg[:, j, SEQ:T], bank(2 * j + 1, 64)))
            ac.sem_inc(S("rw_g_out"), 1)
            for c in range(2):
                a(ac.activation(cols[:, CO + c, :], cols[:, CO + c, :], ACT.Sigmoid))
            ac.wait_ge(S("rw_kk_sum"), 1)
            for j in range(2):
                a(ac.activation(e3[:, j, 0:SEQ], bank(4 + 2 * j), ACT.Sqrt))
                a(ac.activation(e3[:, j, SEQ:T], bank(5 + 2 * j, 64), ACT.Sqrt))
            ac.sem_inc(S("rw_kk_len"), 1)
            ac.wait_ge(S("rw_cum"), 1)
            a(ac.activation(midp, mid, ACT.Exp))
            a(ac.activation(rcumx, rcumx, ACT.Exp), S("rw_e1"))
            a(ac.activation(e3, rcum, ACT.Exp, scale=-1.0), S("rw_e3"))
            a(ac.activation(rcum, rcum, ACT.Exp), S("rw_e2"))

        Yb2 = rkk

        def rwprep_dve(v):
            ve = nc.vector
            for j in range(2):
                v(ve.tensor_scalar(rkk[:, j, :], cols[:, CRK + j, :], V("kk", j), None, ALU.mult))
                v(ve.tensor_tensor(e3[:, j, :], rkk[:, j, :], rkk[:, j, :], ALU.mult), *([S("rw_kk_sq")] if j else []))
            v(ve.tensor_scalar(omka, vec[:, VEC["ka"]:VEC["ka"] + 2], -1.0, 1.0, ALU.mult, ALU.add))
            ve.wait_ge(S("rw_a"), 1)
            for j in range(2):
                v(ve.tensor_scalar(rk2[:, j, :], ra[:, j, :], V("ka", j), omka[:, j:j + 1], ALU.mult, ALU.add))
                v(ve.tensor_tensor(rk2[:, j, :], rk2[:, j, :], cols[:, CRK + j, :], ALU.mult))
            ve.wait_ge(S("rw_kk_len"), 1)
            v(ve.tensor_scalar(e3, e3, 1e-12, None, ALU.max))
            v(ve.reciprocal(e3, e3))
            v(ve.tensor_tensor(nbt, rkk, e3, ALU.mult))
            for j in range(2):
                v(ve.scalar_tensor_tensor(Yb2[:, j, :], cols[:, CR + j, :], V("rk", j), rk2[:, j, :], ALU.mult, ALU.mult))
            v(ve.tensor_scalar(kht, rcumx, -float(np.exp(-0.5)), None, ALU.mult))
            ve.wait_ge(S("rw_g_out"), 1)
            ve.sem_inc(S("rw_rk"), 1)
            for j in range(2):
                v(ve.tensor_tensor_scan(rcum[:, j, :], tb("reset"), kht[:, j, :], 0.0, ALU.mult, ALU.add))
            v(ve.tensor_tensor(rcumx, rcum, kht, ALU.subtract))
            for j in range(2):
                v(ve.tensor_copy(mid[:, j, :], rcum[:, j, P // 2 - 1:SEQ:P]))
            for buf in (rcum, rcumx):
                for j in range(2):
                    w = buf[:, j, 0:SEQ].rearrange("p (c t) -> p c t", t=P)
                    v(ve.tensor_tensor(w, w, mid[:, j, :].unsqueeze(2).to_broadcast([P, PT, P]), ALU.subtract))
            ve.sem_inc(S("rw_cum"), 1)
            ve.wait_ge(S("rw_rk_sum"), 1)
            ve.wait_ge(S("rw_e3"), 1)

            def krv(j, which):
                yield KR[:, j, 0:2 * SEQ].rearrange("p (i w t) -> p i w t", w=2, t=P)[:, :, which, :], 0, SEQ
                yield KR[:, j, 2 * SEQ + which * 64:2 * SEQ + which * 64 + 64].rearrange("p (i t) -> p i t", i=1), SEQ, T

            for j in range(2):
                for dst, a0, b0 in krv(j, 0):
                    n = min(P, b0 - a0)
                    v(ve.tensor_tensor(dst, nbt[:, j, a0:b0].rearrange("p (i t) -> p i t", t=n),
                                       rcumx[:, j, a0:b0].rearrange("p (i t) -> p i t", t=n), ALU.mult))
                v(ve.tensor_tensor(rcumx[:, j, 0:SEQ], cols[:, CRV + j, 0:SEQ], bank(2 * j), ALU.mult))
                v(ve.tensor_tensor(rcumx[:, j, SEQ:T], cols[:, CRV + j, SEQ:T], bank(2 * j + 1, 64), ALU.mult))
            v(ve.scalar_tensor_tensor(nbt, nbt, -1.0, ra, ALU.mult, ALU.mult))
            v(ve.tensor_tensor(nbt, nbt, e3, ALU.mult))
            v(ve.tensor_tensor(kht, rk2, e3, ALU.mult))
            ve.wait_ge(S("rw_e2"), 1)
            for j in range(2):
                for dst, a0, b0 in krv(j, 1):
                    n = min(P, b0 - a0)
                    v(ve.tensor_tensor(dst, cols[:, CR + j, a0:b0].rearrange("p (i t) -> p i t", t=n),
                                       rcum[:, j, a0:b0].rearrange("p (i t) -> p i t", t=n), ALU.mult))
                v(ve.tensor_copy(prod[:, j, 0:4], rcum[:, j, P - 1:SEQ:P]))
                v(ve.tensor_copy(prod[:, j, 4:12], rcum[:, j, SEQ + TS - 1:T:TS]))
            v(ve.tensor_copy(ups, prod[:, :, 0:4]))
            v(ve.tensor_tensor(ups[:, :, 0:3], ups[:, :, 0:3], midp[:, :, 1:4], ALU.mult), S("rw_ready"))
            for i, (t0, n) in enumerate(TILES):
                ve.wait_ge(S("rw_rows"), i + 1)
                v(ve.tensor_copy(TK[0:n, i, 0:512], ps_buf[0:n, 6, 0:512]))
                v(ve.tensor_copy(TK[0:n, i, 512:768], ps_buf[0:n, 7, 0:256]), S("rw_rows_out"))

        def levels(i):
            return 7 if i < 4 else 3

        def rw_pe():
            pe = nc.tensor
            lv, rounds = 0, 0
            for i, (t0, n) in enumerate(TILES):
                if i:
                    pe.wait_ge(S("rw_tile"), i)
                for h in range(4):
                    j, f = h // 2, h % 2
                    lo, hi = 64 * f, 64 * f + 64
                    both = KR[lo:hi, j, 2 * t0:2 * t0 + 2 * n]
                    pe.matmul(ps_buf[0:n, f, j * 2 * n:(j + 1) * 2 * n], nbt[lo:hi, j, t0:t0 + n], both, start=True, stop=True)
                    last = pe.matmul(ps_buf[0:n, 2 + f, j * 2 * n:(j + 1) * 2 * n], kht[lo:hi, j, t0:t0 + n], both,
                                     start=True, stop=True)
                last.then_inc(S("rw_prods"), 1)
                pe.wait_ge(S("rw_D1"), i + 1)
                for q in range(4):
                    last = pe.transpose(ps_buf[0:n, 4, q * n:q * n + n], Dt[0:n, q * n:q * n + n], ident[0:n, 0:n])
                last.then_inc(S("rw_D1T"), 1)
                for k in range(1, levels(i)):
                    lv += 1
                    pe.wait_ge(S("rw_N"), lv)
                    for q in range(4):
                        last = pe.matmul(ps_buf[0:n, 5, q * n:q * n + n], Nb[0:n, q * n:q * n + n], Dm[0:n, q * n:q * n + n],
                                         start=True, stop=True)
                    last.then_inc(S("rw_Y"), 1)
                    pe.wait_ge(S("rw_Y_out"), lv)
                    for q in range(4):
                        s_ = slice(q * n, q * n + n)
                        if k < levels(i) - 1:
                            pe.matmul(ps_buf[0:n, 6, s_], Dt[0:n, s_], Yb[0:n, s_], start=True, stop=True)
                        last = pe.matmul(ps_buf[0:n, 7, s_], Yb[0:n, s_], Dt[0:n, s_], start=True, stop=True)
                    last.then_inc(S("rw_DD"), 1)
                pe.wait_ge(S("rw_inv"), i + 1)
                if i < 4:
                    pe.wait_ge(S("rw_state"), i + 1)
                else:
                    pe.wait_ge(S("rw_state_in"), 16)
                for j in range(2):
                    o = ps_buf[0:n, 4, P * j:P * j + P]
                    if i < 4:
                        pe.matmul(o, kr(j, i, 0, n), S0[:, P * j:P * j + P], start=True, stop=False)
                    else:
                        pe.wait_ge(S("rw_kmask"), j + 1)
                        for b in range(NB):
                            last = pe.matmul(o, kmask[:, b, :], S0s[:, j, b, :], start=b == 0, stop=False)
                        last.then_inc(S("rw_kmask_used"), 1)
                    for f in range(2):
                        c = P * j + 64 * f
                        last = pe.matmul(ps_buf[0:n, 4, c:c + 64], M2[0:n, 2 * f + j, 0:n], TK[0:n, i, 512 + c:512 + c + 64],
                                         start=False, stop=f == 1)
                last.then_inc(S("rw_X"), 1)
                pe.wait_ge(S("rw_X_out"), i + 1)
                for h in range(4):
                    q = (h % 2) * 2 + h // 2
                    last = pe.matmul(ps_buf[0:n, 5, 64 * h:64 * h + 64], Dt[0:n, q * n:q * n + n],
                                     XU[0:n, 0, 64 * h:64 * h + 64], start=True, stop=True)
                last.then_inc(S("rw_U"), 1)
                pe.wait_ge(S("rw_U_out"), i + 1)
                for j in range(2):
                    o = ps_buf[0:n, 6, P * j:P * j + P]
                    if i < 4:
                        pe.matmul(o, kr(j, i, 1, n), S0[:, P * j:P * j + P], start=True, stop=False)
                    else:
                        pe.wait_ge(S("rw_rmask"), j + 1)
                        for b in range(NB):
                            last = pe.matmul(o, rmask[:, b, :], S0s[:, j, b, :], start=b == 0, stop=False)
                        last.then_inc(S("rw_rmask_used"), 1)
                    for f in range(2):
                        c = P * j + 64 * f
                        pe.matmul(ps_buf[0:n, 6, c:c + 64], M1[0:n, 2 * f + j, n:2 * n], XU[0:n, 1, c:c + 64],
                                  start=False, stop=False)
                        last = pe.matmul(ps_buf[0:n, 6, c:c + 64], M2[0:n, 2 * f + j, n:2 * n],
                                         TK[0:n, i, 512 + c:512 + c + 64], start=False, stop=f == 1)
                last.then_inc(S("rw_y"), 1)
                if i < 4:
                    for j in range(2):
                        o = ps_buf[:, 7, P * j:P * j + P]
                        pe.matmul(o, TK[0:n, i, P * j:P * j + P], XU[0:n, 1, P * j:P * j + P], start=True, stop=False)
                        last = pe.matmul(o, TK[0:n, i, 256 + P * j:256 + P * j + P], TK[0:n, i, 512 + P * j:512 + P * j + P],
                                         start=False, stop=True)
                    last.then_inc(S("rw_add"), 1)
                else:
                    for j in range(2):
                        pe.wait_ge(S("rw_umask"), j + 1)
                        for g in range(2):
                            o = ps_buf[:, 2 * j + g, 0:512]
                            pe.matmul(o, TK[0:n, i, P * j:P * j + P], umask[0:n, 4 * g:4 * g + 4, :], start=True, stop=False)
                            last = pe.matmul(o, TK[0:n, i, 256 + P * j:256 + P * j + P], vmask[0:n, 4 * g:4 * g + 4, :],
                                             start=False, stop=True)
                        last.then_inc(S("rw_add"), 1)

        def rw_dve(v):
            ve = nc.vector
            v(ve.memset(S0, 0.0), S("rw_state"))
            done = 0
            for i, (t0, n) in enumerate(TILES):
                mask = tb("rwp" if n == P else "rws", n)[:, 0:2 * n].unsqueeze(1).to_broadcast([n, 2, 2 * n])
                ve.wait_ge(S("rw_prods"), i + 1)
                for f in range(2):
                    for M, b in ((M1, f), (M2, 2 + f)):
                        v(ve.tensor_tensor(M[0:n, 2 * f:2 * f + 2, 0:2 * n],
                                           ps_buf[0:n, b, 0:4 * n].rearrange("p (j c) -> p j c", j=2), mask, ALU.mult))

                def lev(k):
                    return tb("lev", n)[:, P * k:P * k + n].unsqueeze(1).to_broadcast([n, 4, n])

                def q4(b):
                    return b[0:n, 0:4 * n].rearrange("p (q c) -> p q c", q=4)

                v(ve.tensor_tensor(q4(Dt), M1[0:n, :, 0:n], lev(0), ALU.mult))
                v(ve.tensor_tensor(q4(Dt), q4(Dt), ident[0:n, 0:n].unsqueeze(1).to_broadcast([n, 4, n]), ALU.add), S("rw_D1"))
                ve.wait_ge(S("rw_D1T"), i + 1)
                v(ve.tensor_copy(Dm[0:n, 0:4 * n], ps_buf[0:n, 4, 0:4 * n]))
                for k in range(1, levels(i)):
                    done += 1
                    v(ve.tensor_tensor(q4(Nb), M1[0:n, :, 0:n], lev(k), ALU.mult), S("rw_N"))
                    ve.wait_ge(S("rw_Y"), done)
                    v(ve.tensor_copy(Yb[0:n, 0:4 * n], ps_buf[0:n, 5, 0:4 * n]), S("rw_Y_out"))
                    ve.wait_ge(S("rw_DD"), done)
                    v(ve.tensor_tensor(Dt[0:n, 0:4 * n], Dt[0:n, 0:4 * n], ps_buf[0:n, 7, 0:4 * n], ALU.add))
                    if k < levels(i) - 1:
                        v(ve.tensor_tensor(Dm[0:n, 0:4 * n], Dm[0:n, 0:4 * n], ps_buf[0:n, 6, 0:4 * n], ALU.add))
                ve.sem_inc(S("rw_inv"), 1)

                def spread(dst, j, which, sig):
                    v(ve.tensor_tensor(dst, kr(j, 4, which, 64).unsqueeze(1).to_broadcast([P, NB, 64]),
                                       tb("segbt").rearrange("p (b t) -> p b t", b=NB), ALU.mult), S(sig))

                if i == 4:
                    spread(kmask, 0, 0, "rw_kmask")
                    spread(rmask, 0, 1, "rw_rmask")
                    ve.wait_ge(S("rw_kmask_used"), 1)
                    spread(kmask, 1, 0, "rw_kmask")
                ve.wait_ge(S("rw_X"), i + 1)
                v(ve.tensor_copy(XU[0:n, 0, :], ps_buf[0:n, 4, 0:256]), S("rw_X_out"))
                ve.wait_ge(S("rw_U"), i + 1)
                v(ve.tensor_copy(XU[0:n, 1, :], ps_buf[0:n, 5, 0:256]), S("rw_U_out"))
                if i == 4:
                    ve.wait_ge(S("rw_rmask_used"), 1)
                    spread(rmask, 1, 1, "rw_rmask")
                ve.wait_ge(S("rw_y"), i + 1)
                v(ve.tensor_copy(HB[0:n, 1, i, :], ps_buf[0:n, 6, 0:256]))
                if i < 4:
                    ve.wait_ge(S("rw_add"), i + 1)
                    v(ve.tensor_tensor(S0, S0, ps_buf[:, 7, 0:256], ALU.add))
                    for j in range(2):
                        w = S0[:, P * j:P * j + P]
                        v(ve.scalar_tensor_tensor(w, w, ups[:, j, i:i + 1], tb("onesbd"), ALU.mult, ALU.mult),
                          *([S("rw_state"), S("rw_tile")] if j else []))
                else:
                    for j in range(2):
                        if j:
                            ve.wait_ge(S("rw_add"), 5)
                        for m, src in ((umask, XU[0:64, 1, P * j:P * j + P]), (vmask, TK[0:64, 4, 512 + P * j:512 + P * j + P])):
                            v(ve.tensor_tensor(m[0:64], src.unsqueeze(1).to_broadcast([64, NB, P]),
                                               tb("segsb", 64).unsqueeze(2).to_broadcast([64, NB, P]), ALU.mult))
                        ve.sem_inc(S("rw_umask"), 1)
                    ve.wait_ge(S("rw_add"), 6)
                    for j in range(2):
                        for g in range(2):
                            w = S0s[:, j, 4 * g:4 * g + 4, :]
                            v(ve.tensor_tensor(w, w, ps_buf[:, 2 * j + g, 0:512].rearrange("p (b c) -> p b c", b=4), ALU.add))
                        v(ve.tensor_tensor(S0s[:, j], S0s[:, j], prod[:, j, 4:12].unsqueeze(2).to_broadcast([P, NB, P]), ALU.mult))
                    ve.sem_inc(S("rw_final"), 1)

        def hn_dve(v):
            ve = nc.vector
            hb = h_buf[:, :].rearrange("p (g d) -> p g d", d=HD)
            v(ve.tensor_reduce(n64, hb, AX.X, ALU.add))
            v(ve.tensor_scalar(n64, n64, 1.0 / HD, None, ALU.mult))
            v(ve.tensor_tensor(hb, hb, n64.unsqueeze(2).to_broadcast([P, 40, HD]), ALU.subtract))
            v(ve.tensor_tensor(hsq, hb, hb, ALU.mult))
            v(ve.tensor_reduce(n64b, hsq, AX.X, ALU.add))
            v(ve.tensor_scalar(n64b[:, 0:20], n64b[:, 0:20], 1.0 / HD, 1e-6, ALU.mult, ALU.add))
            v(ve.tensor_scalar(n64b[:, 20:40], n64b[:, 20:40], 1.0 / HD, 64e-5, ALU.mult, ALU.add), S("hn_var"))
            ve.wait_ge(S("hn_root"), 1)
            v(ve.reciprocal(n64b, n64b))
            v(ve.tensor_tensor(hb, hb, n64b.unsqueeze(2).to_broadcast([P, 40, HD]), ALU.mult), S("hn_done"))
            for m in range(2):
                for j in range(2):
                    ve.wait_ge(S("hn_T"), 2 * m + j + 1)
                    for a0, b0 in ((0, SEQ), (SEQ, T)):
                        b = bank(2 * (2 * m + j) + (a0 > 0), b0 - a0)
                        o = hmix[:, 2 * m + j, a0:b0]
                        if m == 0:
                            v(ve.scalar_tensor_tensor(o, b, V("mlw", j), cols[:, CO + j, a0:b0], ALU.mult, ALU.mult))
                        else:
                            v(ve.tensor_scalar(o, b, V("lnw", j), V("lnb", j), ALU.mult, ALU.add))
                            v(ve.tensor_tensor(o, o, rcumx[:, j, a0:b0], ALU.add))
                            v(ve.tensor_tensor(o, o, rg[:, j, a0:b0], ALU.mult))

        def hn_act(a):
            nc.scalar.wait_ge(S("hn_var"), 1)
            a(nc.scalar.activation(n64b, n64b, ACT.Sqrt), S("hn_root"))

        def hn_pe():
            pe = nc.tensor
            pe.wait_ge(S("hn_done"), 1)
            for m in range(2):
                for j in range(2):
                    for i, (t0, n) in enumerate(TILES):
                        b = 2 * (2 * m + j)
                        o = ps_buf[:, b, t0:t0 + n] if i < 4 else ps_buf[:, b + 1, 0:n]
                        last = pe.transpose(o, HB[0:n, m, i, P * j:P * j + P], ident[0:n, 0:n])
                    last.then_inc(S("hn_T"), 1)

        ROPED = [(CNQ, 0), (CNQ + 1, 1), (CNQ + 2, 2), (CNQ + 3, 3), (CSK, None), (CWK, None)]

        def cmp_pe():
            pe = nc.tensor
            for r_, (c, _) in enumerate(ROPED):
                if r_ >= 2:
                    pe.wait_ge(S("rope_out"), r_ - 1)
                b = 2 * (r_ % 2)
                pe.matmul(bank(b), tb("rot"), cols[:, c, 0:SEQ], start=True, stop=True)
                last = pe.matmul(bank(b + 1, 64), tb("rot"), cols[:, c, SEQ:T], start=True, stop=True)
                last.then_inc(S("rope_rot"), 1)
            pe.wait_ge(S("rope_out"), 6)
            for w, c in enumerate((CSV, CWV)):
                for i, (t0, n) in enumerate(TILES):
                    o = ps_buf[0:n, 2 * w, i * P:i * P + P] if i < 4 else ps_buf[0:n, 2 * w + 1, 0:P]
                    last = pe.transpose(o, cols[:, c, t0:t0 + n], ident)
            last.then_inc(S("at_vrows"), 1)
            pe.wait_ge(S("at_gspread"), 4)
            for q in range(2):
                last = pe.matmul(ps_buf[:, 4, 24 * q:24 * q + 24], rtmp[64:88, P * q:P * q + P], ident[64:88, 64:88], start=True, stop=True)
            last.then_inc(S("at_gates"), 1)
            pe.wait_ge(S("cmp_in"), 2)
            pe.wait_ge(S("at_rows_out"), 1)
            for j in range(2):
                pe.wait_ge(S("cw1_in"), 16 * (j + 1))
                if j == 0:
                    for b in range(NB):
                        pe.wait_ge(S(f"pages_{b}"), 16 * PAGES)
                for g in range(2):
                    lo = 64 * g
                    u = 2 * j + g
                    for p_ in range(CLEN):
                        pe.matmul(bank(2 * u, 9 * CMP), cw1[lo:lo + 64, p_, :],
                                  ckb[lo:lo + 64, :, j, p_:p_ + STRIDE * (CMP - 1) + 1:STRIDE],
                                  start=p_ == 0, stop=p_ == CLEN - 1)
                        last = pe.matmul(bank(2 * u + 1, 1), cw1[lo:lo + 64, p_, :],
                                         vec[lo:lo + 64, VEC["cpos"] + 32 * j + p_:VEC["cpos"] + 32 * j + p_ + 1],
                                         start=p_ == 0, stop=p_ == CLEN - 1)
                    last.then_inc(S("cmp_hid"), 1)
            pe.wait_ge(S("cmp_silu"), 4)
            pe.wait_ge(S("cw2_in"), 16)
            for g in range(2):
                pe.matmul(ps_buf[64 * g:64 * g + 64, g, 0:9 * CMP], cw2[:, 0, :], hid[:, g, :], start=True, stop=True)
                for s_ in range(9):
                    o = ps_buf[0:CMP, 2 + 2 * g, 64 * s_:64 * s_ + 64] if s_ < 8 else ps_buf[0:CMP, 3 + 2 * g, 0:64]
                    last = pe.matmul(o, hid[:, 2 + g, CMP * s_:CMP * s_ + CMP], cw2[:, 1, :], start=True, stop=True)
            last.then_inc(S("cmp_kv"), 1)

        def cmp_act(a):
            ac = nc.scalar
            a(ac.activation(cols[64:88, CGATE, :], cols[64:88, CGATE, :], ACT.Sigmoid), S("at_gsig"))
            ac.wait_ge(S("cmp_bias"), 4)
            for u in range(4):
                a(ac.activation(hid[:, u, :], bank(2 * u, 9 * CMP), ACT.Silu, bias=posb[:, u:u + 1]), S("cmp_silu"))

        def cmp_dve(v):
            ve = nc.vector
            for r_, (c, q) in enumerate(ROPED):
                ve.wait_ge(S("rope_rot"), r_ + 1)
                b = 2 * (r_ % 2)
                dst = cols[:, c, :] if q is None else qrot[:, q, :]
                v(ve.tensor_tensor(rtmp[:, 0:SEQ], bank(b), tb("sin")[:, 0:SEQ], ALU.mult))
                v(ve.tensor_tensor(rtmp[:, SEQ:T], bank(b + 1, 64), tb("sin")[:, SEQ:T], ALU.mult))
                v(ve.tensor_tensor(dst, cols[:, c, :], tb("cos"), ALU.mult))
                v(ve.tensor_tensor(dst, dst, rtmp, ALU.add), S("rope_out"))
            ve.wait_ge(S("at_gsig"), 1)
            for i in range(4):
                v(ve.tensor_copy(rtmp[64:88, 0:256].rearrange("p (b i t) -> p b i t", i=4, t=TS)[:, :, i, :],
                                 cols[64:88, CGATE, SEQ:T].rearrange("p (b t) -> p b t", t=TS)), S("at_gspread"))
            for j in range(2):
                v(ve.tensor_copy(ckb[:, 8, j, :], cols[:, CCK + j, 0:SEQ]), S("cmp_in"))
            for w, src in ((0, None), (1, qrot)):
                for i in range(4):
                    s_ = cols[:, CNQ + i, SEQ:T] if src is None else qrot[:, i, SEQ:T]
                    dst = qrs[:, w, :].rearrange("p (b i t) -> p b i t", i=4, t=TS)[:, :, i, :]
                    v(ve.tensor_copy(dst, s_.rearrange("p (b t) -> p b t", t=TS)))
            ve.wait_ge(S("at_vrows"), 1)
            for w, dst in enumerate((svt, wvt)):
                v(ve.tensor_copy(dst[:, 0:4, :], bank(2 * w).rearrange("p (i c) -> p i c", i=4)))
                v(ve.tensor_copy(dst[0:64, 4, :], ps_buf[0:64, 2 * w + 1, 0:P]))
            ve.wait_ge(S("at_gates"), 1)
            for q in range(2):
                v(ve.tensor_tensor(sg24, ps_buf[:, 4, 24 * q:24 * q + 24], tb("rowi"), ALU.mult))
                v(ve.tensor_reduce(sgate[:, q, :, :], sg24.rearrange("p (g i k) -> p g k i", g=2, i=4), AX.X, ALU.add),
                  *([S("at_rows_out")] if q else []))
            for u in range(4):
                ve.wait_ge(S("cmp_hid"), u + 1)
                v(ve.tensor_copy(posb[:, u:u + 1], bank(2 * u + 1, 1)), S("cmp_bias"))
            ve.wait_ge(S("cmp_kv"), 1)
            for g in range(2):
                v(ve.tensor_copy(ckT[64 * g:64 * g + 64, :], ps_buf[64 * g:64 * g + 64, g, 0:9 * CMP]))
                v(ve.tensor_copy(cvt[0:CMP, 0:8, g, :], ps_buf[0:CMP, 2 + 2 * g, :].rearrange("p (s d) -> p s d", s=8)))
                v(ve.tensor_copy(cvt[0:CMP, 8, g, :], ps_buf[0:CMP, 3 + 2 * g, 0:64]))

        UNITS = [(i, h, g, br) for i in range(PT) for h in range(4) for g in range(2) for br in range(3)]
        NU = len(UNITS)

        def width(u):
            i, h, g, br = UNITS[u]
            return CMP if br == 0 else P * (i + 1)

        def at_pe():
            pe = nc.tensor

            def scores(u):
                i, h, g, br = UNITS[u]
                lo, t0, n = 64 * g, P * i, width(u)
                if u >= 2:
                    pe.wait_ge(S("at_exp"), u - 1)
                q = (cols[lo:lo + 64, CNQ + h, t0:t0 + P] if br == 0 else qrot[lo:lo + 64, h, t0:t0 + P])
                if br == 0:
                    kk = ckT[lo:lo + 64, 8 * CMP:9 * CMP]
                    mask = tb("cma")[:, CMP * i:CMP * i + CMP]
                else:
                    kk = cols[lo:lo + 64, CSK if br == 1 else CWK, 0:n]
                    mask = tb("tri")
                pe.matmul(bank(u % 2, n), q, kk, start=True, stop=False)
                m = mask.shape[1]
                pe.matmul(ps_buf[:, u % 2, n - m:n], ident, mask, start=False, stop=True).then_inc(S("at_scores"), 1)

            def turn(u):
                i, h, g, br = UNITS[u]
                n = width(u)
                pe.wait_ge(S("at_ready"), u + 1)
                if u >= 2:
                    pe.wait_ge(S("at_PT"), u - 1)
                for c in range((n + P - 1) // P):
                    w = min(P, n - P * c)
                    last = pe.transpose(ps_buf[0:w, 2 + u % 2, P * c:P * c + P], Sb[:, u % 2, P * c:P * c + w], ident)
                last.then_inc(S("at_T"), 1)

            def weigh(u):
                i, h, g, br = UNITS[u]
                n = width(u)
                pe.wait_ge(S("at_PT"), u + 1)
                if u >= 2:
                    pe.wait_ge(S("at_acc"), u - 1)
                cs = (n + P - 1) // P
                for c in range(cs):
                    w = min(P, n - P * c)
                    val = cvt[0:CMP, 8, g, :] if br == 0 else (svt if br == 1 else wvt)[:, c, 64 * g:64 * g + 64]
                    last = pe.matmul(bank(4 + u % 2, 64), PTb[0:w, u % 2, c, :], val, start=c == 0, stop=c == cs - 1)
                last.then_inc(S("at_pv"), 1)

            for s_ in range(NU + 2):
                if s_ < NU:
                    scores(s_)
                if 1 <= s_ <= NU:
                    turn(s_ - 1)
                if s_ >= 2:
                    weigh(s_ - 2)
            for h in range(4):
                if h == 0:
                    pe.wait_ge(S("at_acc"), NU)
                for i in range(PT):
                    last = pe.transpose(ps_buf[:, h, P * i:P * i + P], oacc[:, i, h, :], ident)
                last.then_inc(S("at_oT"), 1)

        def at_act(a):
            ac = nc.scalar
            for s_ in range(NU + 1):
                if s_ < NU:
                    u = s_
                    ac.wait_ge(S("at_max"), u + 1)
                    if u >= 2:
                        ac.wait_ge(S("at_T"), u - 1)
                    a(ac.activation(Sb[:, u % 2, 0:width(u)], bank(u % 2, width(u)), ACT.Exp, scale=SCALE,
                                    bias=stat[:, u % 4, 1:2], accum_out=stat[:, u % 4, 2:3]), S("at_exp"))
                if s_ >= 1:
                    u = s_ - 1
                    n = width(u)
                    ac.wait_ge(S("at_T"), u + 1)
                    if u >= 2:
                        ac.wait_ge(S("at_pv"), u - 1)
                    if n == CMP:
                        a(ac.copy(PTb[0:CMP, u % 2, 0, :], ps_buf[0:CMP, 2 + u % 2, 0:P]), S("at_PT"))
                    else:
                        a(ac.copy(PTb[:, u % 2, 0:n // P, :], bank(2 + u % 2, n).rearrange("p (c t) -> p c t", t=P)),
                          S("at_PT"))

        def at_dve(v):
            ve = nc.vector
            for s_ in range(NU + 2):
                if s_ < NU:
                    u = s_
                    st = stat[:, u % 4, :]
                    ve.wait_ge(S("at_scores"), u + 1)
                    v(ve.tensor_reduce(st[:, 0:1], bank(u % 2, width(u)), AX.X, ALU.max))
                    v(ve.tensor_scalar(st[:, 1:2], st[:, 0:1], -SCALE, None, ALU.mult), S("at_max"))
                if 1 <= s_ <= NU:
                    u = s_ - 1
                    i, h, g, br = UNITS[u]
                    st = stat[:, u % 4, :]
                    ve.wait_ge(S("at_exp"), u + 1)
                    if br == 0:
                        w = Sb[:, u % 2, 0:CMP]
                        v(ve.tensor_tensor(w, w, tb("cm1")[:, CMP * i:CMP * i + CMP], ALU.mult), S("at_ready"))
                        v(ve.tensor_reduce(st[:, 2:3], w, AX.X, ALU.add))
                        v(ve.tensor_scalar(st[:, 2:3], st[:, 2:3], 1e-30, None, ALU.max))
                    else:
                        ve.sem_inc(S("at_ready"), 1)
                if s_ >= 2:
                    u = s_ - 2
                    i, h, g, br = UNITS[u]
                    st = stat[:, u % 4, :]
                    k = 3 * (4 * g + h) + br
                    v(ve.reciprocal(st[:, 3:4], st[:, 2:3]))
                    v(ve.tensor_tensor(st[:, 3:4], st[:, 3:4], gates[:, i, k:k + 1], ALU.mult))
                    ve.wait_ge(S("at_pv"), u + 1)
                    o = oacc[:, i, h, 64 * g:64 * g + 64]
                    if br == 0:
                        v(ve.tensor_scalar(o, bank(4 + u % 2, 64), st[:, 3:4], None, ALU.mult), S("at_acc"))
                    else:
                        v(ve.scalar_tensor_tensor(o, bank(4 + u % 2, 64), st[:, 3:4], o, ALU.mult, ALU.add), S("at_acc"))
            for h in range(4):
                ve.wait_ge(S("at_oT"), h + 1)
                v(ve.tensor_copy(hmix[:, 4 + h, 0:SEQ], bank(h)))

        SU = [(q, g) for q in range(2) for g in range(2)]

        def sa_pe():
            pe = nc.tensor
            for u, (q, g) in enumerate(SU):
                lo = 64 * g
                qc = slice(128 * q, 128 * q + 128)
                if g == 0:
                    for b in range(4):
                        pe.wait_ge(S(f"qpages_{b}"), 16 * (2 * PAGES) * (q + 1))
                    pe.wait_ge(S("qwin"), 16 * 8 * (q + 1))
                if u:
                    pe.wait_ge(S("sa_unit"), u)
                for b in range(4):
                    last = pe.matmul(ps_buf[32 * b:32 * b + 32, 0, 0:CMP], qrs[lo:lo + 64, 0, 128 * q + 32 * b:128 * q + 32 * b + 32],
                                     ckT[lo:lo + 64, CMP * (4 * q + b):CMP * (4 * q + b) + CMP], start=True, stop=True)
                last.then_inc(S("sa_scores"), 1)
                pe.wait_ge(S("sa_p"), 3 * u + 1)
                pe.transpose(ps_buf[0:CMP, 2, 0:P], Sb[:, 0, 0:CMP], ident).then_inc(S("sa_T"), 1)
                pe.wait_ge(S("sa_PT"), 3 * u + 1)
                for b in range(4):
                    pe.matmul(ps_buf[32 * b:32 * b + 32, 4, 0:64], PTb[0:CMP, 0, 0, 32 * b:32 * b + 32],
                              cvt[0:CMP, 4 * q + b, g, :], start=True, stop=True)
                pe.matmul(bank(5, 9), PTb[0:CMP, 0, 0, :], tb("ov"), start=True, stop=True).then_inc(S("sa_pv"), 1)
                pe.wait_ge(S("sa_imp1"), u + 1)
                pe.matmul(bank(5, 9), tb("same"), impz, start=True, stop=True).then_inc(S("sa_imp"), 1)
                for br in (1, 2):
                    kq, kc = (skq, CSK) if br == 1 else (wkq, CWK)
                    vq, vt = (svq, svt) if br == 1 else (wvq, wvt)
                    pe.wait_ge(S("sa_acc"), 3 * u + br)
                    for b in range(4):
                        pe.matmul(ps_buf[32 * b:32 * b + 32, 0, 0:512], qrs[lo:lo + 64, 1, 128 * q + 32 * b:128 * q + 32 * b + 32],
                                  kq[lo:lo + 64, b, :], start=True, stop=True)
                    pe.matmul(bank(1, 64), qrs[lo:lo + 64, 1, qc], cols[lo:lo + 64, kc, SEQ:T], start=True,
                              stop=True).then_inc(S("sa_scores"), 1)
                    pe.wait_ge(S("sa_p"), 3 * u + br + 1)
                    for c in range(4):
                        pe.transpose(ps_buf[:, 2, P * c:P * c + P], Sb[:, 0, P * c:P * c + P], ident)
                    pe.transpose(ps_buf[0:64, 3, 0:P], Sb[:, 0, SEQ:T], ident).then_inc(S("sa_T"), 1)
                    pe.wait_ge(S("sa_PT"), 3 * u + br + 1)
                    for b in range(4):
                        o = ps_buf[32 * b:32 * b + 32, 4, 0:64]
                        r_ = slice(32 * b, 32 * b + 32)
                        for c in range(4):
                            pe.matmul(o, PTb[:, 0, c, r_], vq[:, b, c, lo:lo + 64], start=c == 0, stop=False)
                        last = pe.matmul(o, PTb[0:64, 0, 4, r_], vt[0:64, 4, lo:lo + 64], start=False, stop=True)
                    last.then_inc(S("sa_pv"), 1)
            pe.wait_ge(S("sa_unit"), 4)
            for q in range(2):
                last = pe.transpose(ps_buf[:, 6, P * q:P * q + P], osamp[:, q, :], ident)
            last.then_inc(S("sa_oT"), 1)

        def sa_act(a):
            ac = nc.scalar
            for u in range(4):
                for br in range(3):
                    n = CMP if br == 0 else T
                    ac.wait_ge(S("sa_max"), 3 * u + br + 1)
                    src = bank(0, CMP) if br == 0 else Sb[:, 0, :]
                    a(ac.activation(Sb[:, 0, 0:n], src, ACT.Exp, scale=SCALE, bias=stat[:, 0, 1:2],
                                    accum_out=stat[:, 0, 2:3]), S("sa_exp"))
                    ac.wait_ge(S("sa_T"), 3 * u + br + 1)
                    if br == 0:
                        a(ac.copy(PTb[0:CMP, 0, 0, :], ps_buf[0:CMP, 2, 0:P]), S("sa_PT"))
                    else:
                        a(ac.copy(PTb[:, 0, 0:4, :], bank(2).rearrange("p (c t) -> p c t", t=P)))
                        a(ac.copy(PTb[0:64, 0, 4, :], ps_buf[0:64, 3, 0:P]), S("sa_PT"))

        def sa_dve(v):
            ve = nc.vector
            st = stat[:, 0, :]
            v(ve.memset(kbias, 0.0))
            for u, (q, g) in enumerate(SU):
                for br in range(3):
                    ve.wait_ge(S("sa_scores"), 3 * u + br + 1)
                    if br == 0:
                        src = bank(0, CMP)
                    else:
                        src = Sb[:, 0, :]
                        if br == 1:
                            v(ve.tensor_tensor(Sb[:, 0, 0:512].rearrange("p (s k) -> p s k", s=8),
                                               bank(0).rearrange("p (s k) -> p s k", s=8),
                                               kbias.unsqueeze(2).to_broadcast([P, 8, HD]), ALU.add))
                        else:
                            v(ve.tensor_copy(Sb[:, 0, 0:512], bank(0)))
                            v(ve.tensor_tensor(Sb[:, 0, 0:8], Sb[:, 0, 0:8], tb("winm"), ALU.add))
                        v(ve.tensor_tensor(Sb[:, 0, SEQ:T], bank(1, 64), tb("newm")[:, 64 * q:64 * q + 64], ALU.add))
                    v(ve.tensor_reduce(st[:, 0:1], src, AX.X, ALU.max))
                    v(ve.tensor_scalar(st[:, 1:2], st[:, 0:1], -SCALE, None, ALU.mult), S("sa_max"))
                    ve.wait_ge(S("sa_exp"), 3 * u + br + 1)
                    v(ve.reciprocal(st[:, 3:4], st[:, 2:3]))
                    if br == 0:
                        v(ve.tensor_scalar(Sb[:, 0, 0:CMP], Sb[:, 0, 0:CMP], st[:, 3:4], None, ALU.mult), S("sa_p"))
                    else:
                        v(ve.tensor_tensor(st[:, 3:4], st[:, 3:4], sgate[:, q, g, br:br + 1], ALU.mult), S("sa_p"))
                    ve.wait_ge(S("sa_pv"), 3 * u + br + 1)
                    o = osamp[:, q, 64 * g:64 * g + 64]
                    if br == 0:
                        v(ve.tensor_scalar(o, bank(4, 64), sgate[:, q, g, 0:1], None, ALU.mult))
                        v(ve.tensor_copy(impz, bank(5, 9)), S("sa_imp1"))
                        ve.wait_ge(S("sa_imp"), u + 1)
                        v(ve.tensor_copy(imps, bank(5, 9)))
                        v(ve.tensor_reduce(iw[:, 6:7], imps[:, 1:7], AX.X, ALU.min))
                        v(ve.tensor_scalar(iw[:, 0:6], imps[:, 1:7], iw[:, 6:7], None, ALU.is_equal))
                        v(ve.tensor_tensor(iw[:, 0:6], iw[:, 0:6], tb("rank")[:, 0:6], ALU.mult))
                        v(ve.tensor_reduce(iw[:, 6:7], iw[:, 0:6], AX.X, ALU.max))
                        v(ve.tensor_scalar(kbias[:, 1:7], tb("rank")[:, 0:6], iw[:, 6:7], NEG, ALU.is_equal, ALU.mult))
                        ve.sem_inc(S("sa_acc"), 1)
                    else:
                        v(ve.scalar_tensor_tensor(o, bank(4, 64), st[:, 3:4], o, ALU.mult, ALU.add), S("sa_acc"),
                          *([S("sa_unit")] if br == 2 else []))
            ve.wait_ge(S("sa_oT"), 1)
            for q in range(2):
                for h in range(4):
                    v(ve.tensor_copy(hmix[:, 4 + h, SEQ + 32 * q:SEQ + 32 * q + 32].rearrange("p (b t) -> p b t", t=TS),
                                     ps_buf[:, 6, P * q:P * q + P].rearrange("p (b i t) -> p b i t", i=4, t=TS)[:, :, h, :]))

        def wo_sp(l):
            for c in range(KD):
                if c >= 2:
                    sync.wait_ge(S("wo_done"), c - 1)
                sync.dma_start(woring[:, c % 2], A["w_out"][l * KD + c]).then_inc(S(f"w_out_{c % 2}"), 16)

        def wo_pe():
            pe = nc.tensor
            for c in range(KD):
                pe.wait_ge(S(f"w_out_{c % 2}"), 16 * (c // 2 + 1))
                if c >= 3:
                    pe.wait_ge(S("wo_out"), c - 2)
                b = 2 * (c % 3)
                for k in range(KD):
                    pe.matmul(bank(b), woring[:, c % 2, k, :], hmix[:, k, 0:SEQ], start=k == 0, stop=k == KD - 1)
                    last = pe.matmul(bank(b + 1, 64), woring[:, c % 2, k, :], hmix[:, k, SEQ:T], start=k == 0, stop=k == KD - 1)
                last.then_inc(S("wo_done"), 1)

        def wo_dve(v):
            ve = nc.vector
            for c in range(KD):
                ve.wait_ge(S("wo_done"), c + 1)
                b = 2 * (c % 3)
                v(ve.tensor_tensor(x[:, c, 0:SEQ], x[:, c, 0:SEQ], bank(b), ALU.add))
                v(ve.tensor_tensor(x[:, c, SEQ:T], x[:, c, SEQ:T], bank(b + 1, 64), ALU.add), S("wo_out"))

        def rt_pe():
            pe = nc.tensor
            pe.wait_ge(S("ffn_norm_done"), KD)
            for i, (t0, n) in enumerate(TILES):
                for k in range(KD):
                    last = pe.matmul(ps_buf[0:n, 2, 8 * i:8 * i + 8], xn[:, k, t0:t0 + n], router[:, k, :], start=k == 0,
                                     stop=k == KD - 1)
            last.then_inc(S("rt_logits"), 1)
            pe.wait_ge(S("rt_comb"), 1)
            for i, (t0, n) in enumerate(TILES):
                o = ps_buf[0:8, 3, t0:t0 + n] if i < 4 else ps_buf[0:8, 4, 0:n]
                last = pe.transpose(o, lw[0:n, 0, 8 * i:8 * i + 8], ident[0:n, 0:n])
            last.then_inc(S("rt_T"), 1)
            pe.wait_ge(S("rt_cT"), 1)
            for e in range(8):
                if e >= 4:
                    pe.wait_ge(S("rt_spread_out"), e - 3)
                b = 2 * (e % 4)
                sel = ident[0:8, e:e + 1].to_broadcast([8, P])
                pe.matmul(bank(b), sel, cT[0:8, 0:SEQ], start=True, stop=True)
                pe.matmul(bank(b + 1, 64), sel, cT[0:8, SEQ:T], start=True, stop=True).then_inc(S("rt_spread"), 1)

        def rt_act(a):
            ac = nc.scalar
            ac.wait_ge(S("rt_diff"), 1)
            a(ac.activation(lw[:, 7, 0:5], lw[:, 7, 0:5], ACT.Exp), S("rt_exp"))

        def rt_dve(v):
            ve = nc.vector

            def g5(k):
                return lw[:, k, :].rearrange("p (i e) -> p i e", i=5)

            def spread5(ap):
                return ap.unsqueeze(2).to_broadcast([P, 5, 8])

            v(ve.memset(lg, 0.0))
            ve.wait_ge(S("rt_logits"), 1)
            v(ve.tensor_copy(lg[:, 0:4, :], ps_buf[:, 2, 0:32].rearrange("p (i e) -> p i e", i=4)))
            v(ve.tensor_copy(lg[0:64, 4, :], ps_buf[0:64, 2, 32:40]))
            m = [lw[:, 5, 0:5], lw[:, 6, 0:5]]
            rank = tb("rrank").rearrange("p (i e) -> p i e", i=5)
            for k in range(2):
                v(ve.tensor_reduce(m[k], lg, AX.X, ALU.max))
                v(ve.tensor_tensor(g5(4), lg, spread5(m[k]), ALU.is_equal))
                v(ve.tensor_tensor(g5(4), g5(4), rank, ALU.mult))
                v(ve.tensor_reduce(lw[:, 7, 8:13], g5(4), AX.X, ALU.max))
                v(ve.tensor_tensor(g5(1 + k), rank, spread5(lw[:, 7, 8:13]), ALU.is_equal))
                if k == 0:
                    v(ve.scalar_tensor_tensor(lg, g5(1), NEG, lg, ALU.mult, ALU.add))
            v(ve.tensor_tensor(lw[:, 7, 0:5], m[1], m[0], ALU.subtract), S("rt_diff"))
            ve.wait_ge(S("rt_exp"), 1)
            v(ve.tensor_scalar(lw[:, 5, 0:5], lw[:, 7, 0:5], 1.0, None, ALU.add))
            v(ve.reciprocal(lw[:, 5, 0:5], lw[:, 5, 0:5]))
            v(ve.tensor_tensor(lw[:, 6, 0:5], lw[:, 7, 0:5], lw[:, 5, 0:5], ALU.mult))
            v(ve.tensor_tensor(g5(1), g5(1), spread5(lw[:, 5, 0:5]), ALU.mult))
            v(ve.tensor_tensor(g5(2), g5(2), spread5(lw[:, 6, 0:5]), ALU.mult))
            v(ve.tensor_tensor(lw[:, 0, :], lw[:, 1, :], lw[:, 2, :], ALU.add))
            v(ve.tensor_scalar(lw[:, 0, :], lw[:, 0, :], -1.0, V("flag"), ALU.add, ALU.mult))
            v(ve.tensor_scalar(lw[:, 0, :], lw[:, 0, :], 1.0, None, ALU.add), S("rt_comb"))
            ve.wait_ge(S("rt_T"), 1)
            v(ve.tensor_copy(cT[0:8, 0:SEQ], ps_buf[0:8, 3, :]))
            v(ve.tensor_copy(cT[0:8, SEQ:T], ps_buf[0:8, 4, 0:64]), S("rt_cT"))
            for e in range(8):
                ve.wait_ge(S("rt_spread"), e + 1)
                b = 2 * (e % 4)
                v(ve.tensor_copy(comb[:, e, 0:SEQ], bank(b)))
                v(ve.tensor_copy(comb[:, e, SEQ:T], bank(b + 1, 64)), S("rt_spread_out"))

        def ex_sp(e):
            for f in range(FC):
                if f >= 2:
                    sync.wait_ge(S("ex_up"), f - 1)
                sync.dma_start(w13[:, f % 2], A["w13"][e * FC + f]).then_inc(S(f"w13_in_{f % 2}"), 16)
                if f < 3:
                    sync.dma_start(w2r[:, f], A["w2"][e * KD + f]).then_inc(S(f"w2_in_{f}"), 16)
            for c in range(3, KD):
                sync.wait_ge(S("ex_down"), c - 2)
                sync.dma_start(w2r[:, c % 3], A["w2"][e * KD + c]).then_inc(S(f"w2_in_{c % 3}"), 16)

        def ex_pe():
            pe = nc.tensor
            for f in range(FC):
                pe.wait_ge(S(f"w13_in_{f % 2}"), 16 * (f // 2 + 1))
                if f >= 2:
                    pe.wait_ge(S("ex_h"), f - 1)
                for w in range(2):
                    b = 4 * (f % 2) + 2 * w
                    for k in range(KD):
                        pe.matmul(bank(b), w13[:, f % 2, w, k, :], xn[:, k, 0:SEQ], start=k == 0, stop=k == KD - 1)
                        last = pe.matmul(bank(b + 1, 64), w13[:, f % 2, w, k, :], xn[:, k, SEQ:T], start=k == 0,
                                         stop=k == KD - 1)
                last.then_inc(S("ex_up"), 1)
            for c in range(KD):
                pe.wait_ge(S(f"w2_in_{c % 3}"), 16 * (c // 3 + 1))
                if c == 0:
                    pe.wait_ge(S("ex_h"), FC)
                if c >= 3:
                    pe.wait_ge(S("ex_out"), c - 2)
                b = 2 * (c % 3)
                for k in range(FC):
                    pe.matmul(bank(b), w2r[:, c % 3, k, :], hff[:, k, 0:SEQ], start=k == 0, stop=k == FC - 1)
                    last = pe.matmul(bank(b + 1, 64), w2r[:, c % 3, k, :], hff[:, k, SEQ:T], start=k == 0, stop=k == FC - 1)
                last.then_inc(S("ex_down"), 1)

        def ex_act(a):
            ac = nc.scalar
            for f in range(FC):
                ac.wait_ge(S("ex_up"), f + 1)
                if f >= 2:
                    ac.wait_ge(S("ex_h"), f - 1)
                b = 4 * (f % 2)
                a(ac.activation(sg[:, f % 2, 0:SEQ], bank(b), ACT.Silu))
                a(ac.activation(sg[:, f % 2, SEQ:T], bank(b + 1, 64), ACT.Silu), S("ex_silu"))

        def ex_dve(v, e):
            ve = nc.vector
            for f in range(FC):
                ve.wait_ge(S("ex_silu"), f + 1)
                b = 4 * (f % 2) + 2
                v(ve.tensor_tensor(hff[:, f, 0:SEQ], sg[:, f % 2, 0:SEQ], bank(b), ALU.mult))
                v(ve.tensor_tensor(hff[:, f, SEQ:T], sg[:, f % 2, SEQ:T], bank(b + 1, 64), ALU.mult))
                v(ve.tensor_tensor(hff[:, f, :], hff[:, f, :], comb[:, bass.ds(e, 1), :].rearrange("p a t -> p (a t)"),
                                   ALU.mult), S("ex_h"))
            for c in range(KD):
                ve.wait_ge(S("ex_down"), c + 1)
                b = 2 * (c % 3)
                v(ve.tensor_tensor(x[:, c, 0:SEQ], x[:, c, 0:SEQ], bank(b), ALU.add))
                v(ve.tensor_tensor(x[:, c, SEQ:T], x[:, c, SEQ:T], bank(b + 1, 64), ALU.add), S("ex_out"))

        def iteration_ends(eng, tag):
            eng.drain().then_inc(S(tag + "_arrived"), 1)
            eng.wait_ge(S(tag + "_go"), 1)
            eng.sem_inc(S(tag + "_left"), 1)

        def is_expert(name):
            return name.startswith(("ex_", "w13_in", "w2_in"))

        def clear(tag):
            sync.wait_ge(S(tag + "_arrived"), 3)
            S(tag + "_go"), S(tag + "_left")
            if tag == "half":
                own = {s.num for s in shared}
            else:
                own = {s.num for n, s in sems.items() if not n.startswith(("g_", "layer_", "expert_", "half_"))
                       and is_expert(n) == (tag == "expert")}
            own = sorted(own | {S(tag + "_arrived").num})
            k = 0
            while k < len(own):
                m = k
                while m + 1 < len(own) and own[m + 1] == own[m] + 1:
                    m += 1
                sync.sem_clear(range(own[k], own[m] + 1))
                k = m + 1
            sync.sem_inc(S(tag + "_go"), 1)
            sync.wait_ge(S(tag + "_left"), 3)
            for n in ("_go", "_left"):
                sync.sem_clear(S(tag + n))

        def experts(l):
            return 2 + 6 * l

        with nc.Block() as block:
            @block.vector
            def _(eng):
                v = Chain(eng, S("dve_chain"))
                eng.wait_ge(S("g_in"), 80)
                v0 = Chain(eng, S("g_chain_dve"))
                v0(nc.vector.memset(gates, 0.0))
                with eng.Fori(0, DEPTH) as l:
                    eng.wait_ge(S("small_in"), 48)
                    norm_dve(v, "mix_norm", rstd, lambda k: V("nmix", k))
                    proj_dve(v)
                    meet(eng, "dve")
                    rows_dve(v)
                    ml_dve(v)
                    eng.wait_ge(S("ml_outs"), 48)
                    meet(eng, "dve")
                    rwprep_dve(v)
                    rw_dve(v)
                    hn_dve(v)
                    eng.wait_ge(S("rw_outs"), 32)
                    iteration_ends(eng, "half")
                    cmp_dve(v)
                    meet(eng, "dve")
                    at_dve(v)
                    meet(eng, "dve")
                    sa_dve(v)
                    meet(eng, "dve")
                    wo_dve(v)
                    eng.wait_ge(S("kv_outs"), 32)
                    meet(eng, "dve")
                    norm_dve(v, "ffn_norm", rstd2, lambda k: V("nffn", k))
                    rt_dve(v)
                    meet(eng, "dve")
                    with eng.Fori(0, experts(l)) as e:
                        ve_ = Chain(eng, S("ex_chain_dve"))
                        ex_dve(ve_, e)
                        iteration_ends(eng, "expert")
                    iteration_ends(eng, "layer")
                norm_dve(v0, "g_fin", rstd, lambda k: nfin[:, k:k + 1])

            @block.scalar
            def _(eng):
                a = Chain(eng, S("act_chain"))
                eng.wait_ge(S("g_in"), 80)
                with eng.Fori(0, DEPTH) as l:
                    eng.wait_ge(S("small_in"), 48)
                    norm_act(a, "mix_norm", rstd)
                    proj_act(a)
                    meet(eng, "act")
                    rows_act(a)
                    ml_act(a)
                    meet(eng, "act")
                    rwprep_act(a)
                    hn_act(a)
                    iteration_ends(eng, "half")
                    cmp_act(a)
                    meet(eng, "act")
                    at_act(a)
                    meet(eng, "act")
                    sa_act(a)
                    meet(eng, "act")
                    meet(eng, "act")
                    norm_act(a, "ffn_norm", rstd2)
                    rt_act(a)
                    meet(eng, "act")
                    with eng.Fori(0, experts(l)) as e:
                        ae = Chain(eng, S("ex_chain_act"))
                        ex_act(ae)
                        iteration_ends(eng, "expert")
                    iteration_ends(eng, "layer")
                norm_act(Chain(eng, S("g_chain_act")), "g_fin", rstd)

            @block.tensor
            def _(eng):
                eng.wait_ge(S("g_in"), 80)
                with eng.Fori(0, DEPTH) as l:
                    norm_pe("mix_norm")
                    proj_pe()
                    meet(eng, "pe")
                    ml_pe()
                    meet(eng, "pe")
                    rwprep_pe()
                    rw_pe()
                    hn_pe()
                    iteration_ends(eng, "half")
                    cmp_pe()
                    meet(eng, "pe")
                    at_pe()
                    meet(eng, "pe")
                    sa_pe()
                    meet(eng, "pe")
                    wo_pe()
                    meet(eng, "pe")
                    norm_pe("ffn_norm")
                    rt_pe()
                    meet(eng, "pe")
                    with eng.Fori(0, experts(l)) as e:
                        ex_pe()
                        iteration_ends(eng, "expert")
                    iteration_ends(eng, "layer")
                norm_pe("g_fin")

            @block.sync
            def _(eng):
                eng.dma_start(tab[:, :], A["tab"]).then_inc(S("g_in"), 16)
                eng.dma_start(x, A["x"]).then_inc(S("g_in"), 16)
                eng.dma_start(router, A["router"]).then_inc(S("g_in"), 16)
                eng.dma_start(nfin, A["nfin"]).then_inc(S("g_in"), 16)
                eng.dma_start(page_buf[:, :], A["pages"]).then_inc(S("g_in"), 16)
                eng.wait_ge(S("g_in"), 80)
                for l in range(DEPTH):
                    for b in range(NB):
                        eng.dma_start(A["o_win"][l, b, 0:PAST - TS], A["win"][l, b, TS:PAST]).then_inc(S("g_win"), 16)
                with eng.Fori(0, DEPTH) as l:
                    one = lambda name, k: A[name][bass.ds(k, 1)]

                    def ld(dst, name, k, sem):
                        eng.dma_start(dst, A[name][k]).then_inc(S(sem), 16)

                    ld(vec, "vec", l, "small_in")
                    ld(state_in, "state", l, "small_in")
                    ld(m0_in[0:4, :], "m0", l, "small_in")
                    proj_sp(l)
                    eng.wait_ge(S("conv_done"), 4)
                    eng.wait_ge(S("shift_done"), 8)
                    eng.dma_start(A["o_state"][l], state_out).then_inc(S("state_outs"), 16)
                    eng.wait_ge(S("phase_ended"), 3)
                    for j in range(2):
                        ld(Cs[:, j].rearrange("p b c -> p (b c)"), "C0", 2 * l + j, "ml_state_in")
                    eng.wait_ge(S("m_out"), 1)
                    eng.dma_start(A["o_m"][l], seg12[0:4, 2, :]).then_inc(S("ml_outs"), 16)
                    eng.wait_ge(S("ml_final"), 1)
                    eng.dma_start(A["o_Cp"][l], Cp).then_inc(S("ml_outs"), 16)
                    eng.dma_start(A["o_Cs"][l], Cs.rearrange("p j b c -> p (j b c)")).then_inc(S("ml_outs"), 16)
                    eng.wait_ge(S("phase_ended"), 6)
                    ld(rw_w[:, 0, :], "lora", 2 * l, "rw_w_in")
                    ld(rw_w[:, 1, :], "lora", 2 * l + 1, "rw_w_in")
                    ld(S0s.rearrange("p j b c -> p (j b c)"), "S0", l, "rw_state_in")
                    eng.wait_ge(S("rw_final"), 1)
                    eng.dma_start(A["o_Sp"][l], S0).then_inc(S("rw_outs"), 16)
                    eng.dma_start(A["o_Ss"][l], S0s.rearrange("p j b c -> p (j b c)")).then_inc(S("rw_outs"), 16)
                    clear("half")
                    ld(cw1.rearrange("p a b -> p (a b)"), "cw1", 2 * l, "cw1_in")
                    ld(cw2.rearrange("p a b -> p (a b)"), "cw2", l, "cw2_in")
                    pages = 40
                    for b in range(NB):
                        for c in range(PAGES):
                            k = b * PAGES + c
                            pg = eng.value_load(page_buf[0:1, k:k + 1], min_val=0, max_val=pages - 1)
                            eng.dma_start(ckb[:, b, :, P * c:P * c + P],
                                          A["pages_k"][l * pages + pg][:, 0:2, :]).then_inc(S(f"pages_{b}"), 16)
                    eng.wait_ge(S("rope_out"), 6)
                    eng.dma_start(A["o_kv"][l], cols[:, CCK:CCK + 4, :]).then_inc(S("kv_outs"), 16)
                    eng.dma_start(A["o_wkv"][l], cols[:, CWK:CWK + 2, :]).then_inc(S("kv_outs"), 16)
                    eng.wait_ge(S("cmp_hid"), 2)
                    ld(cw1.rearrange("p a b -> p (a b)"), "cw1", 2 * l + 1, "cw1_in")
                    eng.wait_ge(S("phase_ended"), 9)
                    for q in range(2):
                        if q:
                            eng.wait_ge(S("sa_unit"), 2)
                        for b in range(4):
                            for c in range(PAGES):
                                k = (4 * q + b) * PAGES + c
                                pg = eng.value_load(page_buf[0:1, k:k + 1], min_val=0, max_val=pages - 1)
                                eng.dma_start(skq[:, b, P * c:P * c + P],
                                              A["pages_k"][l * pages + pg][:, 2, :]).then_inc(S(f"qpages_{b}"), 16)
                                eng.dma_start(svq[:, b, c, :],
                                              A["pages_v"][l * pages + pg]).then_inc(S(f"qpages_{b}"), 16)
                            eng.dma_start(wkq[:, b, :], A["win_k"][l * NB + 4 * q + b]).then_inc(S("qwin"), 16)
                            eng.dma_start(wvq[:, b, :, :],
                                          A["win_v"][l * NB + 4 * q + b].rearrange("(c p) d -> p c d", p=P)).then_inc(S("qwin"), 16)
                    eng.wait_ge(S("phase_ended"), 15)
                    wo_sp(l)
                    eng.wait_ge(S("state_outs"), 16)
                    eng.wait_ge(S("phase_ended"), 21)
                    with eng.Fori(0, experts(l)) as e:
                        ex_sp(e + 2 * l)
                        clear("expert")
                    clear("layer")
                eng.wait_ge(S("g_fin_done"), KD)
                eng.dma_start(A["o_y"], xn).then_inc(S("g_y"), 16)
                eng.wait_ge(S("g_y"), 16)
                eng.wait_ge(S("g_win"), 16 * DEPTH * NB)

            return len(sems)


ML_W, RW0, NS0 = 1032, 1032, 2056


def in_columns():
    r = lambda a, n: list(range(a, a + n))
    out = r(0, 1024)
    out += r(RW0, 256) + r(RW0 + 256, 64) + r(RW0 + 832, 64) + r(RW0 + 320, 256) + r(RW0 + 576, 256) + r(RW0 + 896, 128)
    for i in range(4):
        out += r(NS0 + 64 * i, 64) + r(NS0 + 64 * (4 + i), 64)
    out += r(NS0 + 512, 768)
    gate = [-1] * P
    gate[0:4], gate[32:36], gate[64:88] = r(1024, 4), r(1028, 4), r(NS0 + 1280, 24)
    return out + gate


def rw_columns():
    r = lambda a, n: list(range(a, a + n))
    return r(0, 256) + r(256, 64) + r(832, 64) + r(320, 256) + r(576, 256) + r(896, 128)


def pack(inp):
    n = {k: np.asarray(v) for k, v in inp.items()}
    f = np.float32
    o = {}
    at, w = table_layout()
    t = np.zeros((P, w), f)
    for k, a in tables().items():
        c, r, m = at[k]
        t[0:r, c:c + m] = a
    o["tab"] = t
    x = np.concatenate([n["x_prompt"].reshape(SEQ, D), n["x_sample"].reshape(NS_TOK, D)], 0)

    def chans(a):
        return np.moveaxis(a.reshape(a.shape[:-1] + (-1, P)), -1, -2)

    o["x"] = x.T.reshape(KD, P, T).transpose(1, 0, 2)
    cols = np.array(in_columns())
    w_in = np.where(cols >= 0, n["w_in"][:, :, np.maximum(cols, 0)], f(0))
    o["w_in"] = w_in.reshape(DEPTH, KD, P, NCH, P).transpose(0, 3, 2, 1, 4).reshape(DEPTH * NCH, P, KD, P)
    mix = list(range(512))
    for i in range(4):
        mix += list(range(512 + 64 * i, 576 + 64 * i)) + list(range(512 + 64 * (4 + i), 576 + 64 * (4 + i)))
    o["w_out"] = n["w_out"][:, mix].reshape(DEPTH, KD, P, KD, P).transpose(0, 3, 2, 1, 4).reshape(DEPTH * KD, P, KD, P)
    E1 = FC * P

    def up(dense, moe):
        d = dense[0].reshape(D, 2, E1).transpose(1, 0, 2)
        a = np.concatenate([d, moe[0]], 0)
        return a.reshape(10, KD, P, FC, P).transpose(0, 3, 2, 1, 4)

    o["w13"] = np.stack([up(n["ffn_w1"], n["moe_w1"]), up(n["ffn_w3"], n["moe_w3"])], 3).reshape(10 * FC, P, 2, KD, P)
    w2 = np.concatenate([n["ffn_w2"][0].reshape(2, E1, D), n["moe_w2"][0]], 0)
    o["w2"] = w2.reshape(10, FC, P, KD, P).transpose(0, 3, 2, 1, 4).reshape(10 * KD, P, FC, P)
    o["router"] = n["moe_router"][0].reshape(KD, P, 8).transpose(1, 0, 2)
    o["nfin"] = chans(n["norm_final_w"])
    v = np.zeros((DEPTH, P, NV), f)

    def put(name, a):
        v[:, :, VEC[name]:VEC[name] + a.shape[-1]] = a

    rwc = rw_columns()
    put("nmix", chans(n["norm_mix_w"]))
    put("nffn", chans(n["norm_ffn_w"]))
    put("convw", chans(n["ml_conv_w"]).transpose(0, 2, 1, 3).reshape(DEPTH, P, 16))
    put("convb", chans(n["ml_conv_b"]))
    put("mu", chans(n["rw_mu"][:, rwc]))
    for name, key in (("w0", "rw_w0"), ("a0", "rw_a0"), ("kk", "rw_k_k"), ("ka", "rw_k_a"), ("lnw", "rw_ln_w"),
                      ("lnb", "rw_ln_b"), ("mlw", "ml_norm_w")):
        put(name, chans(n[key]))
    put("rk", chans(n["rw_r_k"].reshape(DEPTH, 256)))
    v[:, 0:4, VEC["gb"]] = n["ml_b_i"]
    v[:, 32:36, VEC["gb"]] = n["ml_b_f"]
    v[1, :, VEC["flag"]] = 1.0
    pos = n["nsa_cmp_pos"].transpose(0, 3, 1, 2).reshape(DEPTH, HD, 64)
    put("cpos", np.concatenate([pos, pos], 1))
    o["vec"] = v
    conv = n["state_mlstm_conv"].transpose(0, 3, 1, 2).reshape(DEPTH, 4, P, NB * 3).transpose(0, 2, 1, 3)
    shift = n["state_rwkv_shift"][:, :, rwc].transpose(0, 2, 1).reshape(DEPTH, 8, P, NB).transpose(0, 2, 1, 3)
    o["state"] = np.concatenate([conv.reshape(DEPTH, P, -1), shift.reshape(DEPTH, P, -1)], 2)
    o["m0"] = n["state_mlstm_m"].transpose(0, 2, 1)
    C = np.zeros((DEPTH, 2, P, NB, 130), f)
    S_ = np.zeros((DEPTH, P, 2, NB, P), f)
    for h in range(4):
        j, q = h // 2, h % 2
        C[:, j, 64 * q:64 * q + 64, :, 65 * q:65 * q + 64] = n["state_mlstm_C"][:, :, h].transpose(0, 3, 1, 2)
        C[:, j, 64 * q:64 * q + 64, :, 65 * q + 64] = n["state_mlstm_n"][:, :, h].transpose(0, 2, 1)
        S_[:, 64 * q:64 * q + 64, j, :, 64 * q:64 * q + 64] = n["state_rwkv_S"][:, :, h].transpose(0, 3, 1, 2)
    o["C0"] = C.reshape(DEPTH * 2, P, NB * 130)
    o["S0"] = S_.reshape(DEPTH, P, 2 * NB * P)
    lora = np.zeros((DEPTH, 2, P, 256), f)
    lora[:, 0, 0:64], lora[:, 0, 64:128], lora[:, 1] = n["rw_w2"], n["rw_a2"], n["rw_g2"]
    o["lora"] = lora.reshape(DEPTH * 2, P, 256)
    cw1 = n["nsa_cmp_w1"].reshape(DEPTH, 2, CLEN, HD, P).transpose(0, 1, 3, 2, 4)
    o["cw1"] = np.concatenate([cw1, cw1], 2).reshape(DEPTH * 2, P, CLEN * P)
    o["cw2"] = n["nsa_cmp_w2"].transpose(0, 2, 1, 3).reshape(DEPTH, P, P)
    kv = n["cache_nsa_kv"].reshape(DEPTH * 40, P, 4, P)
    o["pages_k"] = kv[:, :, 0:3].transpose(0, 3, 2, 1)
    o["pages_v"] = kv[:, :, 3]
    win = n["cache_win_kv"].reshape(DEPTH, NB, PAST, 2, P)
    o["win"] = win.reshape(DEPTH, NB, PAST, 256)
    o["win_k"] = win[:, :, :, 0].transpose(0, 1, 3, 2).reshape(DEPTH * NB, P, PAST)
    o["win_v"] = win[:, :, :, 1].reshape(DEPTH * NB, PAST, P)
    o["pages"] = n["page_table"].reshape(1, NB * PAGES).astype(np.int32)
    return {k: np.ascontiguousarray(a) for k, a in o.items()}


OUTS = {
    "o_y": (P, KD, T), "o_kv": (DEPTH, P, 4, T), "o_wkv": (DEPTH, P, 2, T), "o_win": (DEPTH, NB, PAST, 256),
    "o_state": (DEPTH, P, OUT_W), "o_m": (DEPTH, 4, 12), "o_Cp": (DEPTH, P, 260), "o_Cs": (DEPTH, P, 2 * NB * 130),
    "o_Sp": (DEPTH, P, 256), "o_Ss": (DEPTH, P, 2 * NB * P),
}


def unpack(r):
    y = r["o_y"].transpose(2, 1, 0).reshape(T, D)
    out = [y[None, 0:SEQ], y[SEQ:].reshape(NB, TS, D)]
    kv = r["o_kv"].transpose(0, 3, 2, 1)
    out += [kv[:, None, 0:SEQ].reshape(DEPTH, 1, SEQ, 4, 2, HD), kv[:, SEQ:].reshape(DEPTH, NB, TS, 4, 2, HD)]
    wkv = r["o_wkv"].transpose(0, 3, 2, 1)
    win = r["o_win"].copy()
    win[:, :, PAST - TS:] = wkv[:, SEQ:].reshape(DEPTH, NB, TS, 256)
    out += [wkv[:, None, 0:SEQ].reshape(DEPTH, 1, SEQ, 2, 2, HD), win.reshape(DEPTH, NB, PAST, 2, 2, HD)]
    Cp = r["o_Cp"].reshape(DEPTH, P, 2, 1, 130)
    Cs = r["o_Cs"].reshape(DEPTH, P, 2, NB, 130)
    Sp = r["o_Sp"].reshape(DEPTH, P, 2, 1, P)
    Ss = r["o_Ss"].reshape(DEPTH, P, 2, NB, P)

    def by_head(a, w, n):
        return np.stack([a[:, 64 * (h % 2):64 * (h % 2) + 64, h // 2, :, w * (h % 2):w * (h % 2) + n] for h in range(4)], 1)

    for a in (Cp, Cs):
        c = by_head(a, 65, 65)
        out.append(c[..., 0:64].transpose(0, 3, 1, 4, 2))
    for a in (Cp, Cs):
        out.append(by_head(a, 65, 65)[..., 64].transpose(0, 3, 1, 2))
    m = r["o_m"]
    out += [m[:, :, 3][:, None], m[:, :, 4:12].transpose(0, 2, 1)]
    st = r["o_state"]

    def conv(a, nb):
        return a.reshape(DEPTH, P, 4, nb, 3).transpose(0, 3, 4, 2, 1).reshape(DEPTH, nb, 3, 512)

    out += [conv(st[:, :, OUT_CP:OUT_CS], 1), conv(st[:, :, OUT_CS:OUT_SP], NB)]
    for a in (Sp, Ss):
        out.append(by_head(a, 64, 64).transpose(0, 3, 1, 4, 2))
    back = np.argsort(np.array(rw_columns()))

    def shift(a, nb):
        return a.reshape(DEPTH, P, 8, nb).transpose(0, 3, 2, 1).reshape(DEPTH, nb, D)[:, :, back]

    out += [shift(st[:, :, OUT_SP:OUT_SS], 1), shift(st[:, :, OUT_SS:], NB)]
    return tuple(np.ascontiguousarray(a) for a in out)


def kernel(**inputs):
    import concourse.bacc as _bacc
    from concourse.bass_utils import run_bass_kernel_spmd as _run

    nc = _bacc.Bacc("TRN2", target_bir_lowering=False, num_devices=1, dynamic_dma_scratch_size=2048)
    arrays = pack(inputs)
    A = {}
    for name, a in arrays.items():
        A[name] = nc.dram_tensor("d_" + name, a.shape, mybir.dt.from_np(a.dtype), kind="ExternalInput").ap()
    for name, shape in OUTS.items():
        A[name] = nc.dram_tensor("d_" + name, shape, F32, kind="ExternalOutput").ap()
    build(nc, A)
    r = _run(nc, [{"d_" + k: a for k, a in arrays.items()}], core_ids=[0]).results[0]
    return unpack({k: np.asarray(r["d_" + k]) for k in OUTS})
```

```python
from contextlib import ExitStack

import numpy as np
import concourse.bass as bass
from concourse import mybir

F32 = mybir.dt.float32
F32R = mybir.dt.float32r
I32 = mybir.dt.int32
ALU = mybir.AluOpType
ACT = mybir.ActivationFunctionType
AX = mybir.AxisListType

P = 128
D = 1024
KD = D // P
SEQ = 512
NB = 8
TS = 8
NS_TOK = NB * TS
T = SEQ + NS_TOK
HALF = T // 2
PT = SEQ // P
TILES = [(i * P, P) for i in range(PT)] + [(SEQ, NS_TOK)]
DEPTH = 2
PAST = 512
PAGES = PAST // P
HD = 64
CMP = 31
STRIDE = 16
CLEN = 32
NBLK = 9
FC = 11
NEG = -1e30
SCALE = HD ** -0.5

CQ, CK, CV, CO = 0, 2, 4, 6
CR, CWA, CRK, CRV, CG = 8, 10, 11, 13, 15
CNQ, CCK, CCV, CSK, CSV, CWK, CWV, CGATE = 16, 20, 21, 22, 23, 24, 25, 26
NCH = 27

_v = {}
_n = 0
for _name, _w in (("nmix", 8), ("nffn", 8), ("convw", 16), ("convb", 4), ("mu", 8), ("w0", 2), ("a0", 2),
                  ("kk", 2), ("ka", 2), ("rk", 2), ("lnw", 2), ("lnb", 2), ("mlw", 2), ("gb", 1), ("flag", 1),
                  ("cpos", 64)):
    _v[_name] = _n
    _n += _w
NV = _n
VEC = dict(_v)


def tables():
    c = {}
    i = np.arange(P)
    c["ident"] = np.eye(P)
    c["ones"] = np.ones((P, P))
    c["onesbd"] = (i[:, None] // HD == i[None, :] // HD) * 1.0
    rot = np.zeros((P, P))
    for o in (0, HD):
        for d in range(HD // 2):
            rot[o + d + HD // 2, o + d] = -1.0
            rot[o + d, o + d + HD // 2] = 1.0
    c["rot"] = rot
    pos = np.concatenate([np.arange(SEQ), np.tile(PAST + np.arange(TS), NB)]).astype(np.float32)
    half = HD // 2
    inv = (np.float32(10000.0) ** (-np.arange(half, dtype=np.float32) / np.float32(half))).astype(np.float32)
    ang = (pos[None, :] * inv[:, None]).astype(np.float32)
    c["cos"] = np.tile(np.cos(ang), (4, 1))
    c["sin"] = np.tile(np.sin(ang), (4, 1))
    up = i[:, None] <= i[None, :]
    seg = i[:, None] // TS == i[None, :] // TS
    c["tri"] = np.where(i[None, :] <= i[:, None], 0.0, NEG)
    c["mlp"] = np.where(up, 0.0, NEG)
    c["mls"] = np.where(up & seg, 0.0, NEG)
    st = i[:, None] < i[None, :]
    c["rwp"] = np.concatenate([st, up], 1) * 1.0
    c["rws"] = np.concatenate([(st & seg)[:, :64], (up & seg)[:, :64]], 1) * 1.0
    lev = []
    for k in range(7):
        b = 1 << k
        lev.append((i[:, None] // (2 * b) == i[None, :] // (2 * b)) & (i[:, None] // b % 2 == 0)
                   & (i[None, :] // b % 2 == 1))
    c["lev"] = np.concatenate(lev, 1) * 1.0
    c["bd"] = np.tile(c["onesbd"], (1, 2))
    b65 = np.repeat(np.arange(2), 65)
    c["bd65"] = np.tile((i[:, None] // HD == b65[None, :]) * 1.0, (1, 2))
    t64 = np.arange(64)
    c["segbt"] = np.tile((np.arange(NB)[:, None] == t64[None, :] // TS).reshape(1, -1), (P, 1)) * 1.0
    c["segsb"] = (i[:, None] // TS == np.arange(NB)[None, :]) * 1.0
    cm = (np.arange(CMP) * STRIDE + CLEN - 1)[None, None, :] <= (np.arange(PT)[None, :, None] * P + i[:, None, None])
    c["cm1"] = cm.reshape(P, -1) * 1.0
    c["cma"] = np.where(cm, 0.0, NEG).reshape(P, -1)
    r = i
    rb, rt = r // 32, r % TS
    col = np.arange(64)
    new = [((col[None, :] // TS == rb[:, None] + 4 * q) & (col[None, :] % TS <= rt[:, None])) for q in range(2)]
    c["newm"] = np.where(np.concatenate(new, 1), 0.0, NEG)
    c["winm"] = np.where(np.arange(8)[None, :] > rt[:, None], 0.0, NEG)
    c["same"] = ((rb[:, None] == rb[None, :]) & (rt[:, None] == rt[None, :])) * 1.0
    cs, ss = np.arange(CMP) * STRIDE, np.arange(NBLK) * HD
    ov = np.clip(np.minimum(cs[:, None] + CLEN, ss[None, :] + HD) - np.maximum(cs[:, None], ss[None, :]), 0, None)
    c["ov"] = ov / CLEN
    c["rowi"] = np.tile((np.arange(4)[None, :, None] == (r // TS % 4)[:, None, None]) * np.ones((1, 1, 3)), (1, 2, 1)).reshape(P, 24)
    c["rank"] = np.tile(np.arange(1, 10)[None, :], (P, 1))
    c["rrank"] = np.tile(np.arange(8, 0, -1)[None, :], (P, 5))
    for j in range(2):
        s = np.zeros((4, P))
        s[2 * j, :HD] = 1.0
        s[2 * j + 1, HD:] = 1.0
        c[f"pair{j}"] = s
    tt = np.arange(T)
    first = (tt % P == 0) | ((tt >= SEQ) & (tt % TS == 0))
    c["reset"] = np.tile(np.where(first, 0.0, 1.0)[None, :], (P, 1))
    c["kill"] = np.tile(np.where((tt >= SEQ) & (tt % TS == 0), NEG, 0.0)[None, :], (4, 1))
    return {k: np.asarray(v, np.float32) for k, v in c.items()}


def table_layout():
    at, col = {}, 0
    for k, v in tables().items():
        at[k] = (col, v.shape[0], v.shape[1])
        col += v.shape[1]
    return at, col


TAB, TAB_W = table_layout()

ST_CONV, ST_SHIFT, ST_W = 0, 4 * NB * 3, 4 * NB * 3 + 8 * NB
OUT_CP, OUT_CS, OUT_SP, OUT_SS = 0, 12, 12 + 96, 12 + 96 + 8
OUT_W = OUT_SS + 64


class Chain:

    def __init__(self, eng, sem):
        self.eng, self.sem, self.n = eng, sem, 0

    def __call__(self, ins, *signals):
        self.n += 1
        ins.then_inc(self.sem, 1)
        self.eng.wait_ge(self.sem, self.n)
        for s in signals:
            self.eng.sem_inc(s, 1)


class Space:

    def __init__(self, buf, start, end):
        self.buf, self.at, self.end = buf, start, end

    def take(self, *dims):
        n = int(np.prod(dims))
        assert self.at + n <= self.end, (self.at, n, self.end)
        v = self.buf[:, self.at:self.at + n]
        self.at += n
        if len(dims) == 2:
            v = v.rearrange("p (a b) -> p a b", b=dims[1])
        elif len(dims) == 3:
            v = v.rearrange("p (a b c) -> p a b c", b=dims[1], c=dims[2])
        elif len(dims) == 4:
            v = v.rearrange("p (a b c d) -> p a b c d", b=dims[1], c=dims[2], d=dims[3])
        return v


def build(nc, A):
    with ExitStack() as ctx:
        sems = {}

        FIRST = ("mix_norm", "proj_", "w_in_", "conv_", "shift_", "f_", "exp_args", "m_rows", "rows_", "m_out", "ml_",
                 "rw_", "hn_")
        SECOND = ("cmp_", "rope_", "at_", "sa_", "cw", "pages_", "qpages_", "qwin", "wo_", "w_out_", "ffn_norm", "rt_")
        shared, used = [], {True: 0, False: 0}

        def S(name):
            if name not in sems:
                part = name.startswith(FIRST)
                if part or name.startswith(SECOND):
                    if used[part] == len(shared):
                        shared.append(ctx.enter_context(nc.semaphore(f"part_{len(shared)}")))
                    sems[name] = shared[used[part]]
                    used[part] += 1
                else:
                    sems[name] = ctx.enter_context(nc.semaphore(name))
            return sems[name]

        def sb(name, cols):
            return ctx.enter_context(nc.sbuf_tensor(name, [P, cols], F32))

        ARENA = 21000
        place, at_ = {}, 2560 // 4
        for name, n_ in (("tab", TAB_W), ("x", KD * T), ("n", KD * T), ("cols", NCH * T), ("small", 1400),
                         ("h", 5 * 2 * 256), ("arena", ARENA), ("page", NB * PAGES)):
            place[name] = at_
            at_ += -(-n_ // 8) * 8

        def put_at(name, n_, at, dt=F32, rows=P):
            return nc.alloc_sbuf_tensor_at(name, [rows, n_], dt, offset=4 * at)

        tab = put_at("tab", TAB_W, place["tab"])
        x_buf = put_at("x_buf", KD * T, place["x"])
        n_buf = put_at("n_buf", KD * T, place["n"])
        cols_buf = put_at("cols_buf", NCH * T, place["cols"])
        small = put_at("small", 1400, place["small"])
        h_buf = put_at("h_buf", 5 * 2 * 256, place["h"])
        arena = put_at("arena", ARENA, place["arena"])
        page_buf = put_at("page_buf", NB * PAGES, place["page"], I32, 1)
        UNIT = FC * P
        XL_AT = ARENA - KD * T
        xh_buf = put_at("xh_buf", KD * T, place["n"], F32R)
        xl_buf = put_at("xl_buf", KD * T, place["arena"] + XL_AT, F32R)
        whl_buf = put_at("whl_buf", 6 * UNIT, place["arena"] + 3 * UNIT, F32R)
        hh_buf = put_at("hh_buf", FC * T, place["cols"], F32R)
        hl_buf = put_at("hl_buf", FC * T, place["cols"] + FC * T, F32R)
        split_buf = put_at("split_buf", 2 * T, place["h"], F32R)
        ps_buf = ctx.enter_context(nc.psum_tensor("ps_buf", [P, 8, 512], F32))

        def tb(name, rows=None, lo=0):
            c, r, w = TAB[name]
            return tab[lo:(rows or r), c:c + w]

        ident = tb("ident")
        x = x_buf[:, :].rearrange("p (k t) -> p k t", t=T)
        hmix = n_buf[:, :].rearrange("p (k t) -> p k t", t=T)
        XH = xh_buf[:, :].rearrange("p (k t) -> p k t", t=T)
        XL = xl_buf[:, :].rearrange("p (k t) -> p k t", t=T)
        HH = hh_buf[:, :].rearrange("p (k t) -> p k t", t=T)
        HL = hl_buf[:, :].rearrange("p (k t) -> p k t", t=T)
        cols = cols_buf[:, :].rearrange("p (k t) -> p k t", t=T)
        HB = h_buf[:, :].rearrange("p (m i c) -> p m i c", m=2, i=5)
        sm = Space(small, 0, 1400)
        vec = sm.take(NV)
        state_in = sm.take(ST_W)
        state_out = sm.take(OUT_W)
        m0_in = sm.take(NB)
        nfin = sm.take(8)
        n64 = sm.take(40)
        n64b = sm.take(40)
        decb = sm.take(2, 12)
        posb = sm.take(4)
        omka = sm.take(2)
        router = sm.take(8, 8)
        prod = sm.take(2, 12)
        midp = sm.take(2, 4)
        gates = sm.take(5, 24)
        sgate = sm.take(2, 2, 3)
        stat = sm.take(4, 4)
        impz = sm.take(9)
        imps = sm.take(9)
        kbias = sm.take(8)
        iw = sm.take(8)
        sg24 = sm.take(24)
        ups = sm.take(2, 4)

        def V(name, k=0, lo=0, hi=P):
            c = VEC[name] + k
            return vec[lo:hi, c:c + 1]

        def bank(i, n=512, rows=P):
            return ps_buf[0:rows, i, 0:n]

        sync = nc.sync

        hsp = Space(h_buf, 0, 2560)
        rstd = hsp.take(T)
        ntmp = hsp.take(3, T)
        squares = cols_buf[:, 0:KD * T].rearrange("p (k t) -> p k t", t=T)
        split_v = split_buf[:, :].rearrange("p (k t) -> p k t", t=T)
        sp1 = Space(arena, 3 * UNIT + 2 * 2 * KD * P, XL_AT)
        qkpad = sp1.take(4, 3 + SEQ + NB * 11)
        rwpad = sp1.take(8, 1 + SEQ + NB * 9)

        def pad_p(pad, c, h, j, n=SEQ):
            return pad[:, c, j:j + n]

        def pad_s(pad, c, h, j, n=TS):
            return pad[:, c, h + SEQ:].rearrange("p (b t) -> p b t", t=h + TS)[:, :, j:j + n]

        sp2 = Space(arena, 0, ARENA)
        R = sp2.take(12, T)
        G = sp2.take(T)
        GT = sp2.take(5, P)
        qs = sp2.take(2, T)
        qmask = sp2.take(NB, NS_TOK)
        v1 = sp2.take(5, 260)
        wk = sp2.take(5, 256)
        DT = sp2.take(512)
        STb = sp2.take(512)
        Cp = sp2.take(260)
        Cs = sp2.take(2, NB, 130)
        vm = sp2.take(NB, 130)
        seg12 = sp2.take(4, 12)
        den = sp2.take(8)

        sp3 = Space(arena, 0, ARENA)
        rw_w = sp3.take(2, 256)
        ra = sp3.take(2, T)
        rg = sp3.take(2, T)
        rcum = sp3.take(2, T)
        rcumx = sp3.take(2, T)
        rkk = sp3.take(2, T)
        rk2 = sp3.take(2, T)
        KR = sp3.take(2, 2 * T)
        nbt = sp3.take(2, T)
        kht = sp3.take(2, T)
        e3 = sp3.take(2, T)
        tk_flat = sp3.take(5 * 3 * 256)
        TK = tk_flat.rearrange("p (i c) -> p i c", i=5)
        XU = sp3.take(2, 256)
        S0 = sp3.take(256)
        mid = sp3.take(2, 4)
        M1 = cols_buf[:, 0:1024].rearrange("p (h c) -> p h c", h=4)
        M2 = cols_buf[:, 1024:2048].rearrange("p (h c) -> p h c", h=4)
        Dm = cols_buf[:, 2048:2560]
        Dt = cols_buf[:, 2560:3072]
        S0s = sp3.take(2, NB, P)
        Nb = sp3.take(512)
        Yb = sp3.take(512)
        kmask = cols_buf[:, 2048:2560].rearrange("p (b t) -> p b t", b=NB)
        rmask = Nb.rearrange("p (b t) -> p b t", b=NB)
        umask = cols_buf[:, 0:1024].rearrange("p (b c) -> p b c", b=NB)
        vmask = cols_buf[:, 1024:2048].rearrange("p (b c) -> p b c", b=NB)
        hsq = tk_flat[:, 0:2560].rearrange("p (g d) -> p g d", d=HD)

        def kr(j, i, which, n, lo=0, hi=P):
            o = 2 * TILES[i][0] + which * n
            return KR[lo:hi, j, o:o + n]

        sp4 = Space(arena, 0, ARENA)
        ckb = sp4.take(9, 2, 512)
        cw1 = sp4.take(CLEN, P)
        hid = sp4.take(4, 9 * CMP)
        ckT = sp4.take(9 * CMP)
        cvt = sp4.take(9, 2, HD)
        cw2 = sp4.take(2, HD)
        qrs = sp4.take(2, NB * 32)
        svt = sp4.take(5, P)
        wvt = sp4.take(5, P)
        rtmp = sp4.take(T)
        osamp = sp4.take(2, P)
        sp5 = Space(arena, 0, 9 * 1024 + 4096)
        skq = sp5.take(4, 512)
        wkq = sp5.take(4, 512)
        svq = sp5.take(4, PAGES, P)
        wvq = sp5.take(4, 4, P)
        Sb = sp5.take(2, T)
        PTb = sp5.take(2, 5, P)
        oacc = sp5.take(4, 4, P)
        qrot = Space(cols_buf, 0, 4 * T).take(4, T)
        sp6 = Space(arena, 9 * UNIT, XL_AT)
        sg = sp6.take(2, T)
        combE = sp6.take(T)
        cTe = sp6.take(T)
        cT = sp6.take(T)
        lg = sp6.take(5, 8)
        lw = sp6.take(8, 40)
        htmp = Space(cols_buf, 2 * FC * T, NCH * T).take(2, T)

        def raw(slot, nk):
            return arena[:, slot * UNIT:slot * UNIT + nk * P]

        def part(slot, which, nk, size=UNIT):
            a = (2 * slot + which) * size
            return whl_buf[:, a:a + nk * P]

        def split_hi(a, slot, rslot, nk, size, *sig):
            a(nc.scalar.copy(part(slot, 0, nk, size), raw(rslot, nk)), *sig)

        def split_lo(g, slot, rslot, nk, size, *sig):
            g(nc.gpsimd.tensor_tensor(part(slot, 1, nk, size), raw(rslot, nk), part(slot, 0, nk, size).bitcast(F32),
                                      ALU.subtract), *sig)

        def two(b, rows=P):
            return ps_buf[0:rows, b:b + 2, 0:HALF]

        def halves(v):
            return v.rearrange("p (a t) -> p a t", a=2)

        def wide(b, w, m, start=True, stop=True, rows=P):
            for a_ in range(2):
                last = nc.tensor.matmul(ps_buf[0:rows, b + a_, 0:HALF], w, m[:, a_ * HALF:(a_ + 1) * HALF],
                                        start=start, stop=stop)
            return last

        def unit_products(slot, nk, size, xh, xl, b, before=None):
            wh = part(slot, 0, nk, size).rearrange("p (k c) -> p k c", c=P)
            wl = part(slot, 1, nk, size).rearrange("p (k c) -> p k c", c=P)
            for k in range(nk):
                if before:
                    before(k)
                for n_, (w, m) in enumerate(((wh, xh), (wh, xl), (wl, xh))):
                    f_, l_ = k == 0 and n_ == 0, k == nk - 1 and n_ == 2
                    last = wide(b, w[:, k, :], m[:, k, :], f_, l_)
            return last

        meets = {"pe": 0, "act": 0, "dve": 0}

        def meet(eng, who):
            eng.drain().then_inc(S("phase_ended"), 1)
            meets[who] += 1
            eng.wait_ge(S("phase_ended"), 3 * meets[who])

        def norm_act(a, tag, rs, final=False):
            ac = nc.scalar
            for k in range(KD):
                a(ac.activation(squares[:, k, :], x[:, k, :], ACT.Square), S(tag + "_squares"))
            ac.wait_ge(S(tag + "_mean"), 1)
            a(ac.activation(rs, rs, ACT.Sqrt), S(tag + "_root"))
            if not final:
                for k in range(KD):
                    ac.wait_ge(S(tag + "_scaled"), k + 1)
                    a(ac.copy(XH[:, k, :], ntmp[:, k % 3, :]), S(tag + "_hi"))

        def norm_pe(tag):
            for k in range(KD):
                nc.tensor.wait_ge(S(tag + "_squares"), k + 1)
                last = wide(0, tb("ones"), squares[:, k, :], k == 0, k == KD - 1)
            last.then_inc(S(tag + "_sum"), 1)

        def norm_dve(v, tag, rs, w, final=False):
            ve = nc.vector
            ve.wait_ge(S(tag + "_sum"), 1)
            v(ve.tensor_scalar(halves(rs), two(0), 1.0 / D, 1e-6, ALU.mult, ALU.add), S(tag + "_mean"))
            ve.wait_ge(S(tag + "_root"), 1)
            v(ve.reciprocal(rs, rs))
            for k in range(KD + 1):
                if k < KD:
                    dst = hmix[:, k, :] if final else ntmp[:, k % 3, :]
                    v(ve.scalar_tensor_tensor(dst, x[:, k, :], w(k), rs, ALU.mult, ALU.mult),
                      S(tag + ("_done" if final else "_scaled")))
                if k and not final:
                    ve.wait_ge(S(tag + "_hi"), k)
                    v(ve.tensor_tensor(XL[:, k - 1, :], ntmp[:, (k - 1) % 3, :], XH[:, k - 1, :].bitcast(F32), ALU.subtract),
                      S(tag + "_done"))

        def proj_sp(l):
            for c in range(NCH):
                if c >= 3:
                    sync.wait_ge(S("proj_split"), c - 2)
                sync.dma_start(raw(c % 3, KD), A["w_in"][l * NCH + c].rearrange("p k c -> p (k c)"))\
                    .then_inc(S(f"w_in_{c % 3}"), 16)

        def proj_hi(a, c):
            nc.scalar.wait_ge(S(f"w_in_{c % 3}"), 16 * (c // 3 + 1))
            if c >= 2:
                nc.scalar.wait_ge(S("proj_done"), c - 1)
            split_hi(a, c % 2, c % 3, KD, KD * P, S("proj_hi"))

        def proj_pool(g):
            for c in range(NCH):
                nc.gpsimd.wait_ge(S("proj_hi"), c + 1)
                split_lo(g, c % 2, c % 3, KD, KD * P, S("proj_split"))

        def proj_pe():
            for c in range(NCH):
                nc.tensor.wait_ge(S("proj_split"), c + 1)
                if c >= 3:
                    nc.tensor.wait_ge(S("proj_out"), c - 2)
                b = 2 + 2 * (c % 3)
                unit_products(c % 2, KD, KD * P, XH, XL, b,
                              (lambda k: nc.tensor.wait_ge(S("mix_norm_done"), k + 1)) if c == 0 else None)\
                    .then_inc(S("proj_done"), 1)

        def proj_act(a):
            for c in range(2):
                proj_hi(a, c)
            for c in range(NCH):
                nc.scalar.wait_ge(S("proj_done"), c + 1)
                if c + 2 < NCH:
                    proj_hi(a, c + 2)
                b = 2 + 2 * (c % 3)
                rest = SEQ - HALF
                s64 = ps_buf[:, b + 1, rest:HALF].rearrange("p (b t) -> p b t", t=TS)
                if c < 4 or 8 <= c < 16:
                    pad, k, h = (qkpad, c, 3) if c < 4 else (rwpad, c - 8, 1)
                    a(nc.scalar.copy(pad[:, k, h:h + HALF], bank(b, HALF)))
                    a(nc.scalar.copy(pad[:, k, h + HALF:h + SEQ], bank(b + 1, rest)))
                    a(nc.scalar.copy(pad_s(pad, k, h, h), s64), S("proj_out"))
                elif c == CGATE:
                    a(nc.scalar.activation(halves(cols[:, c, :]), two(b), ACT.Identity, bias=V("gb")), S("proj_out"))
                else:
                    a(nc.scalar.copy(halves(cols[:, c, :]), two(b)), S("proj_out"))
            nc.scalar.wait_ge(S("conv_done"), 4)
            for c in range(4):
                a(nc.scalar.activation(cols[:, c, :], cols[:, c, :], ACT.Silu))
                if c >= 2:
                    a(nc.scalar.mul(cols[:, c, :], cols[:, c, :], SCALE))

        def proj_dve(v):
            ve = nc.vector
            v(ve.memset(qkpad[:, :, 0:3], 0.0))
            v(ve.memset(rwpad[:, :, 0:1], 0.0))
            for c in range(4):
                v(ve.tensor_copy(pad_s(qkpad, c, 3, 0, 3),
                                 state_in[:, ST_CONV + 24 * c:ST_CONV + 24 * c + 24].rearrange("p (b j) -> p b j", j=3)))
            for c in range(8):
                v(ve.tensor_copy(pad_s(rwpad, c, 1, 0, 1),
                                 state_in[:, ST_SHIFT + 8 * c:ST_SHIFT + 8 * c + 8].rearrange("p (b j) -> p b j", j=1)))

            def both(c):
                yield cols[:, c, 0:SEQ], pad_p
                yield cols[:, c, SEQ:T].rearrange("p (b t) -> p b t", t=TS), pad_s

            for c in range(4):
                ve.wait_ge(S("proj_out"), c + 1)
                for y, pad in both(c):
                    n = SEQ if pad is pad_p else TS
                    v(ve.tensor_scalar(y, pad(qkpad, c, 3, 0, n), V("convw", c), V("convb", c), ALU.mult, ALU.add))
                    for j in range(1, 4):
                        v(ve.scalar_tensor_tensor(y, pad(qkpad, c, 3, j, n), V("convw", 4 * j + c), y, ALU.mult, ALU.add))
                v(ve.tensor_copy(state_out[:, OUT_CP + 3 * c:OUT_CP + 3 * c + 3], qkpad[:, c, SEQ:SEQ + 3]))
                v(ve.tensor_copy(state_out[:, OUT_CS + 24 * c:OUT_CS + 24 * c + 24].rearrange("p (b j) -> p b j", j=3),
                                 pad_s(qkpad, c, 3, TS, 3)), S("conv_done"))
            for c in range(8):
                ve.wait_ge(S("proj_out"), 8 + c + 1)
                for y, pad in both(8 + c):
                    n = SEQ if pad is pad_p else TS
                    now = pad(rwpad, c, 1, 1, n)
                    v(ve.tensor_tensor(y, pad(rwpad, c, 1, 0, n), now, ALU.subtract))
                    v(ve.scalar_tensor_tensor(y, y, V("mu", c), now, ALU.mult, ALU.add))
                v(ve.tensor_copy(state_out[:, OUT_SP + c:OUT_SP + c + 1], rwpad[:, c, SEQ:SEQ + 1]))
                v(ve.tensor_copy(state_out[:, OUT_SS + 8 * c:OUT_SS + 8 * c + 8].rearrange("p (b j) -> p b j", j=1),
                                 pad_s(rwpad, c, 1, TS, 1)), S("shift_done"))

        def onehot(h, n):
            return ident[0:4, h:h + 1].to_broadcast([4, n])

        def pairsel(j):
            return tb(f"pair{j}")

        RF, RL, RB, RM, RP, RU, RI, RD1, RD0, RT = range(10)

        def rows_dve(v):
            ve = nc.vector

            def r(k, a=0, b=T, s=1):
                return R[0:4, k, a:b:s] if s > 1 else R[0:4, k, a:b]

            def seg(k):
                return R[0:4, k, SEQ:T].rearrange("p (b t) -> p b t", t=TS)

            def til(k, a=0, b=SEQ):
                return R[0:4, k, a:b].rearrange("p (c t) -> p c t", t=P)

            ig = cols[0:4, CGATE, :]
            v(ve.memset(G, 0.0))
            v(ve.memset(seg12, 0.0), S("rows_start"))
            v(ve.tensor_copy(r(RF), cols[32:36, CGATE, :]))
            v(ve.scalar_tensor_tensor(r(RT), r(RF), -1.0, r(RF), ALU.mult, ALU.max), S("f_abs"))
            ve.wait_ge(S("f_exp"), 1)
            v(ve.tensor_scalar(r(RL), r(RL), 1.0, None, ALU.add), S("f_one"))
            ve.wait_ge(S("f_ln"), 1)
            v(ve.scalar_tensor_tensor(r(RL), r(RF), 0.0, r(RL), ALU.min, ALU.subtract))
            v(ve.tensor_tensor_scan(r(RB), tb("reset", 4), r(RL), 0.0, ALU.mult, ALU.add))
            v(ve.tensor_copy(r(RD1), ig))
            v(ve.tensor_tensor(seg12[0:4, 3, 0:8], R[0:4, RL, SEQ:T:TS], m0_in[0:4, :], ALU.add))
            v(ve.tensor_tensor(R[0:4, RD1, SEQ:T:TS], R[0:4, RD1, SEQ:T:TS], seg12[0:4, 3, 0:8], ALU.max))
            v(ve.tensor_tensor(r(RD0), r(RL), tb("kill", 4), ALU.add))
            v(ve.tensor_tensor_scan(r(RM), r(RD0), r(RD1), 0.0, ALU.add, ALU.max), S("m_rows"))
            v(ve.memset(r(RP, 0, P), 0.0))
            v(ve.tensor_copy(til(RP, P, SEQ), R[0:4, RM, P - 1:SEQ - P:P].unsqueeze(2).to_broadcast([4, PT - 1, P])))
            v(ve.tensor_copy(seg(RP), m0_in[0:4, :].unsqueeze(2).to_broadcast([4, NB, TS])))
            v(ve.tensor_tensor(r(RU), r(RB), r(RM), ALU.subtract))
            v(ve.tensor_tensor(r(RI), r(RU), r(RP), ALU.add))
            v(ve.tensor_tensor(G[0:4, :], ig, r(RB), ALU.subtract))
            v(ve.tensor_copy(seg12[0:4, 0, 0:4], R[0:4, RU, P - 1:SEQ:P]))
            v(ve.tensor_copy(seg12[0:4, 0, 4:12], R[0:4, RU, SEQ + TS - 1:T:TS]))
            v(ve.tensor_tensor(seg12[0:4, 1, 0:4], seg12[0:4, 0, 0:4], R[0:4, RP, 0:SEQ:P], ALU.add))
            v(ve.tensor_tensor(seg12[0:4, 1, 4:12], seg12[0:4, 0, 4:12], m0_in[0:4, :], ALU.add))
            v(ve.tensor_tensor(til(RT), G[0:4, 0:SEQ].rearrange("p (c t) -> p c t", t=P),
                               seg12[0:4, 0, 0:4].unsqueeze(2).to_broadcast([4, 4, P]), ALU.add))
            v(ve.tensor_tensor(seg(RT), G[0:4, SEQ:T].rearrange("p (b t) -> p b t", t=TS),
                               seg12[0:4, 0, 4:12].unsqueeze(2).to_broadcast([4, NB, TS]), ALU.add), S("exp_args"))
            v(ve.tensor_copy(seg12[0:4, 2, 0:4], R[0:4, RM, P - 1:SEQ:P]))
            v(ve.tensor_copy(seg12[0:4, 2, 4:12], R[0:4, RM, SEQ + TS - 1:T:TS]), S("m_out"))

        def rows_act(a):
            ac = nc.scalar
            ac.wait_ge(S("rows_start"), 1)
            a(ac.activation(G[96:120, :], cols[64:88, CGATE, :], ACT.Sigmoid))
            ac.wait_ge(S("f_abs"), 1)
            a(ac.activation(R[0:4, RL, :], R[0:4, RT, :], ACT.Exp, scale=-1.0), S("f_exp"))
            ac.wait_ge(S("f_one"), 1)
            a(ac.activation(R[0:4, RL, :], R[0:4, RL, :], ACT.Ln), S("f_ln"))
            ac.wait_ge(S("exp_args"), 1)
            a(ac.activation(G[64:68, :], R[0:4, RM, :], ACT.Exp, scale=-1.0))
            a(ac.activation(R[0:4, RI, :], R[0:4, RI, :], ACT.Exp))
            a(ac.activation(seg12[0:4, 1, :], seg12[0:4, 1, :], ACT.Exp))
            a(ac.activation(G[32:36, :], R[0:4, RT, :], ACT.Exp), S("rows_done"))

        def ml_pe():
            pe = nc.tensor
            pe.wait_ge(S("rows_done"), 1)
            for i, (t0, n) in enumerate(TILES):
                last = pe.transpose(ps_buf[0:n, i // 4, (i % 4) * P:(i % 4) * P + P], G[:, t0:t0 + n], ident)
            last.then_inc(S("ml_cols"), 1)
            for j in range(2):
                wide(2 + 2 * j, pairsel(j), R[0:4, RI, :])
                last = pe.matmul(ps_buf[:, 6, 12 * j:12 * j + 12], pairsel(j), seg12[0:4, 1, :], start=True, stop=True)
            last.then_inc(S("ml_spread"), 1)
            for i, (t0, n) in enumerate(TILES):
                pe.wait_ge(S("ml_spread_out") if i == 0 else S("ml_kv_out"), 1 if i == 0 else i)
                for c in range(4):
                    last = pe.transpose(ps_buf[0:n, 7, c * P:c * P + P], cols[:, CK + c, t0:t0 + n], ident)
                last.then_inc(S("ml_kv"), 1)
            for i, (t0, n) in enumerate(TILES):
                mask = tb("mlp" if n == P else "mls", n)[:, 0:n]
                if i == 0:
                    pe.wait_ge(S("ml_kv_out"), 5)
                for h in range(4):
                    o = ps_buf[0:n, 0, h * n:h * n + n]
                    pe.matmul(o, onehot(h, n), R[0:4, RU, t0:t0 + n], start=True, stop=False)
                    last = pe.matmul(o, ident[0:n, 0:n], mask, start=False, stop=True)
                last.then_inc(S("ml_logd"), 1)
                for h in range(4):
                    j, f = h // 2, h % 2
                    last = pe.matmul(ps_buf[0:n, 1 + f, j * n:j * n + n], cols[64 * f:64 * f + 64, CK + j, t0:t0 + n],
                                     cols[64 * f:64 * f + 64, CQ + j, t0:t0 + n], start=True, stop=True)
                last.then_inc(S("ml_kq"), 1)
                if i == 4:
                    pe.wait_ge(S("ml_state_in"), 32)
                else:
                    pe.wait_ge(S("ml_state"), i + 1)
                for j in range(2):
                    o = ps_buf[0:n, 3, j * 130:j * 130 + 130]
                    if i < 4:
                        pe.matmul(o, qs[:, j, t0:t0 + n], Cp[:, j * 130:j * 130 + 130], start=True, stop=False)
                    else:
                        pe.wait_ge(S("ml_qmask"), j + 1)
                        for b in range(NB):
                            last = pe.matmul(o, qmask[:, b, :], Cs[:, j, b, :], start=b == 0, stop=False)
                        last.then_inc(S("ml_qmask_used"), 1)
                    if j == 0:
                        pe.wait_ge(S("ml_S"), i + 1)
                    for f in range(2):
                        last = pe.matmul(ps_buf[0:n, 3, j * 130 + 65 * f:j * 130 + 65 * f + 65],
                                         STb[0:n, (2 * f + j) * n:(2 * f + j) * n + n],
                                         v1[0:n, i, (2 * j + f) * 65:(2 * j + f) * 65 + 65], start=False, stop=f == 1)
                last.then_inc(S("ml_num"), 1)
                if i < 4:
                    for j in range(2):
                        last = pe.matmul(ps_buf[:, 4, j * 130:j * 130 + 130], wk[:, i, 128 * j:128 * j + 128],
                                         v1[:, i, 130 * j:130 * j + 130], start=True, stop=True)
                    last.then_inc(S("ml_add"), 1)
                else:
                    for j in range(2):
                        pe.wait_ge(S("ml_vm"), j + 1)
                        for g in range(3):
                            nb = min(3, NB - 3 * g)
                            last = pe.matmul(ps_buf[:, 4 + g, 0:nb * 130], wk[0:64, 4, 128 * j:128 * j + 128],
                                             vm[0:64, 3 * g:3 * g + nb, :], start=True, stop=True)
                        last.then_inc(S("ml_add"), 1)
                if i < 4:
                    pe.wait_ge(S("ml_h"), i + 1)

        def ml_act(a):
            ac = nc.scalar
            for i, (t0, n) in enumerate(TILES):
                ac.wait_ge(S("ml_logd"), i + 1)
                ac.wait_ge(S("ml_kv_out"), 5)
                for h in range(4):
                    idx = (h % 2) * 2 + h // 2
                    a(ac.activation(DT[0:n, idx * n:idx * n + n], ps_buf[0:n, 0, h * n:h * n + n], ACT.Exp,
                                    bias=GT[0:n, i, h:h + 1]))
                ac.sem_inc(S("ml_D"), 1)
                if i < 4:
                    ac.wait_ge(S("ml_h"), i + 1)

        def ml_dve(v):
            ve = nc.vector
            v(ve.memset(Cp, 0.0))
            v(ve.memset(v1, 1.0))
            v(ve.memset(h_buf[:, :], 0.0), S("ml_state"))
            ve.wait_ge(S("ml_cols"), 1)
            v(ve.tensor_copy(GT[:, 0:4, :], bank(0).rearrange("p (i c) -> p i c", c=P)))
            v(ve.tensor_copy(GT[0:64, 4, :], ps_buf[0:64, 1, 0:P]))
            v(ve.tensor_copy(gates[:, 0:4, :], GT[:, 0:4, 96:120]))
            ve.wait_ge(S("ml_spread"), 1)
            for j in range(2):
                v(ve.tensor_tensor(halves(qs[:, j, :]), halves(cols[:, CQ + j, :]), two(2 + 2 * j), ALU.mult))
            v(ve.tensor_copy(decb, ps_buf[:, 6, 0:24].rearrange("p (j c) -> p j c", j=2)), S("ml_spread_out"))
            for i, (t0, n) in enumerate(TILES):
                ve.wait_ge(S("ml_kv"), i + 1)
                v(ve.tensor_tensor(wk[0:n, i, :].rearrange("p (h d) -> p h d", h=4),
                                   ps_buf[0:n, 7, 0:256].rearrange("p (h d) -> p h d", h=4),
                                   GT[0:n, i, 32:36].unsqueeze(2).to_broadcast([n, 4, HD]), ALU.mult))
                v(ve.tensor_copy(v1[0:n, i, :].rearrange("p (h d) -> p h d", h=4)[:, :, 0:HD],
                                 ps_buf[0:n, 7, 256:512].rearrange("p (h d) -> p h d", h=4)), S("ml_kv_out"))
            for i, (t0, n) in enumerate(TILES):
                if i == 4:
                    v(ve.tensor_tensor(qmask, qs[:, 0, SEQ:T].unsqueeze(1).to_broadcast([P, NB, NS_TOK]),
                                       tb("segbt").rearrange("p (b t) -> p b t", b=NB), ALU.mult), S("ml_qmask"))
                ve.wait_ge(S("ml_kq"), i + 1)
                ve.wait_ge(S("ml_D"), i + 1)
                for f in range(2):
                    v(ve.tensor_tensor(STb[0:n, 2 * f * n:2 * f * n + 2 * n], ps_buf[0:n, 1 + f, 0:2 * n],
                                       DT[0:n, 2 * f * n:2 * f * n + 2 * n], ALU.mult), *([S("ml_S")] if f else []))
                if i == 4:
                    ve.wait_ge(S("ml_qmask_used"), 1)
                    v(ve.tensor_tensor(qmask, qs[:, 1, SEQ:T].unsqueeze(1).to_broadcast([P, NB, NS_TOK]),
                                       tb("segbt").rearrange("p (b t) -> p b t", b=NB), ALU.mult), S("ml_qmask"))
                ve.wait_ge(S("ml_num"), i + 1)
                num = ps_buf[0:n, 3, 0:260].rearrange("p (h d) -> p h d", h=4)
                v(ve.tensor_copy(den[0:n, 4:8], num[:, :, HD]))
                v(ve.scalar_tensor_tensor(den[0:n, 0:4], den[0:n, 4:8], -1.0, den[0:n, 4:8], ALU.mult, ALU.max))
                v(ve.tensor_tensor(den[0:n, 0:4], den[0:n, 0:4], GT[0:n, i, 64:68], ALU.max))
                v(ve.reciprocal(den[0:n, 4:8], den[0:n, 0:4]))
                v(ve.tensor_tensor(HB[0:n, 0, i, :].rearrange("p (h d) -> p h d", h=4), num[:, :, 0:HD],
                                   den[0:n, 4:8].unsqueeze(2).to_broadcast([n, 4, HD]), ALU.mult))
                if i < 4:
                    ve.wait_ge(S("ml_add"), i + 1)
                    for j in range(2):
                        c = Cp[:, 130 * j:130 * j + 130]
                        v(ve.scalar_tensor_tensor(c, c, decb[:, j, i:i + 1], ps_buf[:, 4, 130 * j:130 * j + 130],
                                                  ALU.mult, ALU.add))
                    v(ve.tensor_tensor(Cp, Cp, tb("bd65"), ALU.mult), S("ml_state"), S("ml_h"))
                else:
                    for j in range(2):
                        v(ve.tensor_tensor(vm[0:64], v1[0:64, 4, 130 * j:130 * j + 130].unsqueeze(1).to_broadcast([64, NB, 130]),
                                           tb("segsb", 64).unsqueeze(2).to_broadcast([64, NB, 130]), ALU.mult), S("ml_vm"))
                        ve.wait_ge(S("ml_add"), 5 + j)
                        v(ve.tensor_tensor(Cs[:, j], Cs[:, j], decb[:, j, 4:12].unsqueeze(2).to_broadcast([P, NB, 130]), ALU.mult))
                        for g in range(3):
                            nb = min(3, NB - 3 * g)
                            v(ve.tensor_tensor(Cs[:, j, 3 * g:3 * g + nb, :], Cs[:, j, 3 * g:3 * g + nb, :],
                                               ps_buf[:, 4 + g, 0:nb * 130].rearrange("p (b c) -> p b c", b=nb), ALU.add))
                    ve.sem_inc(S("ml_final"), 1)

        def rwprep_pe():
            pe = nc.tensor
            pe.wait_ge(S("rw_w_in"), 32)
            pe.wait_ge(S("rw_lora_in"), 1)
            for j in range(2):
                last = wide(2 * j, rw_w[0:64, 0, P * j:P * j + P], cols[0:64, CWA, :])
            last.then_inc(S("rw_w_pre"), 1)
            for j in range(2):
                last = wide(4 + 2 * j, rw_w[64:128, 0, P * j:P * j + P], cols[64:128, CWA, :])
            last.then_inc(S("rw_a_pre"), 1)
            pe.wait_ge(S("rw_decay"), 1)
            for j in range(2):
                last = wide(2 * j, rw_w[:, 1, P * j:P * j + P], cols[:, CG, :])
            last.then_inc(S("rw_g"), 1)
            pe.wait_ge(S("rw_a"), 1)
            pe.wait_ge(S("rw_kk_sq"), 1)
            for j in range(2):
                last = wide(4 + 2 * j, tb("onesbd"), e3[:, j, :])
            last.then_inc(S("rw_kk_sum"), 1)
            pe.wait_ge(S("rw_rk"), 1)
            for j in range(2):
                last = wide(2 * j, tb("onesbd"), Yb2[:, j, :])
            last.then_inc(S("rw_rk_sum"), 1)
            pe.wait_ge(S("rw_ready"), 1)
            for i, (t0, n) in enumerate(TILES):
                if i:
                    pe.wait_ge(S("rw_rows_out"), i)
                for j in range(2):
                    pe.transpose(ps_buf[0:n, 6, P * j:P * j + P], nbt[:, j, t0:t0 + n], ident)
                    pe.transpose(ps_buf[0:n, 6, 256 + P * j:256 + P * j + P], kht[:, j, t0:t0 + n], ident)
                    last = pe.transpose(ps_buf[0:n, 7, P * j:P * j + P], cols[:, CRV + j, t0:t0 + n], ident)
                last.then_inc(S("rw_rows"), 1)

        def rwprep_act(a):
            ac = nc.scalar
            a(ac.activation(cols[0:64, CWA, :], cols[0:64, CWA, :], ACT.Tanh), S("rw_lora_in"))
            a(ac.activation(cols[:, CG, :], cols[:, CG, :], ACT.Sigmoid))
            ac.wait_ge(S("rw_w_pre"), 1)
            for j in range(2):
                a(ac.activation(halves(rcumx[:, j, :]), two(2 * j), ACT.Sigmoid, bias=V("w0", j)),
                  *([S("rw_decay")] if j else []))
            ac.wait_ge(S("rw_a_pre"), 1)
            for j in range(2):
                a(ac.activation(halves(ra[:, j, :]), two(4 + 2 * j), ACT.Sigmoid, bias=V("a0", j)),
                  *([S("rw_a")] if j else []))
            ac.wait_ge(S("rw_g"), 1)
            for j in range(2):
                a(ac.copy(halves(rg[:, j, :]), two(2 * j)))
            ac.sem_inc(S("rw_g_out"), 1)
            for c in range(2):
                a(ac.activation(cols[:, CO + c, :], cols[:, CO + c, :], ACT.Sigmoid))
            ac.wait_ge(S("rw_kk_sum"), 1)
            for j in range(2):
                a(ac.activation(halves(e3[:, j, :]), two(4 + 2 * j), ACT.Sqrt))
            ac.sem_inc(S("rw_kk_len"), 1)
            ac.wait_ge(S("rw_cum"), 1)
            a(ac.activation(midp, mid, ACT.Exp))
            a(ac.activation(rcumx, rcumx, ACT.Exp), S("rw_e1"))
            a(ac.activation(e3, rcum, ACT.Exp, scale=-1.0), S("rw_e3"))
            a(ac.activation(rcum, rcum, ACT.Exp), S("rw_e2"))

        Yb2 = rkk

        def rwprep_dve(v):
            ve = nc.vector
            for j in range(2):
                v(ve.tensor_scalar(rkk[:, j, :], cols[:, CRK + j, :], V("kk", j), None, ALU.mult))
                v(ve.tensor_tensor(e3[:, j, :], rkk[:, j, :], rkk[:, j, :], ALU.mult), *([S("rw_kk_sq")] if j else []))
            v(ve.tensor_scalar(omka, vec[:, VEC["ka"]:VEC["ka"] + 2], -1.0, 1.0, ALU.mult, ALU.add))
            ve.wait_ge(S("rw_a"), 1)
            for j in range(2):
                v(ve.tensor_scalar(rk2[:, j, :], ra[:, j, :], V("ka", j), omka[:, j:j + 1], ALU.mult, ALU.add))
                v(ve.tensor_tensor(rk2[:, j, :], rk2[:, j, :], cols[:, CRK + j, :], ALU.mult))
            ve.wait_ge(S("rw_kk_len"), 1)
            v(ve.tensor_scalar(e3, e3, 1e-12, None, ALU.max))
            v(ve.reciprocal(e3, e3))
            v(ve.tensor_tensor(nbt, rkk, e3, ALU.mult))
            for j in range(2):
                v(ve.scalar_tensor_tensor(Yb2[:, j, :], cols[:, CR + j, :], V("rk", j), rk2[:, j, :], ALU.mult, ALU.mult))
            v(ve.tensor_scalar(kht, rcumx, -float(np.exp(-0.5)), None, ALU.mult))
            ve.wait_ge(S("rw_g_out"), 1)
            ve.sem_inc(S("rw_rk"), 1)
            for j in range(2):
                v(ve.tensor_tensor_scan(rcum[:, j, :], tb("reset"), kht[:, j, :], 0.0, ALU.mult, ALU.add))
            v(ve.tensor_tensor(rcumx, rcum, kht, ALU.subtract))
            for j in range(2):
                v(ve.tensor_copy(mid[:, j, :], rcum[:, j, P // 2 - 1:SEQ:P]))
            for buf in (rcum, rcumx):
                for j in range(2):
                    w = buf[:, j, 0:SEQ].rearrange("p (c t) -> p c t", t=P)
                    v(ve.tensor_tensor(w, w, mid[:, j, :].unsqueeze(2).to_broadcast([P, PT, P]), ALU.subtract))
            ve.sem_inc(S("rw_cum"), 1)
            ve.wait_ge(S("rw_rk_sum"), 1)
            ve.wait_ge(S("rw_e3"), 1)

            def krv(j, which):
                yield KR[:, j, 0:2 * SEQ].rearrange("p (i w t) -> p i w t", w=2, t=P)[:, :, which, :], 0, SEQ
                yield KR[:, j, 2 * SEQ + which * 64:2 * SEQ + which * 64 + 64].rearrange("p (i t) -> p i t", i=1), SEQ, T

            for j in range(2):
                for dst, a0, b0 in krv(j, 0):
                    n = min(P, b0 - a0)
                    v(ve.tensor_tensor(dst, nbt[:, j, a0:b0].rearrange("p (i t) -> p i t", t=n),
                                       rcumx[:, j, a0:b0].rearrange("p (i t) -> p i t", t=n), ALU.mult))
                v(ve.tensor_tensor(halves(rcumx[:, j, :]), halves(cols[:, CRV + j, :]), two(2 * j), ALU.mult))
            v(ve.scalar_tensor_tensor(nbt, nbt, -1.0, ra, ALU.mult, ALU.mult))
            v(ve.tensor_tensor(nbt, nbt, e3, ALU.mult))
            v(ve.tensor_tensor(kht, rk2, e3, ALU.mult))
            ve.wait_ge(S("rw_e2"), 1)
            for j in range(2):
                for dst, a0, b0 in krv(j, 1):
                    n = min(P, b0 - a0)
                    v(ve.tensor_tensor(dst, cols[:, CR + j, a0:b0].rearrange("p (i t) -> p i t", t=n),
                                       rcum[:, j, a0:b0].rearrange("p (i t) -> p i t", t=n), ALU.mult))
                v(ve.tensor_copy(prod[:, j, 0:4], rcum[:, j, P - 1:SEQ:P]))
                v(ve.tensor_copy(prod[:, j, 4:12], rcum[:, j, SEQ + TS - 1:T:TS]))
            v(ve.tensor_copy(ups, prod[:, :, 0:4]))
            v(ve.tensor_tensor(ups[:, :, 0:3], ups[:, :, 0:3], midp[:, :, 1:4], ALU.mult), S("rw_ready"))
            for i, (t0, n) in enumerate(TILES):
                ve.wait_ge(S("rw_rows"), i + 1)
                v(ve.tensor_copy(TK[0:n, i, 0:512], ps_buf[0:n, 6, 0:512]))
                v(ve.tensor_copy(TK[0:n, i, 512:768], ps_buf[0:n, 7, 0:256]), S("rw_rows_out"))

        def levels(i):
            return 7 if i < 4 else 3

        def rw_pe():
            pe = nc.tensor
            lv, rounds = 0, 0
            for i, (t0, n) in enumerate(TILES):
                if i:
                    pe.wait_ge(S("rw_tile"), i)
                for h in range(4):
                    j, f = h // 2, h % 2
                    lo, hi = 64 * f, 64 * f + 64
                    both = KR[lo:hi, j, 2 * t0:2 * t0 + 2 * n]
                    pe.matmul(ps_buf[0:n, f, j * 2 * n:(j + 1) * 2 * n], nbt[lo:hi, j, t0:t0 + n], both, start=True, stop=True)
                    last = pe.matmul(ps_buf[0:n, 2 + f, j * 2 * n:(j + 1) * 2 * n], kht[lo:hi, j, t0:t0 + n], both,
                                     start=True, stop=True)
                last.then_inc(S("rw_prods"), 1)
                pe.wait_ge(S("rw_D1"), i + 1)
                for q in range(4):
                    last = pe.transpose(ps_buf[0:n, 4, q * n:q * n + n], Dt[0:n, q * n:q * n + n], ident[0:n, 0:n])
                last.then_inc(S("rw_D1T"), 1)
                for k in range(1, levels(i)):
                    lv += 1
                    pe.wait_ge(S("rw_N"), lv)
                    for q in range(4):
                        last = pe.matmul(ps_buf[0:n, 5, q * n:q * n + n], Nb[0:n, q * n:q * n + n], Dm[0:n, q * n:q * n + n],
                                         start=True, stop=True)
                    last.then_inc(S("rw_Y"), 1)
                    pe.wait_ge(S("rw_Y_out"), lv)
                    for q in range(4):
                        s_ = slice(q * n, q * n + n)
                        if k < levels(i) - 1:
                            pe.matmul(ps_buf[0:n, 6, s_], Dt[0:n, s_], Yb[0:n, s_], start=True, stop=True)
                        last = pe.matmul(ps_buf[0:n, 7, s_], Yb[0:n, s_], Dt[0:n, s_], start=True, stop=True)
                    last.then_inc(S("rw_DD"), 1)
                pe.wait_ge(S("rw_inv"), i + 1)
                if i < 4:
                    pe.wait_ge(S("rw_state"), i + 1)
                else:
                    pe.wait_ge(S("rw_state_in"), 16)
                for j in range(2):
                    o = ps_buf[0:n, 4, P * j:P * j + P]
                    if i < 4:
                        pe.matmul(o, kr(j, i, 0, n), S0[:, P * j:P * j + P], start=True, stop=False)
                    else:
                        pe.wait_ge(S("rw_kmask"), j + 1)
                        for b in range(NB):
                            last = pe.matmul(o, kmask[:, b, :], S0s[:, j, b, :], start=b == 0, stop=False)
                        last.then_inc(S("rw_kmask_used"), 1)
                    for f in range(2):
                        c = P * j + 64 * f
                        last = pe.matmul(ps_buf[0:n, 4, c:c + 64], M2[0:n, 2 * f + j, 0:n], TK[0:n, i, 512 + c:512 + c + 64],
                                         start=False, stop=f == 1)
                last.then_inc(S("rw_X"), 1)
                pe.wait_ge(S("rw_X_out"), i + 1)
                for h in range(4):
                    q = (h % 2) * 2 + h // 2
                    last = pe.matmul(ps_buf[0:n, 5, 64 * h:64 * h + 64], Dt[0:n, q * n:q * n + n],
                                     XU[0:n, 0, 64 * h:64 * h + 64], start=True, stop=True)
                last.then_inc(S("rw_U"), 1)
                pe.wait_ge(S("rw_U_out"), i + 1)
                for j in range(2):
                    o = ps_buf[0:n, 6, P * j:P * j + P]
                    if i < 4:
                        pe.matmul(o, kr(j, i, 1, n), S0[:, P * j:P * j + P], start=True, stop=False)
                    else:
                        pe.wait_ge(S("rw_rmask"), j + 1)
                        for b in range(NB):
                            last = pe.matmul(o, rmask[:, b, :], S0s[:, j, b, :], start=b == 0, stop=False)
                        last.then_inc(S("rw_rmask_used"), 1)
                    for f in range(2):
                        c = P * j + 64 * f
                        pe.matmul(ps_buf[0:n, 6, c:c + 64], M1[0:n, 2 * f + j, n:2 * n], XU[0:n, 1, c:c + 64],
                                  start=False, stop=False)
                        last = pe.matmul(ps_buf[0:n, 6, c:c + 64], M2[0:n, 2 * f + j, n:2 * n],
                                         TK[0:n, i, 512 + c:512 + c + 64], start=False, stop=f == 1)
                last.then_inc(S("rw_y"), 1)
                if i < 4:
                    for j in range(2):
                        o = ps_buf[:, 7, P * j:P * j + P]
                        pe.matmul(o, TK[0:n, i, P * j:P * j + P], XU[0:n, 1, P * j:P * j + P], start=True, stop=False)
                        last = pe.matmul(o, TK[0:n, i, 256 + P * j:256 + P * j + P], TK[0:n, i, 512 + P * j:512 + P * j + P],
                                         start=False, stop=True)
                    last.then_inc(S("rw_add"), 1)
                else:
                    for j in range(2):
                        pe.wait_ge(S("rw_umask"), j + 1)
                        for g in range(2):
                            o = ps_buf[:, 2 * j + g, 0:512]
                            pe.matmul(o, TK[0:n, i, P * j:P * j + P], umask[0:n, 4 * g:4 * g + 4, :], start=True, stop=False)
                            last = pe.matmul(o, TK[0:n, i, 256 + P * j:256 + P * j + P], vmask[0:n, 4 * g:4 * g + 4, :],
                                             start=False, stop=True)
                        last.then_inc(S("rw_add"), 1)

        def rw_dve(v):
            ve = nc.vector
            v(ve.memset(S0, 0.0), S("rw_state"))
            done = 0
            for i, (t0, n) in enumerate(TILES):
                mask = tb("rwp" if n == P else "rws", n)[:, 0:2 * n].unsqueeze(1).to_broadcast([n, 2, 2 * n])
                ve.wait_ge(S("rw_prods"), i + 1)
                for f in range(2):
                    for M, b in ((M1, f), (M2, 2 + f)):
                        v(ve.tensor_tensor(M[0:n, 2 * f:2 * f + 2, 0:2 * n],
                                           ps_buf[0:n, b, 0:4 * n].rearrange("p (j c) -> p j c", j=2), mask, ALU.mult))

                def lev(k):
                    return tb("lev", n)[:, P * k:P * k + n].unsqueeze(1).to_broadcast([n, 4, n])

                def q4(b):
                    return b[0:n, 0:4 * n].rearrange("p (q c) -> p q c", q=4)

                v(ve.tensor_tensor(q4(Dt), M1[0:n, :, 0:n], lev(0), ALU.mult))
                v(ve.tensor_tensor(q4(Dt), q4(Dt), ident[0:n, 0:n].unsqueeze(1).to_broadcast([n, 4, n]), ALU.add), S("rw_D1"))
                ve.wait_ge(S("rw_D1T"), i + 1)
                v(ve.tensor_copy(Dm[0:n, 0:4 * n], ps_buf[0:n, 4, 0:4 * n]))
                for k in range(1, levels(i)):
                    done += 1
                    v(ve.tensor_tensor(q4(Nb), M1[0:n, :, 0:n], lev(k), ALU.mult), S("rw_N"))
                    ve.wait_ge(S("rw_Y"), done)
                    v(ve.tensor_copy(Yb[0:n, 0:4 * n], ps_buf[0:n, 5, 0:4 * n]), S("rw_Y_out"))
                    ve.wait_ge(S("rw_DD"), done)
                    v(ve.tensor_tensor(Dt[0:n, 0:4 * n], Dt[0:n, 0:4 * n], ps_buf[0:n, 7, 0:4 * n], ALU.add))
                    if k < levels(i) - 1:
                        v(ve.tensor_tensor(Dm[0:n, 0:4 * n], Dm[0:n, 0:4 * n], ps_buf[0:n, 6, 0:4 * n], ALU.add))
                ve.sem_inc(S("rw_inv"), 1)

                def spread(dst, j, which, sig):
                    v(ve.tensor_tensor(dst, kr(j, 4, which, 64).unsqueeze(1).to_broadcast([P, NB, 64]),
                                       tb("segbt").rearrange("p (b t) -> p b t", b=NB), ALU.mult), S(sig))

                if i == 4:
                    spread(kmask, 0, 0, "rw_kmask")
                    spread(rmask, 0, 1, "rw_rmask")
                    ve.wait_ge(S("rw_kmask_used"), 1)
                    spread(kmask, 1, 0, "rw_kmask")
                ve.wait_ge(S("rw_X"), i + 1)
                v(ve.tensor_copy(XU[0:n, 0, :], ps_buf[0:n, 4, 0:256]), S("rw_X_out"))
                ve.wait_ge(S("rw_U"), i + 1)
                v(ve.tensor_copy(XU[0:n, 1, :], ps_buf[0:n, 5, 0:256]), S("rw_U_out"))
                if i == 4:
                    ve.wait_ge(S("rw_rmask_used"), 1)
                    spread(rmask, 1, 1, "rw_rmask")
                ve.wait_ge(S("rw_y"), i + 1)
                v(ve.tensor_copy(HB[0:n, 1, i, :], ps_buf[0:n, 6, 0:256]))
                if i < 4:
                    ve.wait_ge(S("rw_add"), i + 1)
                    v(ve.tensor_tensor(S0, S0, ps_buf[:, 7, 0:256], ALU.add))
                    for j in range(2):
                        w = S0[:, P * j:P * j + P]
                        v(ve.scalar_tensor_tensor(w, w, ups[:, j, i:i + 1], tb("onesbd"), ALU.mult, ALU.mult),
                          *([S("rw_state"), S("rw_tile")] if j else []))
                else:
                    for j in range(2):
                        if j:
                            ve.wait_ge(S("rw_add"), 5)
                        for m, src in ((umask, XU[0:64, 1, P * j:P * j + P]), (vmask, TK[0:64, 4, 512 + P * j:512 + P * j + P])):
                            v(ve.tensor_tensor(m[0:64], src.unsqueeze(1).to_broadcast([64, NB, P]),
                                               tb("segsb", 64).unsqueeze(2).to_broadcast([64, NB, P]), ALU.mult))
                        ve.sem_inc(S("rw_umask"), 1)
                    ve.wait_ge(S("rw_add"), 6)
                    for j in range(2):
                        for g in range(2):
                            w = S0s[:, j, 4 * g:4 * g + 4, :]
                            v(ve.tensor_tensor(w, w, ps_buf[:, 2 * j + g, 0:512].rearrange("p (b c) -> p b c", b=4), ALU.add))
                        v(ve.tensor_tensor(S0s[:, j], S0s[:, j], prod[:, j, 4:12].unsqueeze(2).to_broadcast([P, NB, P]), ALU.mult))
                    ve.sem_inc(S("rw_final"), 1)

        def hn_dve(v):
            ve = nc.vector
            hb = h_buf[:, :].rearrange("p (g d) -> p g d", d=HD)
            v(ve.tensor_reduce(n64, hb, AX.X, ALU.add))
            v(ve.tensor_scalar(n64, n64, 1.0 / HD, None, ALU.mult))
            v(ve.tensor_tensor(hb, hb, n64.unsqueeze(2).to_broadcast([P, 40, HD]), ALU.subtract))
            v(ve.tensor_tensor(hsq, hb, hb, ALU.mult))
            v(ve.tensor_reduce(n64b, hsq, AX.X, ALU.add))
            v(ve.tensor_scalar(n64b[:, 0:20], n64b[:, 0:20], 1.0 / HD, 1e-6, ALU.mult, ALU.add))
            v(ve.tensor_scalar(n64b[:, 20:40], n64b[:, 20:40], 1.0 / HD, 64e-5, ALU.mult, ALU.add), S("hn_var"))
            ve.wait_ge(S("hn_root"), 1)
            v(ve.reciprocal(n64b, n64b))
            v(ve.tensor_tensor(hb, hb, n64b.unsqueeze(2).to_broadcast([P, 40, HD]), ALU.mult), S("hn_done"))
            for m in range(2):
                for j in range(2):
                    ve.wait_ge(S("hn_T"), 2 * m + j + 1)
                    for a0, b0 in ((0, SEQ), (SEQ, T)):
                        b = bank(2 * (2 * m + j) + (a0 > 0), b0 - a0)
                        o = hmix[:, 2 * m + j, a0:b0]
                        if m == 0:
                            v(ve.scalar_tensor_tensor(o, b, V("mlw", j), cols[:, CO + j, a0:b0], ALU.mult, ALU.mult))
                        else:
                            v(ve.tensor_scalar(o, b, V("lnw", j), V("lnb", j), ALU.mult, ALU.add))
                            v(ve.tensor_tensor(o, o, rcumx[:, j, a0:b0], ALU.add))
                            v(ve.tensor_tensor(o, o, rg[:, j, a0:b0], ALU.mult))

        def hn_act(a):
            nc.scalar.wait_ge(S("hn_var"), 1)
            a(nc.scalar.activation(n64b, n64b, ACT.Sqrt), S("hn_root"))

        def hn_pe():
            pe = nc.tensor
            pe.wait_ge(S("hn_done"), 1)
            for m in range(2):
                for j in range(2):
                    for i, (t0, n) in enumerate(TILES):
                        b = 2 * (2 * m + j)
                        o = ps_buf[:, b, t0:t0 + n] if i < 4 else ps_buf[:, b + 1, 0:n]
                        last = pe.transpose(o, HB[0:n, m, i, P * j:P * j + P], ident[0:n, 0:n])
                    last.then_inc(S("hn_T"), 1)

        ROPED = [(CNQ, 0), (CNQ + 1, 1), (CNQ + 2, 2), (CNQ + 3, 3), (CSK, None), (CWK, None)]

        def cmp_pe():
            pe = nc.tensor
            for r_, (c, _) in enumerate(ROPED):
                if r_ >= 2:
                    pe.wait_ge(S("rope_out"), r_ - 1)
                b = 2 * (r_ % 2)
                wide(b, tb("rot"), cols[:, c, :]).then_inc(S("rope_rot"), 1)
            pe.wait_ge(S("rope_out"), 6)
            for w, c in enumerate((CSV, CWV)):
                for i, (t0, n) in enumerate(TILES):
                    o = ps_buf[0:n, 2 * w, i * P:i * P + P] if i < 4 else ps_buf[0:n, 2 * w + 1, 0:P]
                    last = pe.transpose(o, cols[:, c, t0:t0 + n], ident)
            last.then_inc(S("at_vrows"), 1)
            pe.wait_ge(S("at_gspread"), 4)
            for q in range(2):
                last = pe.matmul(ps_buf[:, 4, 24 * q:24 * q + 24], rtmp[64:88, P * q:P * q + P], ident[64:88, 64:88], start=True, stop=True)
            last.then_inc(S("at_gates"), 1)
            pe.wait_ge(S("cmp_in"), 2)
            pe.wait_ge(S("at_rows_out"), 1)
            for j in range(2):
                pe.wait_ge(S("cw1_in"), 16 * (j + 1))
                if j == 0:
                    for b in range(NB):
                        pe.wait_ge(S(f"pages_{b}"), 16 * PAGES)
                for g in range(2):
                    lo = 64 * g
                    u = 2 * j + g
                    for p_ in range(CLEN):
                        pe.matmul(bank(2 * u, 9 * CMP), cw1[lo:lo + 64, p_, :],
                                  ckb[lo:lo + 64, :, j, p_:p_ + STRIDE * (CMP - 1) + 1:STRIDE],
                                  start=p_ == 0, stop=p_ == CLEN - 1)
                        last = pe.matmul(bank(2 * u + 1, 1), cw1[lo:lo + 64, p_, :],
                                         vec[lo:lo + 64, VEC["cpos"] + 32 * j + p_:VEC["cpos"] + 32 * j + p_ + 1],
                                         start=p_ == 0, stop=p_ == CLEN - 1)
                    last.then_inc(S("cmp_hid"), 1)
            pe.wait_ge(S("cmp_silu"), 4)
            pe.wait_ge(S("cw2_in"), 16)
            for g in range(2):
                pe.matmul(ps_buf[64 * g:64 * g + 64, g, 0:9 * CMP], cw2[:, 0, :], hid[:, g, :], start=True, stop=True)
                for s_ in range(9):
                    o = ps_buf[0:CMP, 2 + 2 * g, 64 * s_:64 * s_ + 64] if s_ < 8 else ps_buf[0:CMP, 3 + 2 * g, 0:64]
                    last = pe.matmul(o, hid[:, 2 + g, CMP * s_:CMP * s_ + CMP], cw2[:, 1, :], start=True, stop=True)
            last.then_inc(S("cmp_kv"), 1)

        def cmp_act(a):
            ac = nc.scalar
            a(ac.activation(cols[64:88, CGATE, :], cols[64:88, CGATE, :], ACT.Sigmoid), S("at_gsig"))
            ac.wait_ge(S("cmp_bias"), 4)
            for u in range(4):
                a(ac.activation(hid[:, u, :], bank(2 * u, 9 * CMP), ACT.Silu, bias=posb[:, u:u + 1]), S("cmp_silu"))

        def cmp_dve(v):
            ve = nc.vector
            for r_, (c, q) in enumerate(ROPED):
                ve.wait_ge(S("rope_rot"), r_ + 1)
                b = 2 * (r_ % 2)
                dst = cols[:, c, :] if q is None else qrot[:, q, :]
                v(ve.tensor_tensor(halves(rtmp), two(b), halves(tb("sin")), ALU.mult))
                v(ve.tensor_tensor(dst, cols[:, c, :], tb("cos"), ALU.mult))
                v(ve.tensor_tensor(dst, dst, rtmp, ALU.add), S("rope_out"))
            ve.wait_ge(S("at_gsig"), 1)
            for i in range(4):
                v(ve.tensor_copy(rtmp[64:88, 0:256].rearrange("p (b i t) -> p b i t", i=4, t=TS)[:, :, i, :],
                                 cols[64:88, CGATE, SEQ:T].rearrange("p (b t) -> p b t", t=TS)), S("at_gspread"))
            for j in range(2):
                v(ve.tensor_copy(ckb[:, 8, j, :], cols[:, CCK + j, 0:SEQ]), S("cmp_in"))
            for w, src in ((0, None), (1, qrot)):
                for i in range(4):
                    s_ = cols[:, CNQ + i, SEQ:T] if src is None else qrot[:, i, SEQ:T]
                    dst = qrs[:, w, :].rearrange("p (b i t) -> p b i t", i=4, t=TS)[:, :, i, :]
                    v(ve.tensor_copy(dst, s_.rearrange("p (b t) -> p b t", t=TS)))
            ve.wait_ge(S("at_vrows"), 1)
            for w, dst in enumerate((svt, wvt)):
                v(ve.tensor_copy(dst[:, 0:4, :], bank(2 * w).rearrange("p (i c) -> p i c", i=4)))
                v(ve.tensor_copy(dst[0:64, 4, :], ps_buf[0:64, 2 * w + 1, 0:P]))
            ve.wait_ge(S("at_gates"), 1)
            for q in range(2):
                v(ve.tensor_tensor(sg24, ps_buf[:, 4, 24 * q:24 * q + 24], tb("rowi"), ALU.mult))
                v(ve.tensor_reduce(sgate[:, q, :, :], sg24.rearrange("p (g i k) -> p g k i", g=2, i=4), AX.X, ALU.add),
                  *([S("at_rows_out")] if q else []))
            for u in range(4):
                ve.wait_ge(S("cmp_hid"), u + 1)
                v(ve.tensor_copy(posb[:, u:u + 1], bank(2 * u + 1, 1)), S("cmp_bias"))
            ve.wait_ge(S("cmp_kv"), 1)
            for g in range(2):
                v(ve.tensor_copy(ckT[64 * g:64 * g + 64, :], ps_buf[64 * g:64 * g + 64, g, 0:9 * CMP]))
                v(ve.tensor_copy(cvt[0:CMP, 0:8, g, :], ps_buf[0:CMP, 2 + 2 * g, :].rearrange("p (s d) -> p s d", s=8)))
                v(ve.tensor_copy(cvt[0:CMP, 8, g, :], ps_buf[0:CMP, 3 + 2 * g, 0:64]))

        UNITS = [(i, h, g, br) for i in range(PT) for h in range(4) for g in range(2) for br in range(3)]
        NU = len(UNITS)

        def width(u):
            i, h, g, br = UNITS[u]
            return CMP if br == 0 else P * (i + 1)

        def at_pe():
            pe = nc.tensor

            def scores(u):
                i, h, g, br = UNITS[u]
                lo, t0, n = 64 * g, P * i, width(u)
                if u >= 2:
                    pe.wait_ge(S("at_exp"), u - 1)
                q = (cols[lo:lo + 64, CNQ + h, t0:t0 + P] if br == 0 else qrot[lo:lo + 64, h, t0:t0 + P])
                if br == 0:
                    kk = ckT[lo:lo + 64, 8 * CMP:9 * CMP]
                    mask = tb("cma")[:, CMP * i:CMP * i + CMP]
                else:
                    kk = cols[lo:lo + 64, CSK if br == 1 else CWK, 0:n]
                    mask = tb("tri")
                pe.matmul(bank(u % 2, n), q, kk, start=True, stop=False)
                m = mask.shape[1]
                pe.matmul(ps_buf[:, u % 2, n - m:n], ident, mask, start=False, stop=True).then_inc(S("at_scores"), 1)

            def turn(u):
                i, h, g, br = UNITS[u]
                n = width(u)
                pe.wait_ge(S("at_ready"), u + 1)
                if u >= 2:
                    pe.wait_ge(S("at_PT"), u - 1)
                for c in range((n + P - 1) // P):
                    w = min(P, n - P * c)
                    last = pe.transpose(ps_buf[0:w, 2 + u % 2, P * c:P * c + P], Sb[:, u % 2, P * c:P * c + w], ident)
                last.then_inc(S("at_T"), 1)

            def weigh(u):
                i, h, g, br = UNITS[u]
                n = width(u)
                pe.wait_ge(S("at_PT"), u + 1)
                if u >= 2:
                    pe.wait_ge(S("at_acc"), u - 1)
                cs = (n + P - 1) // P
                for c in range(cs):
                    w = min(P, n - P * c)
                    val = cvt[0:CMP, 8, g, :] if br == 0 else (svt if br == 1 else wvt)[:, c, 64 * g:64 * g + 64]
                    last = pe.matmul(bank(4 + u % 2, 64), PTb[0:w, u % 2, c, :], val, start=c == 0, stop=c == cs - 1)
                last.then_inc(S("at_pv"), 1)

            for s_ in range(NU + 2):
                if s_ < NU:
                    scores(s_)
                if 1 <= s_ <= NU:
                    turn(s_ - 1)
                if s_ >= 2:
                    weigh(s_ - 2)
            for h in range(4):
                if h == 0:
                    pe.wait_ge(S("at_acc"), NU)
                for i in range(PT):
                    last = pe.transpose(ps_buf[:, h, P * i:P * i + P], oacc[:, i, h, :], ident)
                last.then_inc(S("at_oT"), 1)

        def at_act(a):
            ac = nc.scalar
            for s_ in range(NU + 1):
                if s_ < NU:
                    u = s_
                    ac.wait_ge(S("at_max"), u + 1)
                    if u >= 2:
                        ac.wait_ge(S("at_T"), u - 1)
                    a(ac.activation(Sb[:, u % 2, 0:width(u)], bank(u % 2, width(u)), ACT.Exp, scale=SCALE,
                                    bias=stat[:, u % 4, 1:2], accum_out=stat[:, u % 4, 2:3]), S("at_exp"))
                if s_ >= 1:
                    u = s_ - 1
                    n = width(u)
                    ac.wait_ge(S("at_T"), u + 1)
                    if u >= 2:
                        ac.wait_ge(S("at_pv"), u - 1)
                    if n == CMP:
                        a(ac.copy(PTb[0:CMP, u % 2, 0, :], ps_buf[0:CMP, 2 + u % 2, 0:P]), S("at_PT"))
                    else:
                        a(ac.copy(PTb[:, u % 2, 0:n // P, :], bank(2 + u % 2, n).rearrange("p (c t) -> p c t", t=P)),
                          S("at_PT"))

        def at_dve(v):
            ve = nc.vector
            for s_ in range(NU + 2):
                if s_ < NU:
                    u = s_
                    st = stat[:, u % 4, :]
                    ve.wait_ge(S("at_scores"), u + 1)
                    v(ve.tensor_reduce(st[:, 0:1], bank(u % 2, width(u)), AX.X, ALU.max))
                    v(ve.tensor_scalar(st[:, 1:2], st[:, 0:1], -SCALE, None, ALU.mult), S("at_max"))
                if 1 <= s_ <= NU:
                    u = s_ - 1
                    i, h, g, br = UNITS[u]
                    st = stat[:, u % 4, :]
                    ve.wait_ge(S("at_exp"), u + 1)
                    if br == 0:
                        w = Sb[:, u % 2, 0:CMP]
                        v(ve.tensor_tensor(w, w, tb("cm1")[:, CMP * i:CMP * i + CMP], ALU.mult), S("at_ready"))
                        v(ve.tensor_reduce(st[:, 2:3], w, AX.X, ALU.add))
                        v(ve.tensor_scalar(st[:, 2:3], st[:, 2:3], 1e-30, None, ALU.max))
                    else:
                        ve.sem_inc(S("at_ready"), 1)
                if s_ >= 2:
                    u = s_ - 2
                    i, h, g, br = UNITS[u]
                    st = stat[:, u % 4, :]
                    k = 3 * (4 * g + h) + br
                    v(ve.reciprocal(st[:, 3:4], st[:, 2:3]))
                    v(ve.tensor_tensor(st[:, 3:4], st[:, 3:4], gates[:, i, k:k + 1], ALU.mult))
                    ve.wait_ge(S("at_pv"), u + 1)
                    o = oacc[:, i, h, 64 * g:64 * g + 64]
                    if br == 0:
                        v(ve.tensor_scalar(o, bank(4 + u % 2, 64), st[:, 3:4], None, ALU.mult), S("at_acc"))
                    else:
                        v(ve.scalar_tensor_tensor(o, bank(4 + u % 2, 64), st[:, 3:4], o, ALU.mult, ALU.add), S("at_acc"))
            for h in range(4):
                ve.wait_ge(S("at_oT"), h + 1)
                v(ve.tensor_copy(hmix[:, 4 + h, 0:SEQ], bank(h)))

        SU = [(q, g) for q in range(2) for g in range(2)]

        def sa_pe():
            pe = nc.tensor
            for u, (q, g) in enumerate(SU):
                lo = 64 * g
                qc = slice(128 * q, 128 * q + 128)
                if g == 0:
                    for b in range(4):
                        pe.wait_ge(S(f"qpages_{b}"), 16 * (2 * PAGES) * (q + 1))
                    pe.wait_ge(S("qwin"), 16 * 8 * (q + 1))
                if u:
                    pe.wait_ge(S("sa_unit"), u)
                for b in range(4):
                    last = pe.matmul(ps_buf[32 * b:32 * b + 32, 0, 0:CMP], qrs[lo:lo + 64, 0, 128 * q + 32 * b:128 * q + 32 * b + 32],
                                     ckT[lo:lo + 64, CMP * (4 * q + b):CMP * (4 * q + b) + CMP], start=True, stop=True)
                last.then_inc(S("sa_scores"), 1)
                pe.wait_ge(S("sa_p"), 3 * u + 1)
                pe.transpose(ps_buf[0:CMP, 2, 0:P], Sb[:, 0, 0:CMP], ident).then_inc(S("sa_T"), 1)
                pe.wait_ge(S("sa_PT"), 3 * u + 1)
                for b in range(4):
                    pe.matmul(ps_buf[32 * b:32 * b + 32, 4, 0:64], PTb[0:CMP, 0, 0, 32 * b:32 * b + 32],
                              cvt[0:CMP, 4 * q + b, g, :], start=True, stop=True)
                pe.matmul(bank(5, 9), PTb[0:CMP, 0, 0, :], tb("ov"), start=True, stop=True).then_inc(S("sa_pv"), 1)
                pe.wait_ge(S("sa_imp1"), u + 1)
                pe.matmul(bank(5, 9), tb("same"), impz, start=True, stop=True).then_inc(S("sa_imp"), 1)
                for br in (1, 2):
                    kq, kc = (skq, CSK) if br == 1 else (wkq, CWK)
                    vq, vt = (svq, svt) if br == 1 else (wvq, wvt)
                    pe.wait_ge(S("sa_acc"), 3 * u + br)
                    for b in range(4):
                        pe.matmul(ps_buf[32 * b:32 * b + 32, 0, 0:512], qrs[lo:lo + 64, 1, 128 * q + 32 * b:128 * q + 32 * b + 32],
                                  kq[lo:lo + 64, b, :], start=True, stop=True)
                    pe.matmul(bank(1, 64), qrs[lo:lo + 64, 1, qc], cols[lo:lo + 64, kc, SEQ:T], start=True,
                              stop=True).then_inc(S("sa_scores"), 1)
                    pe.wait_ge(S("sa_p"), 3 * u + br + 1)
                    for c in range(4):
                        pe.transpose(ps_buf[:, 2, P * c:P * c + P], Sb[:, 0, P * c:P * c + P], ident)
                    pe.transpose(ps_buf[0:64, 3, 0:P], Sb[:, 0, SEQ:T], ident).then_inc(S("sa_T"), 1)
                    pe.wait_ge(S("sa_PT"), 3 * u + br + 1)
                    for b in range(4):
                        o = ps_buf[32 * b:32 * b + 32, 4, 0:64]
                        r_ = slice(32 * b, 32 * b + 32)
                        for c in range(4):
                            pe.matmul(o, PTb[:, 0, c, r_], vq[:, b, c, lo:lo + 64], start=c == 0, stop=False)
                        last = pe.matmul(o, PTb[0:64, 0, 4, r_], vt[0:64, 4, lo:lo + 64], start=False, stop=True)
                    last.then_inc(S("sa_pv"), 1)
            pe.wait_ge(S("sa_unit"), 4)
            for q in range(2):
                last = pe.transpose(ps_buf[:, 6, P * q:P * q + P], osamp[:, q, :], ident)
            last.then_inc(S("sa_oT"), 1)

        def sa_act(a):
            ac = nc.scalar
            for u in range(4):
                for br in range(3):
                    n = CMP if br == 0 else T
                    ac.wait_ge(S("sa_max"), 3 * u + br + 1)
                    src = bank(0, CMP) if br == 0 else Sb[:, 0, :]
                    a(ac.activation(Sb[:, 0, 0:n], src, ACT.Exp, scale=SCALE, bias=stat[:, 0, 1:2],
                                    accum_out=stat[:, 0, 2:3]), S("sa_exp"))
                    ac.wait_ge(S("sa_T"), 3 * u + br + 1)
                    if br == 0:
                        a(ac.copy(PTb[0:CMP, 0, 0, :], ps_buf[0:CMP, 2, 0:P]), S("sa_PT"))
                    else:
                        a(ac.copy(PTb[:, 0, 0:4, :], bank(2).rearrange("p (c t) -> p c t", t=P)))
                        a(ac.copy(PTb[0:64, 0, 4, :], ps_buf[0:64, 3, 0:P]), S("sa_PT"))

        def sa_dve(v):
            ve = nc.vector
            st = stat[:, 0, :]
            v(ve.memset(kbias, 0.0))
            for u, (q, g) in enumerate(SU):
                for br in range(3):
                    ve.wait_ge(S("sa_scores"), 3 * u + br + 1)
                    if br == 0:
                        src = bank(0, CMP)
                    else:
                        src = Sb[:, 0, :]
                        if br == 1:
                            v(ve.tensor_tensor(Sb[:, 0, 0:512].rearrange("p (s k) -> p s k", s=8),
                                               bank(0).rearrange("p (s k) -> p s k", s=8),
                                               kbias.unsqueeze(2).to_broadcast([P, 8, HD]), ALU.add))
                        else:
                            v(ve.tensor_copy(Sb[:, 0, 0:512], bank(0)))
                            v(ve.tensor_tensor(Sb[:, 0, 0:8], Sb[:, 0, 0:8], tb("winm"), ALU.add))
                        v(ve.tensor_tensor(Sb[:, 0, SEQ:T], bank(1, 64), tb("newm")[:, 64 * q:64 * q + 64], ALU.add))
                    v(ve.tensor_reduce(st[:, 0:1], src, AX.X, ALU.max))
                    v(ve.tensor_scalar(st[:, 1:2], st[:, 0:1], -SCALE, None, ALU.mult), S("sa_max"))
                    ve.wait_ge(S("sa_exp"), 3 * u + br + 1)
                    v(ve.reciprocal(st[:, 3:4], st[:, 2:3]))
                    if br == 0:
                        v(ve.tensor_scalar(Sb[:, 0, 0:CMP], Sb[:, 0, 0:CMP], st[:, 3:4], None, ALU.mult), S("sa_p"))
                    else:
                        v(ve.tensor_tensor(st[:, 3:4], st[:, 3:4], sgate[:, q, g, br:br + 1], ALU.mult), S("sa_p"))
                    ve.wait_ge(S("sa_pv"), 3 * u + br + 1)
                    o = osamp[:, q, 64 * g:64 * g + 64]
                    if br == 0:
                        v(ve.tensor_scalar(o, bank(4, 64), sgate[:, q, g, 0:1], None, ALU.mult))
                        v(ve.tensor_copy(impz, bank(5, 9)), S("sa_imp1"))
                        ve.wait_ge(S("sa_imp"), u + 1)
                        v(ve.tensor_copy(imps, bank(5, 9)))
                        v(ve.tensor_reduce(iw[:, 6:7], imps[:, 1:7], AX.X, ALU.min))
                        v(ve.tensor_scalar(iw[:, 0:6], imps[:, 1:7], iw[:, 6:7], None, ALU.is_equal))
                        v(ve.tensor_tensor(iw[:, 0:6], iw[:, 0:6], tb("rank")[:, 0:6], ALU.mult))
                        v(ve.tensor_reduce(iw[:, 6:7], iw[:, 0:6], AX.X, ALU.max))
                        v(ve.tensor_scalar(kbias[:, 1:7], tb("rank")[:, 0:6], iw[:, 6:7], NEG, ALU.is_equal, ALU.mult))
                        ve.sem_inc(S("sa_acc"), 1)
                    else:
                        v(ve.scalar_tensor_tensor(o, bank(4, 64), st[:, 3:4], o, ALU.mult, ALU.add), S("sa_acc"),
                          *([S("sa_unit")] if br == 2 else []))
            ve.wait_ge(S("sa_oT"), 1)
            for q in range(2):
                for h in range(4):
                    v(ve.tensor_copy(hmix[:, 4 + h, SEQ + 32 * q:SEQ + 32 * q + 32].rearrange("p (b t) -> p b t", t=TS),
                                     ps_buf[:, 6, P * q:P * q + P].rearrange("p (b i t) -> p b i t", i=4, t=TS)[:, :, h, :]))

        def wo_sp(l):
            for c in range(KD):
                if c >= 3:
                    sync.wait_ge(S("wo_split"), c - 2)
                sync.dma_start(raw(c % 3, KD), A["w_out"][l * KD + c].rearrange("p k c -> p (k c)"))\
                    .then_inc(S(f"w_out_{c % 3}"), 16)

        def wo_act(a):
            for k in range(KD):
                if k >= 2:
                    nc.scalar.wait_ge(S("wo_x"), k - 1)
                a(nc.scalar.copy(split_v[:, k % 2, :], hmix[:, k, :]), S("wo_x_hi"))
                if k < 3:
                    wo_hi(a, k)
            for c in range(3, KD):
                wo_hi(a, c)

        def wo_hi(a, c):
            nc.scalar.wait_ge(S(f"w_out_{c % 3}"), 16 * (c // 3 + 1))
            if c >= 3:
                nc.scalar.wait_ge(S("wo_done"), c - 2)
            split_hi(a, c % 3, c % 3, KD, UNIT, S("wo_hi"))

        def wo_pool(g):
            for c in range(KD):
                nc.gpsimd.wait_ge(S("wo_hi"), c + 1)
                split_lo(g, c % 3, c % 3, KD, UNIT, S("wo_split"))

        def wo_pe():
            for c in range(KD):
                nc.tensor.wait_ge(S("wo_split"), c + 1)
                if c >= 3:
                    nc.tensor.wait_ge(S("wo_out"), c - 2)
                b = 2 * (c % 3)
                unit_products(c % 3, KD, UNIT, XH, XL, b,
                              (lambda k: nc.tensor.wait_ge(S("wo_x"), k + 1)) if c == 0 else None)\
                    .then_inc(S("wo_done"), 1)

        def wo_dve(v):
            ve = nc.vector
            for k in range(KD):
                ve.wait_ge(S("wo_x_hi"), k + 1)
                v(ve.tensor_tensor(XL[:, k, :], hmix[:, k, :], split_v[:, k % 2, :].bitcast(F32), ALU.subtract))
                v(ve.tensor_copy(XH[:, k, :], split_v[:, k % 2, :].bitcast(F32)), S("wo_x"))
            for c in range(KD):
                ve.wait_ge(S("wo_done"), c + 1)
                b = 2 * (c % 3)
                v(ve.tensor_tensor(halves(x[:, c, :]), halves(x[:, c, :]), two(b), ALU.add), S("wo_out"))

        def rt_pe():
            pe = nc.tensor
            pe.wait_ge(S("ffn_norm_done"), KD)
            for i, (t0, n) in enumerate(TILES):
                for k in range(KD):
                    for w, m in ((0, XH), (1, XL)):
                        last = pe.matmul(ps_buf[0:n, 2, 8 * i:8 * i + 8], m[:, k, t0:t0 + n].bitcast(F32),
                                         router[:, k, :], start=k == 0 and w == 0, stop=k == KD - 1 and w == 1)
            last.then_inc(S("rt_logits"), 1)
            pe.wait_ge(S("rt_comb"), 1)
            for i, (t0, n) in enumerate(TILES):
                o = ps_buf[0:8, 3, t0:t0 + n] if i < 4 else ps_buf[0:8, 4, 0:n]
                last = pe.transpose(o, lw[0:n, 0, 8 * i:8 * i + 8], ident[0:n, 0:n])
            last.then_inc(S("rt_T"), 1)

        def rt_act(a):
            ac = nc.scalar
            ac.wait_ge(S("rt_diff"), 1)
            a(ac.activation(lw[:, 7, 0:5], lw[:, 7, 0:5], ACT.Exp), S("rt_exp"))

        def rt_dve(v):
            ve = nc.vector

            def g5(k):
                return lw[:, k, :].rearrange("p (i e) -> p i e", i=5)

            def spread5(ap):
                return ap.unsqueeze(2).to_broadcast([P, 5, 8])

            v(ve.memset(lg, 0.0))
            ve.wait_ge(S("rt_logits"), 1)
            v(ve.tensor_copy(lg[:, 0:4, :], ps_buf[:, 2, 0:32].rearrange("p (i e) -> p i e", i=4)))
            v(ve.tensor_copy(lg[0:64, 4, :], ps_buf[0:64, 2, 32:40]))
            m = [lw[:, 5, 0:5], lw[:, 6, 0:5]]
            rank = tb("rrank").rearrange("p (i e) -> p i e", i=5)
            for k in range(2):
                v(ve.tensor_reduce(m[k], lg, AX.X, ALU.max))
                v(ve.tensor_tensor(g5(4), lg, spread5(m[k]), ALU.is_equal))
                v(ve.tensor_tensor(g5(4), g5(4), rank, ALU.mult))
                v(ve.tensor_reduce(lw[:, 7, 8:13], g5(4), AX.X, ALU.max))
                v(ve.tensor_tensor(g5(1 + k), rank, spread5(lw[:, 7, 8:13]), ALU.is_equal))
                if k == 0:
                    v(ve.scalar_tensor_tensor(lg, g5(1), NEG, lg, ALU.mult, ALU.add))
            v(ve.tensor_tensor(lw[:, 7, 0:5], m[1], m[0], ALU.subtract), S("rt_diff"))
            ve.wait_ge(S("rt_exp"), 1)
            v(ve.tensor_scalar(lw[:, 5, 0:5], lw[:, 7, 0:5], 1.0, None, ALU.add))
            v(ve.reciprocal(lw[:, 5, 0:5], lw[:, 5, 0:5]))
            v(ve.tensor_tensor(lw[:, 6, 0:5], lw[:, 7, 0:5], lw[:, 5, 0:5], ALU.mult))
            v(ve.tensor_tensor(g5(1), g5(1), spread5(lw[:, 5, 0:5]), ALU.mult))
            v(ve.tensor_tensor(g5(2), g5(2), spread5(lw[:, 6, 0:5]), ALU.mult))
            v(ve.tensor_tensor(lw[:, 0, :], lw[:, 1, :], lw[:, 2, :], ALU.add))
            v(ve.tensor_scalar(lw[:, 0, :], lw[:, 0, :], -1.0, V("flag"), ALU.add, ALU.mult))
            v(ve.tensor_scalar(lw[:, 0, :], lw[:, 0, :], 1.0, None, ALU.add), S("rt_comb"))
            ve.wait_ge(S("rt_T"), 1)
            v(ve.tensor_copy(cT[0:8, 0:SEQ], ps_buf[0:8, 3, :]))
            v(ve.tensor_copy(cT[0:8, SEQ:T], ps_buf[0:8, 4, 0:64]), S("rt_cT"))

        NUN = 2 * FC + KD
        FREE_RAW, FREE_PARTS, FREE_OUT = 3, 3, 2

        def nk_of(u):
            return KD if u < 2 * FC else FC

        def ex_sp(e):
            for u in range(NUN):
                sync.wait_ge(S("g_raw_free"), e * NUN + (u + 1))
                src = A["w13"][e * 2 * FC + u] if u < 2 * FC else A["w2"][e * KD + (u - 2 * FC)]
                sync.dma_start(raw(u % 3, nk_of(u)), src).then_inc(S(f"g_raw_in_{u % 3}"), 16)

        def ex_act(a, e):
            ac = nc.scalar
            for u in range(NUN):
                ac.wait_ge(S(f"g_raw_in_{u % 3}"), e * (16 * NUN // 3) + 16 * (u // 3 + 1))
                ac.wait_ge(S("g_unit_done"), e * NUN + (u + 1))
                split_hi(a, u % 3, u % 3, nk_of(u), UNIT, S("g_w_hi"))
                if u >= 4 and u % 2 == 0 and (u - 4) // 2 < FC:
                    f = (u - 4) // 2
                    ac.wait_ge(S("g_unit_done"), e * NUN + (2 * f + 1 + FREE_PARTS))
                    ac.wait_ge(S("g_h"), e * FC + (f + 1))
                    a(ac.activation(halves(sg[:, f % 2, :]), two(0), ACT.Silu), S("g_silu"))

        def ex_pool(g, e):
            for u in range(NUN):
                nc.gpsimd.wait_ge(S("g_w_hi"), e * NUN + (u + 1))
                split_lo(g, u % 3, u % 3, nk_of(u), UNIT, S("g_w_ready"), S("g_raw_free"))

        def ex_pe(e):
            pe = nc.tensor
            for u in range(NUN):
                pe.wait_ge(S("g_w_ready"), e * NUN + (u + 1))
                if u < 2 * FC:
                    f, w = u // 2, u % 2
                    if f and w == 0:
                        pe.wait_ge(S("g_silu"), e * FC + f)
                    if f and w == 1:
                        pe.wait_ge(S("g_h"), e * FC + (f + 2))
                    unit_products(u % 3, KD, UNIT, XH, XL, 2 * w)\
                        .then_inc(S("g_unit_done"), 1)
                    if u == 1:
                        pe.wait_ge(S("g_gate_row"), e + 1)
                        wide(6, tb("ones")[0:8, :], cTe[0:8, :]).then_inc(S("g_gate"), 1)
                else:
                    c = u - 2 * FC
                    pe.wait_ge(S("g_out_free"), e * KD + (c + 1))
                    before = None
                    if c == 0:
                        def before(k):
                            if k in (0, FC - 1):
                                pe.wait_ge(S("g_h"), e * FC + ((FC - 1 if k == 0 else FC) + 2))
                    unit_products(u % 3, FC, UNIT, HH, HL, 4 + 2 * (c % 2),
                                  before).then_inc(S("g_unit_done"), 1)

        def ex_dve(v, e, le):
            ve = nc.vector
            v(ve.tensor_scalar(cTe[0:8, :], cT[0:8, :], ident[0:8, bass.ds(le, 1)], None, ALU.mult), S("g_gate_row"))
            ve.wait_ge(S("g_gate"), e + 1)
            v(ve.tensor_copy(halves(combE), two(6)))
            for f in range(FC):
                ve.wait_ge(S("g_silu"), e * FC + (f + 1))
                ve.wait_ge(S("g_unit_done"), e * NUN + (2 * f + 2 + FREE_PARTS))
                h = htmp[:, f % 2, :]
                v(ve.tensor_tensor(halves(h), halves(sg[:, f % 2, :]), two(2), ALU.mult))
                v(ve.tensor_tensor(h, h, combE, ALU.mult))
                v(ve.tensor_copy(HH[:, f, :], h))
                v(ve.tensor_tensor(HL[:, f, :], h, HH[:, f, :].bitcast(F32), ALU.subtract), S("g_h"))
            for c in range(KD):
                ve.wait_ge(S("g_unit_done"), e * NUN + (2 * FC + c + 1 + FREE_PARTS))
                v(ve.tensor_tensor(halves(x[:, c, :]), halves(x[:, c, :]), two(4 + 2 * (c % 2)), ALU.add),
                  S("g_out_free"))

        def iteration_ends(eng, tag):
            eng.drain().then_inc(S(tag + "_arrived"), 1)
            eng.wait_ge(S(tag + "_go"), 1)
            eng.sem_inc(S(tag + "_left"), 1)

        def clear(tag):
            sync.wait_ge(S(tag + "_arrived"), 4)
            S(tag + "_go"), S(tag + "_left")
            if tag == "half":
                own = {s.num for s in shared}
            else:
                own = {s.num for n, s in sems.items() if not n.startswith(("g_", "layer_", "half_"))}
            own = sorted(own | {S(tag + "_arrived").num})
            k = 0
            while k < len(own):
                m = k
                while m + 1 < len(own) and own[m + 1] == own[m] + 1:
                    m += 1
                sync.sem_clear(range(own[k], own[m] + 1))
                k = m + 1
            sync.sem_inc(S(tag + "_go"), 1)
            sync.wait_ge(S(tag + "_left"), 4)
            for n in ("_go", "_left"):
                sync.sem_clear(S(tag + n))

        def experts(l):
            return 2 + 6 * l

        with nc.Block() as block:
            @block.vector
            def _(eng):
                v = Chain(eng, S("dve_chain"))
                eng.wait_ge(S("g_in"), 80)
                v0 = Chain(eng, S("g_chain_dve"))
                v0(nc.vector.memset(gates, 0.0))
                eng.sem_inc(S("g_out_free"), FREE_OUT)
                eng.sem_inc(S("g_h"), 2)
                with eng.Fori(0, DEPTH) as l:
                    eng.wait_ge(S("small_in"), 48)
                    norm_dve(v, "mix_norm", rstd, lambda k: V("nmix", k))
                    proj_dve(v)
                    meet(eng, "dve")
                    rows_dve(v)
                    ml_dve(v)
                    eng.wait_ge(S("ml_outs"), 48)
                    meet(eng, "dve")
                    rwprep_dve(v)
                    rw_dve(v)
                    hn_dve(v)
                    eng.wait_ge(S("rw_outs"), 32)
                    iteration_ends(eng, "half")
                    cmp_dve(v)
                    meet(eng, "dve")
                    at_dve(v)
                    meet(eng, "dve")
                    sa_dve(v)
                    meet(eng, "dve")
                    wo_dve(v)
                    eng.wait_ge(S("kv_outs"), 32)
                    meet(eng, "dve")
                    norm_dve(v, "ffn_norm", rstd, lambda k: V("nffn", k))
                    rt_dve(v)
                    meet(eng, "dve")
                    with eng.Fori(0, experts(l)) as e:
                        ex_dve(Chain(eng, S("g_chain_ex_dve")), e + 2 * l, e)
                        eng.sem_clear(S("g_chain_ex_dve"))
                    iteration_ends(eng, "layer")
                norm_dve(v0, "g_fin", rstd, lambda k: nfin[:, k:k + 1], final=True)

            @block.scalar
            def _(eng):
                a = Chain(eng, S("act_chain"))
                eng.wait_ge(S("g_in"), 80)
                with eng.Fori(0, DEPTH) as l:
                    eng.wait_ge(S("small_in"), 48)
                    norm_act(a, "mix_norm", rstd)
                    proj_act(a)
                    meet(eng, "act")
                    rows_act(a)
                    ml_act(a)
                    meet(eng, "act")
                    rwprep_act(a)
                    hn_act(a)
                    iteration_ends(eng, "half")
                    cmp_act(a)
                    meet(eng, "act")
                    at_act(a)
                    meet(eng, "act")
                    sa_act(a)
                    meet(eng, "act")
                    wo_act(a)
                    meet(eng, "act")
                    norm_act(a, "ffn_norm", rstd)
                    rt_act(a)
                    meet(eng, "act")
                    with eng.Fori(0, experts(l)) as e:
                        ex_act(Chain(eng, S("g_chain_ex_act")), e + 2 * l)
                        eng.sem_clear(S("g_chain_ex_act"))
                    iteration_ends(eng, "layer")
                norm_act(Chain(eng, S("g_chain_act")), "g_fin", rstd, final=True)

            @block.gpsimd
            def _(eng):
                g = Chain(eng, S("pool_chain"))
                with eng.Fori(0, DEPTH) as l:
                    proj_pool(g)
                    iteration_ends(eng, "half")
                    wo_pool(g)
                    with eng.Fori(0, experts(l)) as e:
                        ex_pool(Chain(eng, S("g_chain_ex_pool")), e + 2 * l)
                        eng.sem_clear(S("g_chain_ex_pool"))
                    iteration_ends(eng, "layer")

            @block.tensor
            def _(eng):
                eng.wait_ge(S("g_in"), 80)
                eng.sem_inc(S("g_unit_done"), FREE_PARTS)
                with eng.Fori(0, DEPTH) as l:
                    norm_pe("mix_norm")
                    proj_pe()
                    meet(eng, "pe")
                    ml_pe()
                    meet(eng, "pe")
                    rwprep_pe()
                    rw_pe()
                    hn_pe()
                    iteration_ends(eng, "half")
                    cmp_pe()
                    meet(eng, "pe")
                    at_pe()
                    meet(eng, "pe")
                    sa_pe()
                    meet(eng, "pe")
                    wo_pe()
                    meet(eng, "pe")
                    norm_pe("ffn_norm")
                    rt_pe()
                    meet(eng, "pe")
                    with eng.Fori(0, experts(l)) as e:
                        ex_pe(e + 2 * l)
                    iteration_ends(eng, "layer")
                norm_pe("g_fin")

            @block.sync
            def _(eng):
                eng.dma_start(tab[:, :], A["tab"]).then_inc(S("g_in"), 16)
                eng.dma_start(x, A["x"]).then_inc(S("g_in"), 16)
                eng.dma_start(router, A["router"]).then_inc(S("g_in"), 16)
                eng.dma_start(nfin, A["nfin"]).then_inc(S("g_in"), 16)
                eng.dma_start(page_buf[:, :], A["pages"]).then_inc(S("g_in"), 16)
                eng.wait_ge(S("g_in"), 80)
                eng.sem_inc(S("g_raw_free"), FREE_RAW)
                for l in range(DEPTH):
                    for b in range(NB):
                        eng.dma_start(A["o_win"][l, b, 0:PAST - TS], A["win"][l, b, TS:PAST]).then_inc(S("g_win"), 16)
                with eng.Fori(0, DEPTH) as l:
                    one = lambda name, k: A[name][bass.ds(k, 1)]

                    def ld(dst, name, k, sem):
                        eng.dma_start(dst, A[name][k]).then_inc(S(sem), 16)

                    ld(vec, "vec", l, "small_in")
                    ld(state_in, "state", l, "small_in")
                    ld(m0_in[0:4, :], "m0", l, "small_in")
                    proj_sp(l)
                    eng.wait_ge(S("conv_done"), 4)
                    eng.wait_ge(S("shift_done"), 8)
                    eng.dma_start(A["o_state"][l], state_out).then_inc(S("state_outs"), 16)
                    eng.wait_ge(S("phase_ended"), 3)
                    for j in range(2):
                        ld(Cs[:, j].rearrange("p b c -> p (b c)"), "C0", 2 * l + j, "ml_state_in")
                    eng.wait_ge(S("m_out"), 1)
                    eng.dma_start(A["o_m"][l], seg12[0:4, 2, :]).then_inc(S("ml_outs"), 16)
                    eng.wait_ge(S("ml_final"), 1)
                    eng.dma_start(A["o_Cp"][l], Cp).then_inc(S("ml_outs"), 16)
                    eng.dma_start(A["o_Cs"][l], Cs.rearrange("p j b c -> p (j b c)")).then_inc(S("ml_outs"), 16)
                    eng.wait_ge(S("phase_ended"), 6)
                    ld(rw_w[:, 0, :], "lora", 2 * l, "rw_w_in")
                    ld(rw_w[:, 1, :], "lora", 2 * l + 1, "rw_w_in")
                    ld(S0s.rearrange("p j b c -> p (j b c)"), "S0", l, "rw_state_in")
                    eng.wait_ge(S("rw_final"), 1)
                    eng.dma_start(A["o_Sp"][l], S0).then_inc(S("rw_outs"), 16)
                    eng.dma_start(A["o_Ss"][l], S0s.rearrange("p j b c -> p (j b c)")).then_inc(S("rw_outs"), 16)
                    clear("half")
                    ld(cw1.rearrange("p a b -> p (a b)"), "cw1", 2 * l, "cw1_in")
                    ld(cw2.rearrange("p a b -> p (a b)"), "cw2", l, "cw2_in")
                    pages = 40
                    for b in range(NB):
                        for c in range(PAGES):
                            k = b * PAGES + c
                            pg = eng.value_load(page_buf[0:1, k:k + 1], min_val=0, max_val=pages - 1)
                            eng.dma_start(ckb[:, b, :, P * c:P * c + P],
                                          A["pages_k"][l * pages + pg][:, 0:2, :]).then_inc(S(f"pages_{b}"), 16)
                    eng.wait_ge(S("rope_out"), 6)
                    eng.dma_start(A["o_kv"][l], cols[:, CCK:CCK + 4, :]).then_inc(S("kv_outs"), 16)
                    eng.dma_start(A["o_wkv"][l], cols[:, CWK:CWK + 2, :]).then_inc(S("kv_outs"), 16)
                    eng.wait_ge(S("cmp_hid"), 2)
                    ld(cw1.rearrange("p a b -> p (a b)"), "cw1", 2 * l + 1, "cw1_in")
                    eng.wait_ge(S("phase_ended"), 9)
                    for q in range(2):
                        if q:
                            eng.wait_ge(S("sa_unit"), 2)
                        for b in range(4):
                            for c in range(PAGES):
                                k = (4 * q + b) * PAGES + c
                                pg = eng.value_load(page_buf[0:1, k:k + 1], min_val=0, max_val=pages - 1)
                                eng.dma_start(skq[:, b, P * c:P * c + P],
                                              A["pages_k"][l * pages + pg][:, 2, :]).then_inc(S(f"qpages_{b}"), 16)
                                eng.dma_start(svq[:, b, c, :],
                                              A["pages_v"][l * pages + pg]).then_inc(S(f"qpages_{b}"), 16)
                            eng.dma_start(wkq[:, b, :], A["win_k"][l * NB + 4 * q + b]).then_inc(S("qwin"), 16)
                            eng.dma_start(wvq[:, b, :, :],
                                          A["win_v"][l * NB + 4 * q + b].rearrange("(c p) d -> p c d", p=P)).then_inc(S("qwin"), 16)
                    eng.wait_ge(S("phase_ended"), 15)
                    wo_sp(l)
                    eng.wait_ge(S("state_outs"), 16)
                    eng.wait_ge(S("phase_ended"), 21)
                    with eng.Fori(0, experts(l)) as e:
                        ex_sp(e + 2 * l)
                    clear("layer")
                eng.wait_ge(S("g_fin_done"), KD)
                eng.dma_start(A["o_y"], hmix).then_inc(S("g_y"), 16)
                eng.wait_ge(S("g_y"), 16)
                eng.wait_ge(S("g_win"), 16 * DEPTH * NB)

            return len(sems)


ML_W, RW0, NS0 = 1032, 1032, 2056


def in_columns():
    r = lambda a, n: list(range(a, a + n))
    out = r(0, 1024)
    out += r(RW0, 256) + r(RW0 + 256, 64) + r(RW0 + 832, 64) + r(RW0 + 320, 256) + r(RW0 + 576, 256) + r(RW0 + 896, 128)
    for i in range(4):
        out += r(NS0 + 64 * i, 64) + r(NS0 + 64 * (4 + i), 64)
    out += r(NS0 + 512, 768)
    gate = [-1] * P
    gate[0:4], gate[32:36], gate[64:88] = r(1024, 4), r(1028, 4), r(NS0 + 1280, 24)
    return out + gate


def rw_columns():
    r = lambda a, n: list(range(a, a + n))
    return r(0, 256) + r(256, 64) + r(832, 64) + r(320, 256) + r(576, 256) + r(896, 128)


def pack(inp):
    n = {k: np.asarray(v) for k, v in inp.items()}
    f = np.float32
    o = {}
    at, w = table_layout()
    t = np.zeros((P, w), f)
    for k, a in tables().items():
        c, r, m = at[k]
        t[0:r, c:c + m] = a
    o["tab"] = t
    x = np.concatenate([n["x_prompt"].reshape(SEQ, D), n["x_sample"].reshape(NS_TOK, D)], 0)

    def chans(a):
        return np.moveaxis(a.reshape(a.shape[:-1] + (-1, P)), -1, -2)

    o["x"] = x.T.reshape(KD, P, T).transpose(1, 0, 2)
    cols = np.array(in_columns())
    w_in = np.where(cols >= 0, n["w_in"][:, :, np.maximum(cols, 0)], f(0))
    o["w_in"] = w_in.reshape(DEPTH, KD, P, NCH, P).transpose(0, 3, 2, 1, 4).reshape(DEPTH * NCH, P, KD, P)
    mix = list(range(512))
    for i in range(4):
        mix += list(range(512 + 64 * i, 576 + 64 * i)) + list(range(512 + 64 * (4 + i), 576 + 64 * (4 + i)))
    o["w_out"] = n["w_out"][:, mix].reshape(DEPTH, KD, P, KD, P).transpose(0, 3, 2, 1, 4).reshape(DEPTH * KD, P, KD, P)
    E1 = FC * P

    def up(dense, moe):
        d = dense[0].reshape(D, 2, E1).transpose(1, 0, 2)
        a = np.concatenate([d, moe[0]], 0)
        return a.reshape(10, KD, P, FC, P).transpose(0, 3, 2, 1, 4)

    o["w13"] = np.stack([up(n["ffn_w1"], n["moe_w1"]), up(n["ffn_w3"], n["moe_w3"])], 2).reshape(20 * FC, P, KD * P)
    w2 = np.concatenate([n["ffn_w2"][0].reshape(2, E1, D), n["moe_w2"][0]], 0)
    o["w2"] = w2.reshape(10, FC, P, KD, P).transpose(0, 3, 2, 1, 4).reshape(10 * KD, P, FC * P)
    o["router"] = n["moe_router"][0].reshape(KD, P, 8).transpose(1, 0, 2)
    o["nfin"] = chans(n["norm_final_w"])
    v = np.zeros((DEPTH, P, NV), f)

    def put(name, a):
        v[:, :, VEC[name]:VEC[name] + a.shape[-1]] = a

    rwc = rw_columns()
    put("nmix", chans(n["norm_mix_w"]))
    put("nffn", chans(n["norm_ffn_w"]))
    put("convw", chans(n["ml_conv_w"]).transpose(0, 2, 1, 3).reshape(DEPTH, P, 16))
    put("convb", chans(n["ml_conv_b"]))
    put("mu", chans(n["rw_mu"][:, rwc]))
    for name, key in (("w0", "rw_w0"), ("a0", "rw_a0"), ("kk", "rw_k_k"), ("ka", "rw_k_a"), ("lnw", "rw_ln_w"),
                      ("lnb", "rw_ln_b"), ("mlw", "ml_norm_w")):
        put(name, chans(n[key]))
    put("rk", chans(n["rw_r_k"].reshape(DEPTH, 256)))
    v[:, 0:4, VEC["gb"]] = n["ml_b_i"]
    v[:, 32:36, VEC["gb"]] = n["ml_b_f"]
    v[1, :, VEC["flag"]] = 1.0
    pos = n["nsa_cmp_pos"].transpose(0, 3, 1, 2).reshape(DEPTH, HD, 64)
    put("cpos", np.concatenate([pos, pos], 1))
    o["vec"] = v
    conv = n["state_mlstm_conv"].transpose(0, 3, 1, 2).reshape(DEPTH, 4, P, NB * 3).transpose(0, 2, 1, 3)
    shift = n["state_rwkv_shift"][:, :, rwc].transpose(0, 2, 1).reshape(DEPTH, 8, P, NB).transpose(0, 2, 1, 3)
    o["state"] = np.concatenate([conv.reshape(DEPTH, P, -1), shift.reshape(DEPTH, P, -1)], 2)
    o["m0"] = n["state_mlstm_m"].transpose(0, 2, 1)
    C = np.zeros((DEPTH, 2, P, NB, 130), f)
    S_ = np.zeros((DEPTH, P, 2, NB, P), f)
    for h in range(4):
        j, q = h // 2, h % 2
        C[:, j, 64 * q:64 * q + 64, :, 65 * q:65 * q + 64] = n["state_mlstm_C"][:, :, h].transpose(0, 3, 1, 2)
        C[:, j, 64 * q:64 * q + 64, :, 65 * q + 64] = n["state_mlstm_n"][:, :, h].transpose(0, 2, 1)
        S_[:, 64 * q:64 * q + 64, j, :, 64 * q:64 * q + 64] = n["state_rwkv_S"][:, :, h].transpose(0, 3, 1, 2)
    o["C0"] = C.reshape(DEPTH * 2, P, NB * 130)
    o["S0"] = S_.reshape(DEPTH, P, 2 * NB * P)
    lora = np.zeros((DEPTH, 2, P, 256), f)
    lora[:, 0, 0:64], lora[:, 0, 64:128], lora[:, 1] = n["rw_w2"], n["rw_a2"], n["rw_g2"]
    o["lora"] = lora.reshape(DEPTH * 2, P, 256)
    cw1 = n["nsa_cmp_w1"].reshape(DEPTH, 2, CLEN, HD, P).transpose(0, 1, 3, 2, 4)
    o["cw1"] = np.concatenate([cw1, cw1], 2).reshape(DEPTH * 2, P, CLEN * P)
    o["cw2"] = n["nsa_cmp_w2"].transpose(0, 2, 1, 3).reshape(DEPTH, P, P)
    kv = n["cache_nsa_kv"].reshape(DEPTH * 40, P, 4, P)
    o["pages_k"] = kv[:, :, 0:3].transpose(0, 3, 2, 1)
    o["pages_v"] = kv[:, :, 3]
    win = n["cache_win_kv"].reshape(DEPTH, NB, PAST, 2, P)
    o["win"] = win.reshape(DEPTH, NB, PAST, 256)
    o["win_k"] = win[:, :, :, 0].transpose(0, 1, 3, 2).reshape(DEPTH * NB, P, PAST)
    o["win_v"] = win[:, :, :, 1].reshape(DEPTH * NB, PAST, P)
    o["pages"] = n["page_table"].reshape(1, NB * PAGES).astype(np.int32)
    return {k: np.ascontiguousarray(a) for k, a in o.items()}


OUTS = {
    "o_y": (P, KD, T), "o_kv": (DEPTH, P, 4, T), "o_wkv": (DEPTH, P, 2, T), "o_win": (DEPTH, NB, PAST, 256),
    "o_state": (DEPTH, P, OUT_W), "o_m": (DEPTH, 4, 12), "o_Cp": (DEPTH, P, 260), "o_Cs": (DEPTH, P, 2 * NB * 130),
    "o_Sp": (DEPTH, P, 256), "o_Ss": (DEPTH, P, 2 * NB * P),
}


def unpack(r):
    y = r["o_y"].transpose(2, 1, 0).reshape(T, D)
    out = [y[None, 0:SEQ], y[SEQ:].reshape(NB, TS, D)]
    kv = r["o_kv"].transpose(0, 3, 2, 1)
    out += [kv[:, None, 0:SEQ].reshape(DEPTH, 1, SEQ, 4, 2, HD), kv[:, SEQ:].reshape(DEPTH, NB, TS, 4, 2, HD)]
    wkv = r["o_wkv"].transpose(0, 3, 2, 1)
    win = r["o_win"].copy()
    win[:, :, PAST - TS:] = wkv[:, SEQ:].reshape(DEPTH, NB, TS, 256)
    out += [wkv[:, None, 0:SEQ].reshape(DEPTH, 1, SEQ, 2, 2, HD), win.reshape(DEPTH, NB, PAST, 2, 2, HD)]
    Cp = r["o_Cp"].reshape(DEPTH, P, 2, 1, 130)
    Cs = r["o_Cs"].reshape(DEPTH, P, 2, NB, 130)
    Sp = r["o_Sp"].reshape(DEPTH, P, 2, 1, P)
    Ss = r["o_Ss"].reshape(DEPTH, P, 2, NB, P)

    def by_head(a, w, n):
        return np.stack([a[:, 64 * (h % 2):64 * (h % 2) + 64, h // 2, :, w * (h % 2):w * (h % 2) + n] for h in range(4)], 1)

    for a in (Cp, Cs):
        c = by_head(a, 65, 65)
        out.append(c[..., 0:64].transpose(0, 3, 1, 4, 2))
    for a in (Cp, Cs):
        out.append(by_head(a, 65, 65)[..., 64].transpose(0, 3, 1, 2))
    m = r["o_m"]
    out += [m[:, :, 3][:, None], m[:, :, 4:12].transpose(0, 2, 1)]
    st = r["o_state"]

    def conv(a, nb):
        return a.reshape(DEPTH, P, 4, nb, 3).transpose(0, 3, 4, 2, 1).reshape(DEPTH, nb, 3, 512)

    out += [conv(st[:, :, OUT_CP:OUT_CS], 1), conv(st[:, :, OUT_CS:OUT_SP], NB)]
    for a in (Sp, Ss):
        out.append(by_head(a, 64, 64).transpose(0, 3, 1, 4, 2))
    back = np.argsort(np.array(rw_columns()))

    def shift(a, nb):
        return a.reshape(DEPTH, P, 8, nb).transpose(0, 3, 2, 1).reshape(DEPTH, nb, D)[:, :, back]

    out += [shift(st[:, :, OUT_SP:OUT_SS], 1), shift(st[:, :, OUT_SS:], NB)]
    return tuple(np.ascontiguousarray(a) for a in out)


def kernel(**inputs):
    import concourse.bacc as _bacc
    from concourse.bass_utils import run_bass_kernel_spmd as _run

    nc = _bacc.Bacc("TRN2", target_bir_lowering=False, num_devices=1, dynamic_dma_scratch_size=2048)
    arrays = pack(inputs)
    A = {}
    for name, a in arrays.items():
        A[name] = nc.dram_tensor("d_" + name, a.shape, mybir.dt.from_np(a.dtype), kind="ExternalInput").ap()
    for name, shape in OUTS.items():
        A[name] = nc.dram_tensor("d_" + name, shape, F32, kind="ExternalOutput").ap()
    build(nc, A)
    r = _run(nc, [{"d_" + k: a for k, a in arrays.items()}], core_ids=[0]).results[0]
    return unpack({k: np.asarray(r["d_" + k]) for k in OUTS})
```

```python
from contextlib import ExitStack

import numpy as np
import concourse.bass as bass
from concourse import mybir

F32 = mybir.dt.float32
F32R = mybir.dt.float32r
I32 = mybir.dt.int32
ALU = mybir.AluOpType
ACT = mybir.ActivationFunctionType
AX = mybir.AxisListType

P = 128
D = 1024
KD = D // P
SEQ = 512
NB = 8
TS = 8
NS_TOK = NB * TS
T = SEQ + NS_TOK
HALF = T // 2
PT = SEQ // P
TILES = [(i * P, P) for i in range(PT)] + [(SEQ, NS_TOK)]
DEPTH = 2
PAST = 512
PAGES = PAST // P
HD = 64
CMP = 31
STRIDE = 16
CLEN = 32
NBLK = 9
FC = 11
NEG = -1e30
SCALE = HD ** -0.5

CQ, CK, CV, CO = 0, 2, 4, 6
CR, CWA, CRK, CRV, CG = 8, 10, 11, 13, 15
CNQ, CCK, CCV, CSK, CSV, CWK, CWV, CGATE = 16, 20, 21, 22, 23, 24, 25, 26
NCH = 27

_v = {}
_n = 0
for _name, _w in (("nmix", 8), ("nffn", 8), ("convw", 16), ("convb", 4), ("mu", 8), ("w0", 2), ("a0", 2),
                  ("kk", 2), ("ka", 2), ("rk", 2), ("lnw", 2), ("lnb", 2), ("mlw", 2), ("gb", 1), ("flag", 1),
                  ("cpos", 32)):
    _v[_name] = _n
    _n += _w
NV = _n
VEC = dict(_v)


def tables():
    c = {}
    i = np.arange(P)
    c["ident"] = np.eye(P)
    c["ones"] = np.ones((P, P))
    c["onesbd"] = (i[:, None] // HD == i[None, :] // HD) * 1.0
    rot = np.zeros((P, P))
    for o in (0, HD):
        for d in range(HD // 2):
            rot[o + d + HD // 2, o + d] = -1.0
            rot[o + d, o + d + HD // 2] = 1.0
    c["rot"] = rot
    pos = np.concatenate([np.arange(SEQ), np.tile(PAST + np.arange(TS), NB)]).astype(np.float32)
    half = HD // 2
    inv = (np.float32(10000.0) ** (-np.arange(half, dtype=np.float32) / np.float32(half))).astype(np.float32)
    ang = (pos[None, :] * inv[:, None]).astype(np.float32)
    c["cos"] = np.tile(np.cos(ang), (4, 1))
    c["sin"] = np.tile(np.sin(ang), (4, 1))
    up = i[:, None] <= i[None, :]
    seg = i[:, None] // TS == i[None, :] // TS
    c["tri"] = np.where(i[None, :] <= i[:, None], 0.0, NEG)
    c["mlp"] = np.where(up, 0.0, NEG)
    c["mls"] = np.where(up & seg, 0.0, NEG)
    st = i[:, None] < i[None, :]
    c["rwp"] = np.concatenate([st, up], 1) * 1.0
    c["rws"] = np.concatenate([(st & seg)[:, :64], (up & seg)[:, :64]], 1) * 1.0
    lev = []
    for k in range(7):
        b = 1 << k
        m = ((i[:, None] // (2 * b) == i[None, :] // (2 * b)) & (i[:, None] // b % 2 == 0)
             & (i[None, :] // b % 2 == 1))
        lev.append(m.T if k else m)
    c["lev"] = np.concatenate(lev, 1) * 1.0
    c["bd"] = np.tile(c["onesbd"], (1, 2))
    b65 = np.repeat(np.arange(2), 65)
    c["bd65"] = np.tile((i[:, None] // HD == b65[None, :]) * 1.0, (1, 2))
    t64 = np.arange(64)
    c["segbt"] = np.tile((np.arange(NB)[:, None] == t64[None, :] // TS).reshape(1, -1), (P, 1)) * 1.0
    c["segsb"] = (i[:, None] // TS == np.arange(NB)[None, :]) * 1.0
    cm = (np.arange(CMP) * STRIDE + CLEN - 1)[None, None, :] <= (np.arange(PT)[None, :, None] * P + i[:, None, None])
    cm = np.concatenate([cm, np.zeros((P, PT, 1), bool)], 2)
    c["cm1"] = cm.reshape(P, -1) * 1.0
    c["cma"] = np.where(cm, 0.0, NEG).reshape(P, -1)
    r = i
    rb, rt = r // 32, r % TS
    col = np.arange(64)
    new = [((col[None, :] // TS == rb[:, None] + 4 * q) & (col[None, :] % TS <= rt[:, None])) for q in range(2)]
    c["newm"] = np.where(np.concatenate(new, 1), 0.0, NEG)
    c["winm"] = np.where(np.arange(8)[None, :] > rt[:, None], 0.0, NEG)
    c["same"] = ((rb[:, None] == rb[None, :]) & (rt[:, None] == rt[None, :])) * 1.0
    cs, ss = np.arange(CMP) * STRIDE, np.arange(NBLK) * HD
    ov = np.clip(np.minimum(cs[:, None] + CLEN, ss[None, :] + HD) - np.maximum(cs[:, None], ss[None, :]), 0, None)
    c["ov"] = ov / CLEN
    c["rowi"] = np.tile((np.arange(4)[None, :, None] == (r // TS % 4)[:, None, None]) * np.ones((1, 1, 3)), (1, 2, 1)).reshape(P, 24)
    c["rank"] = np.tile(np.arange(1, 10)[None, :], (P, 1))
    c["rrank"] = np.tile(np.arange(8, 0, -1)[None, :], (P, 5))
    for j in range(2):
        s = np.zeros((4, P))
        s[2 * j, :HD] = 1.0
        s[2 * j + 1, HD:] = 1.0
        c[f"pair{j}"] = s
    tt = np.arange(T)
    first = (tt % P == 0) | ((tt >= SEQ) & (tt % TS == 0))
    c["reset"] = np.tile(np.where(first, 0.0, 1.0)[None, :], (P, 1))
    c["kill"] = np.tile(np.where((tt >= SEQ) & (tt % TS == 0), NEG, 0.0)[None, :], (4, 1))
    return {k: np.asarray(v, np.float32) for k, v in c.items()}


def table_layout():
    at, col = {}, 0
    for k, v in tables().items():
        at[k] = (col, v.shape[0], v.shape[1])
        col += v.shape[1]
    return at, col


TAB, TAB_W = table_layout()

ST_CONV, ST_SHIFT, ST_W = 0, 4 * NB * 3, 4 * NB * 3 + 8 * NB
OUT_CP, OUT_CS, OUT_SP, OUT_SS = 0, 12, 12 + 96, 12 + 96 + 8
OUT_W = OUT_SS + 64


class Chain:

    def __init__(self, eng, sem):
        self.eng, self.sem, self.n = eng, sem, 0

    def __call__(self, ins, *signals):
        self.n += 1
        ins.then_inc(self.sem, 1)
        self.eng.wait_ge(self.sem, self.n)
        for s in signals:
            self.eng.sem_inc(s, 1)


class Space:

    def __init__(self, buf, start, end):
        self.buf, self.at, self.end = buf, start, end

    def take(self, *dims):
        n = int(np.prod(dims))
        assert self.at + n <= self.end, (self.at, n, self.end)
        v = self.buf[:, self.at:self.at + n]
        self.at += n
        if len(dims) == 2:
            v = v.rearrange("p (a b) -> p a b", b=dims[1])
        elif len(dims) == 3:
            v = v.rearrange("p (a b c) -> p a b c", b=dims[1], c=dims[2])
        elif len(dims) == 4:
            v = v.rearrange("p (a b c d) -> p a b c d", b=dims[1], c=dims[2], d=dims[3])
        return v


def build(nc, A):
    with ExitStack() as ctx:
        sems = {}

        FIRST = ("mix_norm", "proj_", "w_in_", "conv_", "shift_", "f_", "exp_args", "m_rows", "rows_", "m_out", "ml_",
                 "rw_", "hn_")
        SECOND = ("cmp_", "rope_", "at_", "sa_", "cw", "pages_", "qpages_", "qwin", "wo_", "w_out_", "ffn_norm", "rt_")
        shared, used = [], {True: 0, False: 0}

        def S(name):
            if name not in sems:
                part = name.startswith(FIRST)
                if part or name.startswith(SECOND):
                    if used[part] == len(shared):
                        shared.append(ctx.enter_context(nc.semaphore(f"part_{len(shared)}")))
                    sems[name] = shared[used[part]]
                    used[part] += 1
                else:
                    sems[name] = ctx.enter_context(nc.semaphore(name))
            return sems[name]

        def sb(name, cols):
            return ctx.enter_context(nc.sbuf_tensor(name, [P, cols], F32))

        ARENA = 21000
        place, at_ = {}, 2560 // 4
        for name, n_ in (("tab", TAB_W), ("x", KD * T), ("n", KD * T), ("cols", NCH * T), ("small", 1400),
                         ("h", 5 * 2 * 256), ("arena", ARENA), ("page", NB * PAGES)):
            place[name] = at_
            at_ += -(-n_ // 8) * 8

        def put_at(name, n_, at, dt=F32, rows=P):
            return nc.alloc_sbuf_tensor_at(name, [rows, n_], dt, offset=4 * at)

        tab = put_at("tab", TAB_W, place["tab"])
        x_buf = put_at("x_buf", KD * T, place["x"])
        n_buf = put_at("n_buf", KD * T, place["n"])
        cols_buf = put_at("cols_buf", NCH * T, place["cols"])
        small = put_at("small", 1400, place["small"])
        h_buf = put_at("h_buf", 5 * 2 * 256, place["h"])
        arena = put_at("arena", ARENA, place["arena"])
        page_buf = put_at("page_buf", NB * PAGES, place["page"], I32, 1)
        UNIT = FC * P
        XL_AT = ARENA - KD * T
        xh_buf = put_at("xh_buf", KD * T, place["n"], F32R)
        xl_buf = put_at("xl_buf", KD * T, place["arena"] + XL_AT, F32R)
        whl_buf = put_at("whl_buf", 6 * UNIT, place["arena"] + 3 * UNIT, F32R)
        hh_buf = put_at("hh_buf", FC * T, place["cols"], F32R)
        hl_buf = put_at("hl_buf", FC * T, place["cols"] + FC * T, F32R)
        split_buf = put_at("split_buf", 2 * T, place["h"], F32R)
        ps_buf = ctx.enter_context(nc.psum_tensor("ps_buf", [P, 8, 512], F32))

        def tb(name, rows=None, lo=0):
            c, r, w = TAB[name]
            return tab[lo:(rows or r), c:c + w]

        ident = tb("ident")
        x = x_buf[:, :].rearrange("p (k t) -> p k t", t=T)
        hmix = n_buf[:, :].rearrange("p (k t) -> p k t", t=T)
        XH = xh_buf[:, :].rearrange("p (k t) -> p k t", t=T)
        XL = xl_buf[:, :].rearrange("p (k t) -> p k t", t=T)
        HH = hh_buf[:, :].rearrange("p (k t) -> p k t", t=T)
        HL = hl_buf[:, :].rearrange("p (k t) -> p k t", t=T)
        cols = cols_buf[:, :].rearrange("p (k t) -> p k t", t=T)
        HB = h_buf[:, :].rearrange("p (m i c) -> p m i c", m=2, i=5)
        sm = Space(small, 0, 1400)
        vec = sm.take(NV)
        state_in = sm.take(ST_W)
        state_out = sm.take(OUT_W)
        m0_in = sm.take(NB)
        nfin = sm.take(8)
        n64 = sm.take(40)
        n64b = sm.take(40)
        decb = sm.take(2, 12)
        posb = sm.take(4)
        omka = sm.take(2)
        router = sm.take(8, 8)
        prod = sm.take(2, 12)
        midp = sm.take(2, 4)
        gates = sm.take(5, 24)
        sgate = sm.take(2, 2, 3)
        stat = sm.take(4, 4)
        impz = sm.take(4, 9)
        imps = sm.take(4, 9)
        kbias = sm.take(4, 8)
        iw = sm.take(4, 6)
        ifew = sm.take(4)
        csum = sm.take(4)
        sg24 = sm.take(24)
        ups = sm.take(2, 4)
        sums = sm.take(2, 3, 8)
        cmax = sm.take(8)
        wbr = sm.take(8)
        assert sm.at <= 1400

        def V(name, k=0, lo=0, hi=P):
            c = VEC[name] + k
            return vec[lo:hi, c:c + 1]

        def bank(i, n=512, rows=P):
            return ps_buf[0:rows, i, 0:n]

        sync = nc.sync

        hsp = Space(h_buf, 0, 2560)
        rstd = hsp.take(T)
        ntmp = hsp.take(3, T)
        squares = cols_buf[:, 4 * T:(4 + KD) * T].rearrange("p (k t) -> p k t", t=T)
        split_v = split_buf[:, :].rearrange("p (k t) -> p k t", t=T)
        sp1 = Space(arena, 3 * UNIT + 2 * 2 * KD * P, XL_AT)
        qkpad = sp1.take(4, 3 + SEQ + NB * 11)
        rwpad = sp1.take(8, 1 + SEQ + NB * 9)

        def pad_p(pad, c, h, j, n=SEQ):
            return pad[:, c, j:j + n]

        def pad_s(pad, c, h, j, n=TS):
            return pad[:, c, h + SEQ:].rearrange("p (b t) -> p b t", t=h + TS)[:, :, j:j + n]

        sp2 = Space(arena, 0, ARENA)
        R = sp2.take(12, T)
        G = sp2.take(T)
        GT = sp2.take(5, P)
        qs = sp2.take(2, T)
        qmask = sp2.take(NB, NS_TOK)
        v1 = sp2.take(5, 260)
        wk = sp2.take(5, 256)
        DT = sp2.take(512)
        STb = sp2.take(512)
        Cp = sp2.take(260)
        Cs = sp2.take(2, NB, 130)
        vm = sp2.take(NB, 130)
        seg12 = sp2.take(4, 12)
        den = sp2.take(8)

        sp3 = Space(arena, 0, ARENA)
        rw_w = sp3.take(2, 256)
        ra = sp3.take(2, T)
        rcum = sp3.take(2, T)
        rkk = sp3.take(2, T)
        rk2 = sp3.take(2, T)
        e3 = sp3.take(2, T)
        EARLY_B = sp3.at // (PAGES * 4 * HD)
        rg = sp3.take(2, T)
        rcumx = sp3.take(2, T)
        KR = sp3.take(2, 2 * T)
        nbt = sp3.take(2, T)
        kht = sp3.take(2, T)
        tk_flat = sp3.take(5 * 3 * 256)
        TK = tk_flat.rearrange("p (i c) -> p i c", i=5)
        XU = sp3.take(2, 256)
        S0 = sp3.take(256)
        mid = sp3.take(2, 4)
        RW_AT = (0, CR * T)
        M1 = [cols_buf[:, c:c + 1024].rearrange("p (h c) -> p h c", h=4) for c in RW_AT]
        M2 = [cols_buf[:, c + 1024:c + 2048].rearrange("p (h c) -> p h c", h=4) for c in RW_AT]
        Dm = [cols_buf[:, c + 2048:c + 2560] for c in RW_AT]
        Dt = [cols_buf[:, c + 2560:c + 3072] for c in RW_AT]
        S0s = sp3.take(2, NB, P)
        rmask = sp3.take(NB, 64)
        Yb = [sp3.take(512), cols_buf[:, RW_AT[1] + 3072:RW_AT[1] + 3584]]
        kmask = cols_buf[:, 2048:2560].rearrange("p (b t) -> p b t", b=NB)
        umask = cols_buf[:, 0:1024].rearrange("p (b c) -> p b c", b=NB)
        vmask = cols_buf[:, 1024:2048].rearrange("p (b c) -> p b c", b=NB)
        hsq = tk_flat[:, 0:1280].rearrange("p (g d) -> p g d", d=HD)

        def kr(j, i, which, n, lo=0, hi=P):
            o = 2 * TILES[i][0] + which * n
            return KR[lo:hi, j, o:o + n]

        sp4 = Space(arena, 0, ARENA)
        ckb = sp4.take(9 * PAGES + 1, 2, 2, HD)
        cw1 = sp4.take(2, CLEN // 2, P)
        hid = sp4.take(4, 9 * CMP)
        ckT = sp4.take(9 * CMP + 1)
        cvt = sp4.take(8, 2, HD)
        cvbd = sp4.take(2, 4 * HD)
        cw2 = sp4.take(2, HD)
        qrs = sp4.take(2, NB * 32)
        svt = sp4.take(5, P)
        wvt = sp4.take(5, P)
        osamp = sp4.take(2, P)
        after_cmp = Space(arena, sp4.at, ARENA)
        rtmp = sp4.take(T)
        rtmp2 = sp4.take(2 * P)
        sp5 = Space(arena, 0, 9 * 1024 + 256 + 4096 + 4 * 9 * CMP)
        lo_c = Space(cols_buf, 4 * T, CNQ * T)
        skq = [sp5.take(4, 512), lo_c.take(4, 512)]
        wkq = [sp5.take(4, 512), lo_c.take(4, 512)]
        svq = [sp5.take(4, PAGES, P), lo_c.take(4, PAGES, P)]
        wvq = [sp5.take(4, 4, P), after_cmp.take(4, 4, P)]
        Sb = sp5.take(3, T)
        PTb = sp5.take(3, 5, P)
        obr = sp5.take(8, HD)
        oacc = sp5.take(4, 4, P)
        Cb = oacc[:, 0, 0, :].rearrange("p (m k) -> p m k", m=4)
        PTc = oacc[:, 1, :, :]
        qrot = Space(cols_buf, 0, 4 * T).take(4, T)
        sp6 = Space(arena, 9 * UNIT, XL_AT)
        sg = sp6.take(2, T)
        combE = sp6.take(T)
        cTe = sp6.take(T)
        cT = sp6.take(T)
        lg = sp6.take(5, 8)
        lgT = cTe
        lw = sp6.take(8, 40)
        htmp = Space(cols_buf, 2 * FC * T, NCH * T).take(2, T)

        def raw(slot, nk):
            return arena[:, slot * UNIT:slot * UNIT + nk * P]

        def part(slot, which, nk, size=UNIT):
            a = (2 * slot + which) * size
            return whl_buf[:, a:a + nk * P]

        def split_hi(a, slot, src, nk, size, *sig):
            a(nc.scalar.copy(part(slot, 0, nk, size), src), *sig)

        def split_lo(g, slot, src, nk, size, *sig):
            g(nc.gpsimd.tensor_tensor(part(slot, 1, nk, size), src, part(slot, 0, nk, size).bitcast(F32),
                                      ALU.subtract), *sig)

        def two(b, rows=P):
            return ps_buf[0:rows, b:b + 2, 0:HALF]

        def halves(v):
            return v.rearrange("p (a t) -> p a t", a=2)

        def wide(b, w, m, start=True, stop=True, rows=P):
            for a_ in range(2):
                last = nc.tensor.matmul(ps_buf[0:rows, b + a_, 0:HALF], w, m[:, a_ * HALF:(a_ + 1) * HALF],
                                        start=start, stop=stop)
            return last

        def unit_products(slot, nk, size, xh, xl, b, before=None):
            wh = part(slot, 0, nk, size).rearrange("p (k c) -> p k c", c=P)
            wl = part(slot, 1, nk, size).rearrange("p (k c) -> p k c", c=P)
            for k in range(nk):
                if before:
                    before(k)
                for n_, (w, m) in enumerate(((wh, xh), (wh, xl), (wl, xh))):
                    f_, l_ = k == 0 and n_ == 0, k == nk - 1 and n_ == 2
                    last = wide(b, w[:, k, :], m[:, k, :], f_, l_)
            return last

        meets = {"pe": 0, "act": 0, "dve": 0}

        def meet(eng, who):
            eng.drain().then_inc(S("phase_ended"), 1)
            meets[who] += 1
            eng.wait_ge(S("phase_ended"), 3 * meets[who])

        def norm_act(a, tag, rs, final=False):
            ac = nc.scalar
            for k in range(KD):
                if tag == "ffn_norm":
                    ac.wait_ge(S("wo_out"), k + 1)
                a(ac.activation(squares[:, k, :], x[:, k, :], ACT.Square), S(tag + "_squares"))
            if tag == "mix_norm":
                for c in range(2):
                    proj_hi(a, c)
            ac.wait_ge(S(tag + "_mean"), 1)
            a(ac.activation(rs, rs, ACT.Sqrt), S(tag + "_root"))
            if not final:
                for k in range(KD):
                    ac.wait_ge(S(tag + "_scaled"), k + 1)
                    a(ac.copy(XH[:, k, :], ntmp[:, k % 3, :]), S(tag + "_hi"))

        def norm_pe(tag):
            for k in range(KD):
                nc.tensor.wait_ge(S(tag + "_squares"), k + 1)
                last = wide(6, tb("ones"), squares[:, k, :], k == 0, k == KD - 1)
            last.then_inc(S(tag + "_sum"), 1)

        def norm_dve(v, tag, rs, w, final=False):
            ve = nc.vector
            ve.wait_ge(S(tag + "_sum"), 1)
            v(ve.tensor_scalar(halves(rs), two(6), 1.0 / D, 1e-6, ALU.mult, ALU.add), S(tag + "_mean"))
            ve.wait_ge(S(tag + "_root"), 1)
            v(ve.reciprocal(rs, rs))
            for k in range(KD + 1):
                if k < KD:
                    dst = hmix[:, k, :] if final else ntmp[:, k % 3, :]
                    if tag == "ffn_norm" and k >= 3:
                        ve.wait_ge(S("rt_rows"), k - 2)
                    v(ve.scalar_tensor_tensor(dst, x[:, k, :], w(k), rs, ALU.mult, ALU.mult),
                      S(tag + ("_done" if final else "_scaled")))
                if k and not final:
                    ve.wait_ge(S(tag + "_hi"), k)
                    v(ve.tensor_tensor(XL[:, k - 1, :], ntmp[:, (k - 1) % 3, :], XH[:, k - 1, :].bitcast(F32), ALU.subtract),
                      S(tag + "_done"))

        def proj_sp(l):
            for c in range(NCH):
                if c >= 3:
                    sync.wait_ge(S("proj_split"), c - 2)
                sync.dma_start(raw(c % 3, KD), A["w_in"][l * NCH + c].rearrange("p k c -> p (k c)"))\
                    .then_inc(S(f"w_in_{c % 3}"), 16)

        def proj_hi(a, c):
            nc.scalar.wait_ge(S(f"w_in_{c % 3}"), 16 * (c // 3 + 1))
            if c >= 2:
                nc.scalar.wait_ge(S("proj_done"), c - 1)
            split_hi(a, c % 2, raw(c % 3, KD), KD, KD * P, S("proj_hi"))

        def proj_pool(g):
            for c in range(NCH):
                nc.gpsimd.wait_ge(S("proj_hi"), c + 1)
                split_lo(g, c % 2, raw(c % 3, KD), KD, KD * P, S("proj_split"))

        def proj_pe():
            for c in range(NCH):
                nc.tensor.wait_ge(S("proj_split"), c + 1)
                if c >= 3:
                    nc.tensor.wait_ge(S("proj_out"), c - 2)
                b = 2 + 2 * (c % 3)
                unit_products(c % 2, KD, KD * P, XH, XL, b,
                              (lambda k: nc.tensor.wait_ge(S("mix_norm_done"), k + 1)) if c == 0 else None)\
                    .then_inc(S("proj_done"), 1)

        def proj_act(a):
            for c in range(NCH):
                nc.scalar.wait_ge(S("proj_done"), c + 1)
                if c + 2 < NCH:
                    proj_hi(a, c + 2)
                b = 2 + 2 * (c % 3)
                rest = SEQ - HALF
                s64 = ps_buf[:, b + 1, rest:HALF].rearrange("p (b t) -> p b t", t=TS)
                if c < 4 or 8 <= c < 16:
                    pad, k, h = (qkpad, c, 3) if c < 4 else (rwpad, c - 8, 1)
                    a(nc.scalar.copy(pad[:, k, h:h + HALF], bank(b, HALF)))
                    a(nc.scalar.copy(pad[:, k, h + HALF:h + SEQ], bank(b + 1, rest)))
                    a(nc.scalar.copy(pad_s(pad, k, h, h), s64), S("proj_out"))
                elif c == CGATE:
                    a(nc.scalar.activation(halves(cols[:, c, :]), two(b), ACT.Identity, bias=V("gb")), S("proj_out"))
                elif CNQ <= c < CNQ + 4:
                    a(nc.scalar.mul(halves(cols[:, c, :]), two(b), SCALE), S("proj_out"))
                else:
                    a(nc.scalar.copy(halves(cols[:, c, :]), two(b)), S("proj_out"))
            nc.scalar.wait_ge(S("conv_done"), 4)
            for c in range(4):
                a(nc.scalar.activation(cols[:, c, :], cols[:, c, :], ACT.Silu))
                if c >= 2:
                    a(nc.scalar.mul(cols[:, c, :], cols[:, c, :], SCALE))

        def proj_dve(v):
            ve = nc.vector
            v(ve.memset(qkpad[:, :, 0:3], 0.0))
            v(ve.memset(rwpad[:, :, 0:1], 0.0))
            for c in range(4):
                v(ve.tensor_copy(pad_s(qkpad, c, 3, 0, 3),
                                 state_in[:, ST_CONV + 24 * c:ST_CONV + 24 * c + 24].rearrange("p (b j) -> p b j", j=3)))
            for c in range(8):
                v(ve.tensor_copy(pad_s(rwpad, c, 1, 0, 1),
                                 state_in[:, ST_SHIFT + 8 * c:ST_SHIFT + 8 * c + 8].rearrange("p (b j) -> p b j", j=1)))

            def both(c):
                yield cols[:, c, 0:SEQ], pad_p
                yield cols[:, c, SEQ:T].rearrange("p (b t) -> p b t", t=TS), pad_s

            for c in range(4):
                ve.wait_ge(S("proj_out"), c + 1)
                for y, pad in both(c):
                    n = SEQ if pad is pad_p else TS
                    v(ve.tensor_scalar(y, pad(qkpad, c, 3, 0, n), V("convw", c), V("convb", c), ALU.mult, ALU.add))
                    for j in range(1, 4):
                        v(ve.scalar_tensor_tensor(y, pad(qkpad, c, 3, j, n), V("convw", 4 * j + c), y, ALU.mult, ALU.add))
                v(ve.tensor_copy(state_out[:, OUT_CP + 3 * c:OUT_CP + 3 * c + 3], qkpad[:, c, SEQ:SEQ + 3]))
                v(ve.tensor_copy(state_out[:, OUT_CS + 24 * c:OUT_CS + 24 * c + 24].rearrange("p (b j) -> p b j", j=3),
                                 pad_s(qkpad, c, 3, TS, 3)), S("conv_done"))
            for c in range(8):
                ve.wait_ge(S("proj_out"), 8 + c + 1)
                for y, pad in both(8 + c):
                    n = SEQ if pad is pad_p else TS
                    now = pad(rwpad, c, 1, 1, n)
                    v(ve.tensor_tensor(y, pad(rwpad, c, 1, 0, n), now, ALU.subtract))
                    v(ve.scalar_tensor_tensor(y, y, V("mu", c), now, ALU.mult, ALU.add))
                v(ve.tensor_copy(state_out[:, OUT_SP + c:OUT_SP + c + 1], rwpad[:, c, SEQ:SEQ + 1]))
                v(ve.tensor_copy(state_out[:, OUT_SS + 8 * c:OUT_SS + 8 * c + 8].rearrange("p (b j) -> p b j", j=1),
                                 pad_s(rwpad, c, 1, TS, 1)), S("shift_done"))

        def onehot(h, n):
            return ident[0:4, h:h + 1].to_broadcast([4, n])

        def pairsel(j):
            return tb(f"pair{j}")

        RF, RL, RB, RM, RP, RU, RI, RD1, RD0, RT = range(10)

        def rows_dve(v):
            ve = nc.vector

            def r(k, a=0, b=T, s=1):
                return R[0:4, k, a:b:s] if s > 1 else R[0:4, k, a:b]

            def seg(k):
                return R[0:4, k, SEQ:T].rearrange("p (b t) -> p b t", t=TS)

            def til(k, a=0, b=SEQ):
                return R[0:4, k, a:b].rearrange("p (c t) -> p c t", t=P)

            ig = cols[0:4, CGATE, :]
            v(ve.memset(G, 0.0))
            v(ve.memset(seg12, 0.0), S("rows_start"))
            v(ve.tensor_copy(r(RF), cols[32:36, CGATE, :]))
            v(ve.scalar_tensor_tensor(r(RT), r(RF), -1.0, r(RF), ALU.mult, ALU.max), S("f_abs"))
            ve.wait_ge(S("f_exp"), 1)
            v(ve.tensor_scalar(r(RL), r(RL), 1.0, None, ALU.add), S("f_one"))
            ve.wait_ge(S("f_ln"), 1)
            v(ve.scalar_tensor_tensor(r(RL), r(RF), 0.0, r(RL), ALU.min, ALU.subtract))
            v(ve.tensor_tensor_scan(r(RB), tb("reset", 4), r(RL), 0.0, ALU.mult, ALU.add))
            v(ve.tensor_copy(r(RD1), ig))
            v(ve.tensor_tensor(seg12[0:4, 3, 0:8], R[0:4, RL, SEQ:T:TS], m0_in[0:4, :], ALU.add))
            v(ve.tensor_tensor(R[0:4, RD1, SEQ:T:TS], R[0:4, RD1, SEQ:T:TS], seg12[0:4, 3, 0:8], ALU.max))
            v(ve.tensor_tensor(r(RD0), r(RL), tb("kill", 4), ALU.add))
            v(ve.tensor_tensor_scan(r(RM), r(RD0), r(RD1), 0.0, ALU.add, ALU.max), S("m_rows"))
            v(ve.memset(r(RP, 0, P), 0.0))
            v(ve.tensor_copy(til(RP, P, SEQ), R[0:4, RM, P - 1:SEQ - P:P].unsqueeze(2).to_broadcast([4, PT - 1, P])))
            v(ve.tensor_copy(seg(RP), m0_in[0:4, :].unsqueeze(2).to_broadcast([4, NB, TS])))
            v(ve.tensor_tensor(r(RU), r(RB), r(RM), ALU.subtract))
            v(ve.tensor_tensor(r(RI), r(RU), r(RP), ALU.add))
            v(ve.tensor_tensor(G[0:4, :], ig, r(RB), ALU.subtract))
            v(ve.tensor_copy(seg12[0:4, 0, 0:4], R[0:4, RU, P - 1:SEQ:P]))
            v(ve.tensor_copy(seg12[0:4, 0, 4:12], R[0:4, RU, SEQ + TS - 1:T:TS]))
            v(ve.tensor_tensor(seg12[0:4, 1, 0:4], seg12[0:4, 0, 0:4], R[0:4, RP, 0:SEQ:P], ALU.add))
            v(ve.tensor_tensor(seg12[0:4, 1, 4:12], seg12[0:4, 0, 4:12], m0_in[0:4, :], ALU.add))
            v(ve.tensor_tensor(til(RT), G[0:4, 0:SEQ].rearrange("p (c t) -> p c t", t=P),
                               seg12[0:4, 0, 0:4].unsqueeze(2).to_broadcast([4, 4, P]), ALU.add))
            v(ve.tensor_tensor(seg(RT), G[0:4, SEQ:T].rearrange("p (b t) -> p b t", t=TS),
                               seg12[0:4, 0, 4:12].unsqueeze(2).to_broadcast([4, NB, TS]), ALU.add), S("exp_args"))
            v(ve.tensor_copy(seg12[0:4, 2, 0:4], R[0:4, RM, P - 1:SEQ:P]))
            v(ve.tensor_copy(seg12[0:4, 2, 4:12], R[0:4, RM, SEQ + TS - 1:T:TS]), S("m_out"))

        def rows_act(a):
            ac = nc.scalar
            ac.wait_ge(S("rows_start"), 1)
            a(ac.activation(G[96:120, :], cols[64:88, CGATE, :], ACT.Sigmoid))
            ac.wait_ge(S("f_abs"), 1)
            a(ac.activation(R[0:4, RL, :], R[0:4, RT, :], ACT.Exp, scale=-1.0), S("f_exp"))
            ac.wait_ge(S("f_one"), 1)
            a(ac.activation(R[0:4, RL, :], R[0:4, RL, :], ACT.Ln), S("f_ln"))
            ac.wait_ge(S("ml_clear"), 1)
            for i, (t0, n) in enumerate(TILES):
                ac.wait_ge(S("ml_kv"), i + 1)
                a(ac.copy(wk[0:n, i, :], ps_buf[0:n, KV_BANK[i], 0:256]))
                a(ac.copy(v1[0:n, i, :].rearrange("p (h d) -> p h d", h=4)[:, :, 0:HD],
                          ps_buf[0:n, KV_BANK[i], 256:512].rearrange("p (h d) -> p h d", h=4)), S("ml_kv_out"))
            ac.wait_ge(S("exp_args"), 1)
            a(ac.activation(G[64:68, :], R[0:4, RM, :], ACT.Exp, scale=-1.0))
            a(ac.activation(R[0:4, RI, :], R[0:4, RI, :], ACT.Exp))
            a(ac.activation(seg12[0:4, 1, :], seg12[0:4, 1, :], ACT.Exp))
            a(ac.activation(G[32:36, :], R[0:4, RT, :], ACT.Exp), S("rows_done"))

        KV_BANK = (2, 3, 4, 5, 7)

        def ml_pool(g):
            nc.gpsimd.wait_ge(S("phase_ended"), 3)
            g(nc.gpsimd.memset(v1, 1.0))
            g(nc.gpsimd.memset(Cp, 0.0))
            g(nc.gpsimd.memset(h_buf[:, :], 0.0), S("ml_clear"))

        def ml_pe():
            pe = nc.tensor
            for i, (t0, n) in enumerate(TILES):
                for c in range(4):
                    last = pe.transpose(ps_buf[0:n, KV_BANK[i], c * P:c * P + P], cols[:, CK + c, t0:t0 + n], ident)
                last.then_inc(S("ml_kv"), 1)
            pe.wait_ge(S("rows_done"), 1)
            for i, (t0, n) in enumerate(TILES):
                last = pe.transpose(ps_buf[0:n, i // 4, (i % 4) * P:(i % 4) * P + P], G[:, t0:t0 + n], ident)
            last.then_inc(S("ml_cols"), 1)
            pe.wait_ge(S("ml_kv_out"), 5)
            for j in range(2):
                wide(2 + 2 * j, pairsel(j), R[0:4, RI, :])
                last = pe.matmul(ps_buf[:, 6, 12 * j:12 * j + 12], pairsel(j), seg12[0:4, 1, :], start=True, stop=True)
            last.then_inc(S("ml_spread"), 1)
            for i, (t0, n) in enumerate(TILES):
                mask = tb("mlp" if n == P else "mls", n)[:, 0:n]
                if i == 0:
                    pe.wait_ge(S("ml_spread_out"), 1)
                for h in range(4):
                    o = ps_buf[0:n, 0, h * n:h * n + n]
                    pe.matmul(o, onehot(h, n), R[0:4, RU, t0:t0 + n], start=True, stop=False)
                    last = pe.matmul(o, ident[0:n, 0:n], mask, start=False, stop=True)
                last.then_inc(S("ml_logd"), 1)
                for h in range(4):
                    j, f = h // 2, h % 2
                    last = pe.matmul(ps_buf[0:n, 1 + f, j * n:j * n + n], cols[64 * f:64 * f + 64, CK + j, t0:t0 + n],
                                     cols[64 * f:64 * f + 64, CQ + j, t0:t0 + n], start=True, stop=True)
                last.then_inc(S("ml_kq"), 1)
                if i == 4:
                    pe.wait_ge(S("ml_state_in"), 32)
                    pe.wait_ge(S("ml_h"), 4)
                else:
                    pe.wait_ge(S("ml_state"), i + 1)
                for j in range(2):
                    o = ps_buf[0:n, 3, j * 130:j * 130 + 130]
                    if i < 4:
                        pe.matmul(o, qs[:, j, t0:t0 + n], Cp[:, j * 130:j * 130 + 130], start=True, stop=False)
                    else:
                        pe.wait_ge(S("ml_qmask"), j + 1)
                        for b in range(NB):
                            last = pe.matmul(o, qmask[:, b, :], Cs[:, j, b, :], start=b == 0, stop=False)
                        last.then_inc(S("ml_qmask_used"), 1)
                    if j == 0:
                        pe.wait_ge(S("ml_S"), i + 1)
                    for f in range(2):
                        last = pe.matmul(ps_buf[0:n, 3, j * 130 + 65 * f:j * 130 + 65 * f + 65],
                                         STb[0:n, (2 * f + j) * n:(2 * f + j) * n + n],
                                         v1[0:n, i, (2 * j + f) * 65:(2 * j + f) * 65 + 65], start=False, stop=f == 1)
                last.then_inc(S("ml_num"), 1)
                if i < 4:
                    for j in range(2):
                        last = pe.matmul(ps_buf[:, 4, j * 130:j * 130 + 130], wk[:, i, 128 * j:128 * j + 128],
                                         v1[:, i, 130 * j:130 * j + 130], start=True, stop=True)
                    last.then_inc(S("ml_add"), 1)
                else:
                    for j in range(2):
                        pe.wait_ge(S("ml_vm"), j + 1)
                        for g in range(3):
                            nb = min(3, NB - 3 * g)
                            last = pe.matmul(ps_buf[:, 4 + g, 0:nb * 130], wk[0:64, 4, 128 * j:128 * j + 128],
                                             vm[0:64, 3 * g:3 * g + nb, :], start=True, stop=True)
                        last.then_inc(S("ml_add"), 1)

        def ml_act(a):
            ac = nc.scalar
            for i, (t0, n) in enumerate(TILES):
                ac.wait_ge(S("ml_logd"), i + 1)
                ac.wait_ge(S("ml_spread_out"), 1)
                for h in range(4):
                    idx = (h % 2) * 2 + h // 2
                    a(ac.activation(DT[0:n, idx * n:idx * n + n], ps_buf[0:n, 0, h * n:h * n + n], ACT.Exp,
                                    bias=GT[0:n, i, h:h + 1]))
                ac.sem_inc(S("ml_D"), 1)
                if i < 4:
                    ac.wait_ge(S("ml_S"), i + 1)

        def ml_dve(v):
            ve = nc.vector
            ve.wait_ge(S("ml_clear"), 1)
            ve.sem_inc(S("ml_state"), 1)
            ve.wait_ge(S("ml_cols"), 1)
            v(ve.tensor_copy(GT[:, 0:4, :], bank(0).rearrange("p (i c) -> p i c", c=P)))
            v(ve.tensor_copy(GT[0:64, 4, :], ps_buf[0:64, 1, 0:P]))
            v(ve.tensor_copy(gates[:, 0:4, :], GT[:, 0:4, 96:120]))
            ve.wait_ge(S("ml_spread"), 1)
            for j in range(2):
                v(ve.tensor_tensor(halves(qs[:, j, :]), halves(cols[:, CQ + j, :]), two(2 + 2 * j), ALU.mult))
            v(ve.tensor_copy(decb, ps_buf[:, 6, 0:24].rearrange("p (j c) -> p j c", j=2)), S("ml_spread_out"))
            ve.wait_ge(S("ml_kv_out"), 5)
            for i, (t0, n) in enumerate(TILES):
                rows_k = wk[0:n, i, :].rearrange("p (h d) -> p h d", h=4)
                v(ve.tensor_tensor(rows_k, rows_k, GT[0:n, i, 32:36].unsqueeze(2).to_broadcast([n, 4, HD]), ALU.mult))
                if i == 4:
                    v(ve.tensor_tensor(qmask, qs[:, 0, SEQ:T].unsqueeze(1).to_broadcast([P, NB, NS_TOK]),
                                       tb("segbt").rearrange("p (b t) -> p b t", b=NB), ALU.mult), S("ml_qmask"))
                ve.wait_ge(S("ml_kq"), i + 1)
                ve.wait_ge(S("ml_D"), i + 1)
                for f in range(2):
                    v(ve.tensor_tensor(STb[0:n, 2 * f * n:2 * f * n + 2 * n], ps_buf[0:n, 1 + f, 0:2 * n],
                                       DT[0:n, 2 * f * n:2 * f * n + 2 * n], ALU.mult), *([S("ml_S")] if f else []))
                if i == 4:
                    ve.wait_ge(S("ml_qmask_used"), 1)
                    v(ve.tensor_tensor(qmask, qs[:, 1, SEQ:T].unsqueeze(1).to_broadcast([P, NB, NS_TOK]),
                                       tb("segbt").rearrange("p (b t) -> p b t", b=NB), ALU.mult), S("ml_qmask"))
                ve.wait_ge(S("ml_num"), i + 1)
                num = ps_buf[0:n, 3, 0:260].rearrange("p (h d) -> p h d", h=4)
                v(ve.tensor_copy(den[0:n, 4:8], num[:, :, HD]))
                v(ve.scalar_tensor_tensor(den[0:n, 0:4], den[0:n, 4:8], -1.0, den[0:n, 4:8], ALU.mult, ALU.max))
                v(ve.tensor_tensor(den[0:n, 0:4], den[0:n, 0:4], GT[0:n, i, 64:68], ALU.max))
                v(ve.reciprocal(den[0:n, 4:8], den[0:n, 0:4]))
                v(ve.tensor_tensor(HB[0:n, 0, i, :].rearrange("p (h d) -> p h d", h=4), num[:, :, 0:HD],
                                   den[0:n, 4:8].unsqueeze(2).to_broadcast([n, 4, HD]), ALU.mult))
                if i < 4:
                    ve.wait_ge(S("ml_add"), i + 1)
                    for j in range(2):
                        c = Cp[:, 130 * j:130 * j + 130]
                        v(ve.scalar_tensor_tensor(c, c, decb[:, j, i:i + 1], ps_buf[:, 4, 130 * j:130 * j + 130],
                                                  ALU.mult, ALU.add))
                    v(ve.tensor_tensor(Cp, Cp, tb("bd65"), ALU.mult), S("ml_state"), S("ml_h"))
                else:
                    for j in range(2):
                        v(ve.tensor_tensor(vm[0:64], v1[0:64, 4, 130 * j:130 * j + 130].unsqueeze(1).to_broadcast([64, NB, 130]),
                                           tb("segsb", 64).unsqueeze(2).to_broadcast([64, NB, 130]), ALU.mult), S("ml_vm"))
                        ve.wait_ge(S("ml_add"), 5 + j)
                        v(ve.tensor_tensor(Cs[:, j], Cs[:, j], decb[:, j, 4:12].unsqueeze(2).to_broadcast([P, NB, 130]), ALU.mult))
                        for g in range(3):
                            nb = min(3, NB - 3 * g)
                            v(ve.tensor_tensor(Cs[:, j, 3 * g:3 * g + nb, :], Cs[:, j, 3 * g:3 * g + nb, :],
                                               ps_buf[:, 4 + g, 0:nb * 130].rearrange("p (b c) -> p b c", b=nb), ALU.add))
                    ve.sem_inc(S("ml_final"), 1)

        def rwprep_pe():
            pe = nc.tensor
            pe.wait_ge(S("rw_kk_sq"), 1)
            for j in range(2):
                last = wide(2 * j, tb("onesbd"), e3[:, j, :])
            last.then_inc(S("rw_kk_sum"), 1)
            pe.wait_ge(S("rw_w_in"), 32)
            pe.wait_ge(S("rw_lora_in"), 1)
            for j in range(2):
                last = wide(4 + 2 * j, rw_w[0:64, 0, P * j:P * j + P], cols[0:64, CWA, :])
            last.then_inc(S("rw_w_pre"), 1)
            pe.wait_ge(S("rw_kk_len"), 1)
            for j in range(2):
                last = wide(2 * j, rw_w[64:128, 0, P * j:P * j + P], cols[64:128, CWA, :])
            last.then_inc(S("rw_a_pre"), 1)
            pe.wait_ge(S("rw_decay"), 1)
            for j in range(2):
                last = wide(4 + 2 * j, rw_w[:, 1, P * j:P * j + P], cols[:, CG, :])
            last.then_inc(S("rw_g"), 1)
            pe.wait_ge(S("rw_rk"), 1)
            for j in range(2):
                last = wide(2 * j, tb("onesbd"), Yb2[:, j, :])
            last.then_inc(S("rw_rk_sum"), 1)
            pe.wait_ge(S("rw_ready"), 1)
            for i, (t0, n) in enumerate(TILES):
                if i >= 2:
                    pe.wait_ge(S("rw_rows_out"), i - 1)
                b = 6 - 2 * (i % 2)
                for j in range(2):
                    pe.transpose(ps_buf[0:n, b, P * j:P * j + P], nbt[:, j, t0:t0 + n], ident)
                    pe.transpose(ps_buf[0:n, b, 256 + P * j:256 + P * j + P], kht[:, j, t0:t0 + n], ident)
                    last = pe.transpose(ps_buf[0:n, b + 1, P * j:P * j + P], cols[:, CRV + j, t0:t0 + n], ident)
                last.then_inc(S("rw_rows"), 1)

        def rwprep_act(a):
            ac = nc.scalar
            a(ac.activation(cols[0:64, CWA, :], cols[0:64, CWA, :], ACT.Tanh), S("rw_lora_in"))
            a(ac.activation(cols[:, CG, :], cols[:, CG, :], ACT.Sigmoid))
            ac.wait_ge(S("rw_kk_sum"), 1)
            for j in range(2):
                a(ac.activation(halves(e3[:, j, :]), two(2 * j), ACT.Sqrt))
            ac.sem_inc(S("rw_kk_len"), 1)
            hn_act(a, 0)
            ac.wait_ge(S("rw_w_pre"), 1)
            for j in range(2):
                a(ac.activation(halves(rcumx[:, j, :]), two(4 + 2 * j), ACT.Sigmoid, bias=V("w0", j)),
                  *([S("rw_decay")] if j else []))
            ac.wait_ge(S("rw_a_pre"), 1)
            for j in range(2):
                a(ac.activation(halves(ra[:, j, :]), two(2 * j), ACT.Sigmoid, bias=V("a0", j)),
                  *([S("rw_a")] if j else []))
            ac.wait_ge(S("rw_g"), 1)
            for j in range(2):
                a(ac.copy(halves(rg[:, j, :]), two(4 + 2 * j)))
            ac.sem_inc(S("rw_g_out"), 1)
            for c in range(2):
                a(ac.activation(cols[:, CO + c, :], cols[:, CO + c, :], ACT.Sigmoid))
            ac.wait_ge(S("rw_cum"), 1)
            a(ac.activation(midp, mid, ACT.Exp))
            a(ac.activation(rcumx, rcumx, ACT.Exp), S("rw_e1"))
            a(ac.activation(e3, rcum, ACT.Exp, scale=-1.0), S("rw_e3"))
            a(ac.activation(rcum, rcum, ACT.Exp), S("rw_e2"))

        Yb2 = rkk

        def rwprep_dve(v):
            ve = nc.vector
            for j in range(2):
                v(ve.tensor_scalar(rkk[:, j, :], cols[:, CRK + j, :], V("kk", j), None, ALU.mult))
                v(ve.tensor_tensor(e3[:, j, :], rkk[:, j, :], rkk[:, j, :], ALU.mult), *([S("rw_kk_sq")] if j else []))
            v(ve.tensor_scalar(omka, vec[:, VEC["ka"]:VEC["ka"] + 2], -1.0, 1.0, ALU.mult, ALU.add))
            ve.wait_ge(S("ml_outs"), 48)
            head_norm_var(v, 0)
            ve.wait_ge(S("rw_kk_len"), 1)
            v(ve.tensor_scalar(e3, e3, 1e-12, None, ALU.max))
            v(ve.reciprocal(e3, e3))
            v(ve.tensor_tensor(nbt, rkk, e3, ALU.mult))
            ve.wait_ge(S("rw_a"), 1)
            for j in range(2):
                v(ve.tensor_scalar(rk2[:, j, :], ra[:, j, :], V("ka", j), omka[:, j:j + 1], ALU.mult, ALU.add))
                v(ve.tensor_tensor(rk2[:, j, :], rk2[:, j, :], cols[:, CRK + j, :], ALU.mult))
            for j in range(2):
                v(ve.scalar_tensor_tensor(Yb2[:, j, :], cols[:, CR + j, :], V("rk", j), rk2[:, j, :], ALU.mult, ALU.mult),
                  *([S("rw_rk")] if j else []))
            v(ve.tensor_scalar(kht, rcumx, -float(np.exp(-0.5)), None, ALU.mult))
            ve.wait_ge(S("rw_g_out"), 1)
            for j in range(2):
                v(ve.tensor_tensor_scan(rcum[:, j, :], tb("reset"), kht[:, j, :], 0.0, ALU.mult, ALU.add))
            v(ve.tensor_tensor(rcumx, rcum, kht, ALU.subtract))
            for j in range(2):
                v(ve.tensor_copy(mid[:, j, :], rcum[:, j, P // 2 - 1:SEQ:P]))
            for buf in (rcum, rcumx):
                for j in range(2):
                    w = buf[:, j, 0:SEQ].rearrange("p (c t) -> p c t", t=P)
                    v(ve.tensor_tensor(w, w, mid[:, j, :].unsqueeze(2).to_broadcast([P, PT, P]), ALU.subtract))
            ve.sem_inc(S("rw_cum"), 1)
            ve.wait_ge(S("rw_rk_sum"), 1)
            ve.wait_ge(S("rw_e3"), 1)

            def krv(j, which):
                yield KR[:, j, 0:2 * SEQ].rearrange("p (i w t) -> p i w t", w=2, t=P)[:, :, which, :], 0, SEQ
                yield KR[:, j, 2 * SEQ + which * 64:2 * SEQ + which * 64 + 64].rearrange("p (i t) -> p i t", i=1), SEQ, T

            for j in range(2):
                for dst, a0, b0 in krv(j, 0):
                    n = min(P, b0 - a0)
                    v(ve.tensor_tensor(dst, nbt[:, j, a0:b0].rearrange("p (i t) -> p i t", t=n),
                                       rcumx[:, j, a0:b0].rearrange("p (i t) -> p i t", t=n), ALU.mult))
                v(ve.tensor_tensor(halves(rcumx[:, j, :]), halves(cols[:, CRV + j, :]), two(2 * j), ALU.mult))
            v(ve.scalar_tensor_tensor(nbt, nbt, -1.0, ra, ALU.mult, ALU.mult))
            v(ve.tensor_tensor(nbt, nbt, e3, ALU.mult))
            v(ve.tensor_tensor(kht, rk2, e3, ALU.mult))
            ve.wait_ge(S("rw_e2"), 1)
            for j in range(2):
                for dst, a0, b0 in krv(j, 1):
                    n = min(P, b0 - a0)
                    v(ve.tensor_tensor(dst, cols[:, CR + j, a0:b0].rearrange("p (i t) -> p i t", t=n),
                                       rcum[:, j, a0:b0].rearrange("p (i t) -> p i t", t=n), ALU.mult))
                v(ve.tensor_copy(prod[:, j, 0:4], rcum[:, j, P - 1:SEQ:P]))
                v(ve.tensor_copy(prod[:, j, 4:12], rcum[:, j, SEQ + TS - 1:T:TS]))
            v(ve.tensor_copy(ups, prod[:, :, 0:4]))
            v(ve.tensor_tensor(ups[:, :, 0:3], ups[:, :, 0:3], midp[:, :, 1:4], ALU.mult), S("rw_ready"))
            head_norm_scale(v, 0)
            for i, (t0, n) in enumerate(TILES):
                ve.wait_ge(S("rw_rows"), i + 1)
                b = 6 - 2 * (i % 2)
                v(ve.tensor_copy(TK[0:n, i, 0:512], ps_buf[0:n, b, 0:512]))
                v(ve.tensor_copy(TK[0:n, i, 512:768], ps_buf[0:n, b + 1, 0:256]), S("rw_rows_out"))

        def levels(i):
            return 7 if i < 4 else 3

        RW_GROUPS = [(0, 1), (2, 3), (4,)]

        def rw_pe():
            pe = nc.tensor
            rounds = [0, 0]
            for group in RW_GROUPS:
                for s_, i in enumerate(group):
                    t0, n = TILES[i]
                    if s_ and group[0]:
                        pe.wait_ge(S("rw_tile"), group[0])
                        pe.wait_ge(S("rw_state"), group[0] + 1)
                    if s_ and not group[0]:
                        pe.wait_ge(S("rw_rows_out"), len(TILES))
                    for b, m, sig in ((0, nbt, "rw_prods"), (2, kht, "rw_prods2")):
                        for h in range(4):
                            j, f = h // 2, h % 2
                            lo, hi = 64 * f, 64 * f + 64
                            last = pe.matmul(ps_buf[0:n, 4 * s_ + b + f, j * 2 * n:(j + 1) * 2 * n], m[lo:hi, j, t0:t0 + n],
                                             KR[lo:hi, j, 2 * t0:2 * t0 + 2 * n], start=True, stop=True)
                        last.then_inc(S(sig), 1)
                for s_, i in enumerate(group):
                    n = TILES[i][1]
                    pe.wait_ge(S("rw_D1"), i + 1)
                    for q in range(4):
                        last = pe.transpose(ps_buf[0:n, 4 * s_, q * n:q * n + n], Dt[s_][0:n, q * n:q * n + n], ident[0:n, 0:n])
                    last.then_inc(S("rw_D1T"), 1)
                n, L = TILES[group[0]][1], levels(group[0])
                for k in range(1, L):
                    for s_ in range(len(group)):
                        rounds[s_] += 1
                        pe.wait_ge(S(f"rw_level_{s_}"), rounds[s_])
                        for q in range(4):
                            last = pe.matmul(ps_buf[0:n, 4 * s_, q * n:q * n + n], M1[s_][0:n, q, 0:n],
                                             Dm[s_][0:n, q * n:q * n + n], start=True, stop=True)
                        last.then_inc(S(f"rw_Y_{s_}"), 1)
                    for s_ in range(len(group)):
                        pe.wait_ge(S(f"rw_Y_out_{s_}"), rounds[s_])
                        for b, l_, r_ in ((1, Dt, Yb), (2, Yb, Dt)):
                            if b == 2 or k < L - 1:
                                for q in range(4):
                                    c = slice(q * n, q * n + n)
                                    last = pe.matmul(ps_buf[0:n, 4 * s_ + b, c], l_[s_][0:n, c], r_[s_][0:n, c],
                                                     start=True, stop=True)
                        last.then_inc(S(f"rw_DD_{s_}"), 1)
                for s_, i in enumerate(group):
                    rw_tile_pe(i, s_)

        def rw_tile_pe(i, s_):
            pe = nc.tensor
            t0, n = TILES[i]
            pe.wait_ge(S("rw_inv"), i + 1)
            if i < 4:
                pe.wait_ge(S("rw_state"), i + 1)
            else:
                pe.wait_ge(S("rw_state_in"), 16)
            for j in range(2):
                o = ps_buf[0:n, 3, P * j:P * j + P]
                if i < 4:
                    pe.matmul(o, kr(j, i, 0, n), S0[:, P * j:P * j + P], start=True, stop=False)
                else:
                    pe.wait_ge(S("rw_kmask"), j + 1)
                    for b in range(NB):
                        last = pe.matmul(o, kmask[:, b, :], S0s[:, j, b, :], start=b == 0, stop=False)
                    last.then_inc(S("rw_kmask_used"), 1)
                for f in range(2):
                    c = P * j + 64 * f
                    last = pe.matmul(ps_buf[0:n, 3, c:c + 64], M2[s_][0:n, 2 * f + j, 0:n], TK[0:n, i, 512 + c:512 + c + 64],
                                     start=False, stop=f == 1)
            last.then_inc(S("rw_X"), 1)
            pe.wait_ge(S("rw_inv"), i + 1 if s_ or i == 4 else i + 2)
            if i:
                pe.wait_ge(S("rw_tile"), i)
            for j in range(2):
                o = ps_buf[0:n, 4 + j, 0:P]
                if i < 4:
                    pe.matmul(o, kr(j, i, 1, n), S0[:, P * j:P * j + P], start=True, stop=False)
                else:
                    pe.wait_ge(S("rw_rmask"), j + 1)
                    for b in range(NB):
                        last = pe.matmul(o, rmask[:, b, :], S0s[:, j, b, :], start=b == 0, stop=False)
                    last.then_inc(S("rw_rmask_used"), 1)
                for f in range(2):
                    c = P * j + 64 * f
                    pe.matmul(ps_buf[0:n, 4 + j, 64 * f:64 * f + 64], M2[s_][0:n, 2 * f + j, n:2 * n],
                              TK[0:n, i, 512 + c:512 + c + 64], start=False, stop=False)
                if i < 4:
                    pe.matmul(ps_buf[:, 6 + j, 0:P], TK[0:n, i, 256 + P * j:256 + P * j + P],
                              TK[0:n, i, 512 + P * j:512 + P * j + P], start=True, stop=False)
            pe.wait_ge(S("rw_X_out"), i + 1)
            for h in range(4):
                q = (h % 2) * 2 + h // 2
                last = pe.matmul(ps_buf[0:n, 3, 256 + 64 * h:256 + 64 * h + 64], Dt[s_][0:n, q * n:q * n + n],
                                 XU[0:n, 0, 64 * h:64 * h + 64], start=True, stop=True)
            last.then_inc(S("rw_U"), 1)
            pe.wait_ge(S("rw_U_out"), i + 1)
            if i < 4:
                for j in range(2):
                    last = pe.matmul(ps_buf[:, 6 + j, 0:P], TK[0:n, i, P * j:P * j + P],
                                     XU[0:n, 1, P * j:P * j + P], start=False, stop=True)
                last.then_inc(S("rw_state_add"), 1)
            for j in range(2):
                for f in range(2):
                    c = P * j + 64 * f
                    last = pe.matmul(ps_buf[0:n, 4 + j, 64 * f:64 * f + 64], M1[s_][0:n, 2 * f + j, n:2 * n], XU[0:n, 1, c:c + 64],
                                     start=False, stop=f == 1)
            last.then_inc(S("rw_y"), 1)
            if i == 4:
                for j in range(2):
                    pe.wait_ge(S("rw_umask"), j + 1)
                    for g in range(2):
                        o = ps_buf[:, 2 * j + g, 0:512]
                        pe.matmul(o, TK[0:n, i, P * j:P * j + P], umask[0:n, 4 * g:4 * g + 4, :], start=True, stop=False)
                        last = pe.matmul(o, TK[0:n, i, 256 + P * j:256 + P * j + P], vmask[0:n, 4 * g:4 * g + 4, :],
                                         start=False, stop=True)
                    last.then_inc(S("rw_add"), 1)

        def rw_act(a):
            for i, (t0, n) in enumerate(TILES):
                nc.scalar.wait_ge(S("rw_y"), i + 1)
                a(nc.scalar.copy(HB[0:n, 1, i, :].rearrange("p (j c) -> p j c", j=2), ps_buf[0:n, 4:6, 0:P]), S("rw_tile"))

        def rw_dve(v):
            ve = nc.vector
            v(ve.memset(S0, 0.0), S("rw_state"))
            rounds = [0, 0]
            for group in RW_GROUPS:
                n, L = TILES[group[0]][1], levels(group[0])
                mask = tb("rwp" if n == P else "rws", n)[:, 0:2 * n].unsqueeze(1).to_broadcast([n, 2, 2 * n])

                def lev(k):
                    return tb("lev", n)[:, P * k:P * k + n].unsqueeze(1).to_broadcast([n, 4, n])

                def q4(b):
                    return b[0:n, 0:4 * n].rearrange("p (q c) -> p q c", q=4)

                def masked(M, s_, b):
                    for f in range(2):
                        v(ve.tensor_tensor(M[s_][0:n, 2 * f:2 * f + 2, 0:2 * n],
                                           ps_buf[0:n, 4 * s_ + b + f, 0:4 * n].rearrange("p (j c) -> p j c", j=2), mask, ALU.mult))

                for s_, i in enumerate(group):
                    ve.wait_ge(S("rw_prods"), i + 1)
                    masked(M1, s_, 0)
                    v(ve.tensor_tensor(q4(Dt[s_]), M1[s_][0:n, :, 0:n], lev(0), ALU.mult))
                    v(ve.tensor_tensor(q4(Dt[s_]), q4(Dt[s_]), ident[0:n, 0:n].unsqueeze(1).to_broadcast([n, 4, n]), ALU.add),
                      S("rw_D1"))
                for s_, i in enumerate(group):
                    ve.wait_ge(S("rw_D1T"), i + 1)
                    v(ve.tensor_copy(Dm[s_][0:n, 0:4 * n], ps_buf[0:n, 4 * s_, 0:4 * n]), S(f"rw_level_{s_}"))
                    ve.wait_ge(S("rw_prods2"), i + 1)
                    masked(M2, s_, 2)

                def keep(s_):
                    rounds[s_] += 1
                    ve.wait_ge(S(f"rw_Y_{s_}"), rounds[s_])
                    v(ve.tensor_tensor(q4(Yb[s_]), q4(ps_buf[:, 4 * s_, :]), lev(k), ALU.mult), S(f"rw_Y_out_{s_}"))

                def grow(b, D, s_, *sig):
                    v(ve.tensor_tensor(D[s_][0:n, 0:4 * n], D[s_][0:n, 0:4 * n], ps_buf[0:n, 4 * s_ + b, 0:4 * n], ALU.add), *sig)

                pair = len(group) == 2
                for k in range(1, L):
                    keep(0)
                    if pair:
                        if k > 1:
                            grow(2, Dt, 1)
                        keep(1)
                    ve.wait_ge(S("rw_DD_0"), rounds[0])
                    if k < L - 1:
                        grow(1, Dm, 0, S("rw_level_0"))
                    grow(2, Dt, 0)
                    if pair:
                        ve.wait_ge(S("rw_DD_1"), rounds[1])
                        if k < L - 1:
                            grow(1, Dm, 1, S("rw_level_1"))
                ve.sem_inc(S("rw_inv"), 1)
                if pair:
                    grow(2, Dt, 1, S("rw_inv"))
                for i in group:
                    rw_tile_dve(v, i)

        def rw_tile_dve(v, i):
            ve = nc.vector
            t0, n = TILES[i]

            def spread(dst, j, which, sig):
                v(ve.tensor_tensor(dst, kr(j, 4, which, 64).unsqueeze(1).to_broadcast([P, NB, 64]),
                                   tb("segbt").rearrange("p (b t) -> p b t", b=NB), ALU.mult), S(sig))

            if i == 4:
                spread(kmask, 0, 0, "rw_kmask")
                spread(rmask, 0, 1, "rw_rmask")
                ve.wait_ge(S("rw_kmask_used"), 1)
                spread(kmask, 1, 0, "rw_kmask")
            ve.wait_ge(S("rw_X"), i + 1)
            v(ve.tensor_copy(XU[0:n, 0, :], ps_buf[0:n, 3, 0:256]), S("rw_X_out"))
            if i == 4:
                ve.wait_ge(S("rw_rmask_used"), 1)
                spread(rmask, 1, 1, "rw_rmask")
            ve.wait_ge(S("rw_U"), i + 1)
            v(ve.tensor_copy(XU[0:n, 1, :], ps_buf[0:n, 3, 256:512]), S("rw_U_out"))
            if i < 4:
                ve.wait_ge(S("rw_state_add"), i + 1)
                v(ve.tensor_tensor(S0.rearrange("p (j c) -> p j c", j=2), S0.rearrange("p (j c) -> p j c", j=2),
                                   ps_buf[:, 6:8, 0:P], ALU.add))
                for j in range(2):
                    w = S0[:, P * j:P * j + P]
                    v(ve.scalar_tensor_tensor(w, w, ups[:, j, i:i + 1], tb("onesbd"), ALU.mult, ALU.mult),
                      *([S("rw_state")] if j else []))
            else:
                ve.wait_ge(S("rw_y"), 5)
            if i == 4:
                for j in range(2):
                    if j:
                        ve.wait_ge(S("rw_add"), 1)
                    for m, src in ((umask, XU[0:64, 1, P * j:P * j + P]), (vmask, TK[0:64, 4, 512 + P * j:512 + P * j + P])):
                        v(ve.tensor_tensor(m[0:64], src.unsqueeze(1).to_broadcast([64, NB, P]),
                                           tb("segsb", 64).unsqueeze(2).to_broadcast([64, NB, P]), ALU.mult))
                    ve.sem_inc(S("rw_umask"), 1)
                ve.wait_ge(S("rw_tile"), len(TILES))
                head_norm_var(v, 1)
                head_norm_scale(v, 1)
                ve.wait_ge(S("rw_add"), 2)
                for j in range(2):
                    for g in range(2):
                        w = S0s[:, j, 4 * g:4 * g + 4, :]
                        v(ve.tensor_tensor(w, w, ps_buf[:, 2 * j + g, 0:512].rearrange("p (b c) -> p b c", b=4), ALU.add))
                    v(ve.tensor_tensor(S0s[:, j], S0s[:, j], prod[:, j, 4:12].unsqueeze(2).to_broadcast([P, NB, P]), ALU.mult))
                ve.sem_inc(S("rw_final"), 1)

        def head_norm_var(v, m):
            ve = nc.vector
            hb = h_buf[:, 1280 * m:1280 * m + 1280].rearrange("p (g d) -> p g d", d=HD)
            mean, var = n64[:, 20 * m:20 * m + 20], n64b[:, 20 * m:20 * m + 20]
            v(ve.tensor_reduce(mean, hb, AX.X, ALU.add))
            v(ve.tensor_scalar(mean, mean, 1.0 / HD, None, ALU.mult))
            v(ve.tensor_tensor(hb, hb, mean.unsqueeze(2).to_broadcast([P, 20, HD]), ALU.subtract))
            v(ve.tensor_tensor(hsq, hb, hb, ALU.mult))
            v(ve.tensor_reduce(var, hsq, AX.X, ALU.add))
            v(ve.tensor_scalar(var, var, 1.0 / HD, 64e-5 if m else 1e-6, ALU.mult, ALU.add), S("hn_var"))

        def head_norm_scale(v, m):
            ve = nc.vector
            hb = h_buf[:, 1280 * m:1280 * m + 1280].rearrange("p (g d) -> p g d", d=HD)
            var = n64b[:, 20 * m:20 * m + 20]
            ve.wait_ge(S("hn_root"), m + 1)
            v(ve.reciprocal(var, var))
            v(ve.tensor_tensor(hb, hb, var.unsqueeze(2).to_broadcast([P, 20, HD]), ALU.mult), S("hn_done"))

        def hn_dve(v):
            ve = nc.vector
            for m in range(2):
                for j in range(2):
                    ve.wait_ge(S("hn_T"), 2 * m + j + 1)
                    for a0, b0 in ((0, SEQ), (SEQ, T)):
                        b = bank(2 * (2 * (1 - m) + j) + (a0 > 0), b0 - a0)
                        o = hmix[:, 2 * m + j, a0:b0]
                        if m == 0:
                            v(ve.scalar_tensor_tensor(o, b, V("mlw", j), cols[:, CO + j, a0:b0], ALU.mult, ALU.mult))
                        else:
                            v(ve.tensor_scalar(o, b, V("lnw", j), V("lnb", j), ALU.mult, ALU.add))
                            v(ve.tensor_tensor(o, o, rcumx[:, j, a0:b0], ALU.add))
                            v(ve.tensor_tensor(o, o, rg[:, j, a0:b0], ALU.mult))

        def hn_act(a, m):
            nc.scalar.wait_ge(S("hn_var"), m + 1)
            var = n64b[:, 20 * m:20 * m + 20]
            a(nc.scalar.activation(var, var, ACT.Sqrt), S("hn_root"))

        def hn_pe():
            pe = nc.tensor
            for m in range(2):
                pe.wait_ge(S("hn_done"), m + 1)
                pe.wait_ge(S("rw_final") if m else S("rw_tile"), 1 if m else len(TILES))
                for j in range(2):
                    for i, (t0, n) in enumerate(TILES):
                        b = 2 * (2 * (1 - m) + j)
                        o = ps_buf[:, b, t0:t0 + n] if i < 4 else ps_buf[:, b + 1, 0:n]
                        last = pe.transpose(o, HB[0:n, m, i, P * j:P * j + P], ident[0:n, 0:n])
                    last.then_inc(S("hn_T"), 1)

        ROPED = [(CNQ, 0), (CNQ + 1, 1), (CNQ + 2, 2), (CNQ + 3, 3), (CSK, None), (CWK, None)]

        def cmp_pe():
            pe = nc.tensor
            for r_, (c, _) in enumerate(ROPED):
                if r_ >= 2:
                    pe.wait_ge(S("rope_out"), r_ - 1)
                b = 2 * (r_ % 2)
                wide(b, tb("rot"), cols[:, c, :]).then_inc(S("rope_rot"), 1)
            pe.wait_ge(S("rope_out"), 6)
            for w, c in enumerate((CSV, CWV)):
                for i, (t0, n) in enumerate(TILES):
                    o = ps_buf[0:n, 2 * w, i * P:i * P + P] if i < 4 else ps_buf[0:n, 2 * w + 1, 0:P]
                    last = pe.transpose(o, cols[:, c, t0:t0 + n], ident)
            last.then_inc(S("at_vrows"), 1)
            pe.wait_ge(S("at_gspread"), 4)
            for q in range(2):
                last = pe.matmul(ps_buf[:, 4, 24 * q:24 * q + 24], rtmp2[64:88, P * q:P * q + P], ident[64:88, 64:88], start=True, stop=True)
            last.then_inc(S("at_gates"), 1)
            pe.wait_ge(S("at_vrows_out"), 1)
            pe.wait_ge(S("cmp_in"), 2)
            pe.wait_ge(S("kpages_in"), 16 * NB * PAGES)
            pe.wait_ge(S("cw1_in"), 16)
            for j in range(2):
                if j:
                    pe.wait_ge(S("at_rows_out"), 1)
                for g in range(2):
                    for half in range(2):
                        for p_ in range(8):
                            last = pe.matmul(bank(4 * j + 2 * g + half, 9 * 32 + 8), cw1[:, j, 8 * half + p_, :],
                                             ckb[:, :, j, g, p_::8], start=p_ == 0, stop=p_ == 7)
                    last.then_inc(S("cmp_hid"), 1)
            pe.wait_ge(S("cmp_silu"), 4)
            pe.wait_ge(S("cw2_in"), 16)
            for g in range(2):
                pe.matmul(ps_buf[64 * g:64 * g + 64, g, 0:9 * CMP], cw2[:, 0, :], hid[:, g, :], start=True, stop=True)
                for s_ in range(8):
                    pe.matmul(ps_buf[0:CMP, 2 + g, 64 * s_:64 * s_ + 64], hid[:, 2 + g, CMP * s_:CMP * s_ + CMP],
                              cw2[:, 1, :], start=True, stop=True)
                for h in range(4):
                    last = pe.matmul(ps_buf[32 * h:32 * h + CMP, 4 + g, 0:64], hid[:, 2 + g, CMP * 8:CMP * 9],
                                     cw2[:, 1, :], start=True, stop=True)
            last.then_inc(S("cmp_kv"), 1)

        def cmp_act(a):
            ac = nc.scalar
            a(ac.activation(cols[64:88, CGATE, :], cols[64:88, CGATE, :], ACT.Sigmoid))
            for i in range(4):
                a(ac.copy(rtmp2[64:88, 0:256].rearrange("p (b i t) -> p b i t", i=4, t=TS)[:, :, i, :],
                          cols[64:88, CGATE, SEQ:T].rearrange("p (b t) -> p b t", t=TS)), S("at_gspread"))
            ac.wait_ge(S("at_vrows"), 1)
            for w, dst in enumerate((svt, wvt)):
                a(ac.copy(dst[:, 0:4, :], bank(2 * w).rearrange("p (i c) -> p i c", i=4)))
                a(ac.copy(dst[0:64, 4, :], ps_buf[0:64, 2 * w + 1, 0:P]))
            ac.sem_inc(S("at_vrows_out"), 1)
            for w, src in ((0, None), (1, qrot)):
                for i in range(4):
                    s_ = cols[:, CNQ + i, SEQ:T] if src is None else qrot[:, i, SEQ:T]
                    dst = qrs[:, w, :].rearrange("p (b i t) -> p b i t", i=4, t=TS)[:, :, i, :]
                    a(ac.copy(dst, s_.rearrange("p (b t) -> p b t", t=TS)))
            for u in range(4):
                ac.wait_ge(S("cmp_sum"), u + 1)
                a(ac.activation(hid[:, u, :], hid[:, u, :], ACT.Silu, bias=posb[:, u:u + 1]), S("cmp_silu"))

        def cmp_dve(v):
            ve = nc.vector
            for r_, (c, q) in enumerate(ROPED):
                ve.wait_ge(S("rope_rot"), r_ + 1)
                b = 2 * (r_ % 2)
                dst = cols[:, c, :] if q is None else qrot[:, q, :]
                v(ve.tensor_tensor(halves(rtmp), two(b), halves(tb("sin")), ALU.mult))
                v(ve.tensor_tensor(dst, cols[:, c, :], tb("cos"), ALU.mult))
                v(ve.tensor_tensor(dst, dst, rtmp, ALU.add), S("rope_out"))
            v(ve.memset(cvbd, 0.0))
            v(ve.memset(ckb[:, 9 * PAGES, :, :, :], 0.0))
            for g in range(2):
                v(ve.tensor_copy(ckb[:, 9 * PAGES, :, g, 0:16],
                                 vec[:, VEC["cpos"]:VEC["cpos"] + 32].rearrange("p (j t) -> p j t", j=2)))
            v(ve.memset(ckT[:, 9 * CMP:], 0.0))
            for j in range(2):
                for g in range(2):
                    for parity in range(2):
                        v(ve.tensor_copy(ckb[64 * parity:64 * parity + 64, 8 * PAGES:9 * PAGES, j, g, :],
                                         cols[64 * g:64 * g + 64, CCK + j, parity:SEQ:2].rearrange("p (c t) -> p c t", t=HD)))
                ve.sem_inc(S("cmp_in"), 1)
            ve.wait_ge(S("at_gates"), 1)
            for q in range(2):
                v(ve.tensor_tensor(sg24, ps_buf[:, 4, 24 * q:24 * q + 24], tb("rowi"), ALU.mult))
                v(ve.tensor_reduce(sgate[:, q, :, :], sg24.rearrange("p (g i k) -> p g k i", g=2, i=4), AX.X, ALU.add),
                  *([S("at_rows_out")] if q else []))
            for u in range(4):
                ve.wait_ge(S("cmp_hid"), u + 1)
                h = hid[:, u, :].rearrange("p (s c) -> p s c", c=CMP)
                v(ve.tensor_copy(posb[:, u:u + 1], ps_buf[:, 2 * u, 288:289]))
                v(ve.tensor_tensor(posb[:, u:u + 1], posb[:, u:u + 1], ps_buf[:, 2 * u + 1, 289:290], ALU.add))
                both = [bank(2 * u + half, 9 * 32).rearrange("p (s c) -> p s c", c=32) for half in range(2)]
                v(ve.tensor_copy(h, both[0][:, :, 0:CMP]))
                v(ve.tensor_tensor(h, h, both[1][:, :, 1:32], ALU.add), S("cmp_sum"))
            ve.wait_ge(S("cmp_kv"), 1)
            for g in range(2):
                v(ve.tensor_copy(ckT[64 * g:64 * g + 64, 0:9 * CMP], ps_buf[64 * g:64 * g + 64, g, 0:9 * CMP]))
                v(ve.tensor_copy(cvt[0:CMP, :, g, :], ps_buf[0:CMP, 2 + g, :].rearrange("p (s d) -> p s d", s=8)))
                for h in range(4):
                    r_ = slice(32 * h, 32 * h + CMP)
                    v(ve.tensor_copy(cvbd[r_, g, 64 * h:64 * h + 64], ps_buf[r_, 4 + g, 0:64]))

        UNITS = [(i, br, g, h) for i in range(PT) for br in range(3) for h in range(4) for g in range(2)
                 if br or h == 0]
        NU = len(UNITS)

        def width(u):
            i, br, g, h = UNITS[u]
            return P * (i + 1) if br else 4 * 32

        def ends_branch(u):
            return 0 <= u < NU and (u == NU - 1 or UNITS[u + 1][1] != UNITS[u][1])

        def at_pe():
            pe = nc.tensor

            def scores(u):
                i, br, g, h = UNITS[u]
                t0, n, b = P * i, width(u), u % 3
                if u >= 3:
                    pe.wait_ge(S("at_exp"), u - 2)
                if br == 0:
                    lo = 64 * g
                    for h in range(4):
                        last = pe.matmul(ps_buf[:, b, 32 * h:32 * h + 32], cols[lo:lo + 64, CNQ + h, t0:t0 + P],
                                         ckT[lo:lo + 64, 8 * CMP:9 * CMP + 1], start=True, stop=True)
                else:
                    lo = 64 * g
                    pe.matmul(bank(b, n), qrot[lo:lo + 64, h, t0:t0 + P], cols[lo:lo + 64, CSK if br == 1 else CWK, 0:n],
                              start=True, stop=False)
                    last = pe.matmul(ps_buf[:, b, n - P:n], ident, tb("tri"), start=False, stop=True)
                last.then_inc(S("at_scores"), 1)

            def turn(u):
                i, br, g, h = UNITS[u]
                if br == 0:
                    pe.wait_ge(S("at_seen"), 2 * i + g + 1)
                else:
                    pe.wait_ge(S("at_exp"), u + 1)
                if u >= 2:
                    pe.wait_ge(S("at_PT"), u - 1)
                for c in range(width(u) // P):
                    last = pe.transpose(ps_buf[:, 3 + u % 2, P * c:P * c + P], Sb[:, u % 3, P * c:P * c + P], ident)
                last.then_inc(S("at_T"), 1)

            def weigh(u):
                i, br, g, h = UNITS[u]
                pe.wait_ge(S("at_PT"), u + 1)
                if i and (g, h) == (0, 0):
                    pe.wait_ge(S("at_acc"), 3 * (i - 1) + br + 1)
                if br == 0:
                    last = pe.matmul(ps_buf[:, 5, 256 * g:256 * g + 256], PTb[:, u % 3, 0, :], cvbd[:, g, :],
                                     start=True, stop=True)
                else:
                    o = ps_buf[:, 5 + br, 64 * (4 * g + h):64 * (4 * g + h) + 64]
                    for c in range(i + 1):
                        last = pe.matmul(o, PTb[:, u % 3, c, :], (svt if br == 1 else wvt)[:, c, 64 * g:64 * g + 64],
                                         start=c == 0, stop=c == i)
                last.then_inc(S("at_pv"), 1)

            for s_ in range(NU + 3):
                if s_ < NU:
                    scores(s_)
                if 2 <= s_ < NU + 2:
                    turn(s_ - 2)
                if s_ >= 3:
                    weigh(s_ - 3)
            pe.wait_ge(S("at_acc"), 3 * PT)
            for h in range(4):
                for i in range(PT):
                    last = pe.transpose(ps_buf[:, h, P * i:P * i + P], oacc[:, i, h, :], ident)
                last.then_inc(S("at_oT"), 1)

        def at_act(a):
            ac = nc.scalar
            for s_ in range(1, NU + 2):
                if s_ <= NU:
                    u = s_ - 1
                    i, br, g, h = UNITS[u]
                    ac.wait_ge(S("at_max"), u + 1)
                    if br == 0:
                        w = Sb[:, u % 3, 0:width(u)]
                        a(ac.activation(w, w, ACT.Exp), S("at_exp"))
                    else:
                        if u >= 3:
                            ac.wait_ge(S("at_T"), u - 2)
                        m = 4 * g + h
                        a(ac.activation(Sb[:, u % 3, 0:width(u)], bank(u % 3, width(u)), ACT.Exp,
                                        bias=stat[:, u % 4, 1:2], accum_out=sums[:, i % 2, br, m:m + 1]), S("at_exp"))
                if s_ >= 2:
                    u = s_ - 2
                    n = width(u)
                    ac.wait_ge(S("at_T"), u + 1)
                    if u >= 3:
                        ac.wait_ge(S("at_pv"), u - 2)
                    a(ac.copy(PTb[:, u % 3, 0:n // P, :], bank(3 + u % 2, n).rearrange("p (c t) -> p c t", t=P)),
                      S("at_PT"))

        def at_dve(v):
            ve = nc.vector
            for s_ in range(NU + 5):
                if s_ < NU:
                    u = s_
                    i, br, g, h = UNITS[u]
                    ve.wait_ge(S("at_scores"), u + 1)
                    if br:
                        v(ve.tensor_reduce(stat[:, u % 4, 1:2], bank(u % 3, width(u)), AX.X, ALU.max, negate=True), S("at_max"))
                    else:
                        w = Sb[:, u % 3, 0:P].rearrange("p (m k) -> p m k", m=4)
                        if u >= 3:
                            ve.wait_ge(S("at_T"), u - 2)
                        v(ve.tensor_tensor(w, bank(u % 3, P).rearrange("p (m k) -> p m k", m=4),
                                           tb("cma")[:, 32 * i:32 * i + 32].unsqueeze(1).to_broadcast([P, 4, 32]), ALU.add))
                        v(ve.tensor_reduce(cmax[:, 0:4], w, AX.X, ALU.max))
                        v(ve.tensor_tensor(w, w, cmax[:, 0:4].unsqueeze(2).to_broadcast([P, 4, 32]), ALU.subtract), S("at_max"))
                if 1 <= s_ <= NU and UNITS[s_ - 1][1] == 0:
                    u = s_ - 1
                    i, _, g, _ = UNITS[u]
                    total = sums[:, i % 2, 0, 4 * g:4 * g + 4]
                    w = Sb[:, u % 3, 0:P].rearrange("p (m k) -> p m k", m=4)
                    ve.wait_ge(S("at_exp"), u + 1)
                    v(ve.tensor_tensor(w, w, tb("cm1")[:, 32 * i:32 * i + 32].unsqueeze(1).to_broadcast([P, 4, 32]), ALU.mult),
                      S("at_seen"))
                    v(ve.tensor_reduce(total, w, AX.X, ALU.add))
                    v(ve.tensor_scalar(total, total, 1e-30, None, ALU.max))
                if ends_branch(s_ - 4):
                    u = s_ - 4
                    i, br, g, h = UNITS[u]
                    ve.wait_ge(S("at_exp"), u + 1)
                    v(ve.reciprocal(wbr, sums[:, i % 2, br, :]))
                    v(ve.tensor_tensor(wbr, wbr, gates[:, i, br::3], ALU.mult))
                    ve.wait_ge(S("at_pv"), u + 1)
                    for g in range(2):
                        dst = oacc[:, i, :, 64 * g:64 * g + 64]
                        src = ps_buf[:, 5 + br, 256 * g:256 * g + 256].rearrange("p (h d) -> p h d", h=4)
                        f_ = wbr[:, 4 * g:4 * g + 4].unsqueeze(2).to_broadcast([P, 4, HD])
                        if br == 0:
                            v(ve.tensor_tensor(dst, src, f_, ALU.mult))
                        else:
                            v(ve.tensor_tensor(obr[:, 4 * g:4 * g + 4, :], src, f_, ALU.mult))
                            v(ve.tensor_tensor(dst, dst, obr[:, 4 * g:4 * g + 4, :], ALU.add))
                    ve.sem_inc(S("at_acc"), 1)
            for h in range(4):
                ve.wait_ge(S("at_oT"), h + 1)
                v(ve.tensor_copy(hmix[:, 4 + h, 0:SEQ], bank(h)))

        CU = [(g, q) for g in range(2) for q in range(2)]
        SU = [(br, q, g) for br in (2, 1) for q in range(2) for g in range(2)]
        NSU = len(SU)

        def sa_pe():
            pe = nc.tensor

            def scores(u):
                br, q, g = SU[u]
                lo = 64 * g
                kq, kc = (skq, CSK) if br == 1 else (wkq, CWK)
                if br == 2 and g == 0:
                    pe.wait_ge(S(f"qwin_{q}"), 16 * 8)
                if br == 1 and g == 0:
                    for b in range(4):
                        pe.wait_ge(S(f"qpages_{4 * q + b}"), 16 * 2 * PAGES)
                if u >= 2:
                    pe.wait_ge(S("sa_max"), u - 1)
                k = 2 * (u % 2)
                for b in range(4):
                    pe.matmul(ps_buf[32 * b:32 * b + 32, k, 0:512], qrs[lo:lo + 64, 1, 128 * q + 32 * b:128 * q + 32 * b + 32],
                              kq[q][lo:lo + 64, b, :], start=True, stop=True)
                pe.matmul(bank(k + 1, 64), qrs[lo:lo + 64, 1, 128 * q:128 * q + 128], cols[lo:lo + 64, kc, SEQ:T],
                          start=True, stop=True).then_inc(S("sa_scores"), 1)

            def turn(u):
                pe.wait_ge(S("sa_exp"), u + 1)
                if u:
                    pe.wait_ge(S("sa_PT"), u)
                for c in range(4):
                    pe.transpose(ps_buf[:, 4, P * c:P * c + P], Sb[:, u % 3, P * c:P * c + P], ident)
                pe.transpose(ps_buf[0:64, 5, 0:P], Sb[:, u % 3, SEQ:T], ident).then_inc(S("sa_T"), 1)

            def weigh(u):
                br, q, g = SU[u]
                lo = 64 * g
                vq, vt = (svq, svt) if br == 1 else (wvq, wvt)
                pe.wait_ge(S("sa_PT"), u + 1)
                if u >= 2:
                    pe.wait_ge(S("sa_acc"), u - 1)
                for b in range(4):
                    o = ps_buf[32 * b:32 * b + 32, 6 + u % 2, 0:64]
                    r_ = slice(32 * b, 32 * b + 32)
                    for c in range(4):
                        pe.matmul(o, PTb[:, u % 3, c, r_], vq[q][:, b, c, lo:lo + 64], start=c == 0, stop=False)
                    last = pe.matmul(o, PTb[0:64, u % 3, 4, r_], vt[0:64, 4, lo:lo + 64], start=False, stop=True)
                last.then_inc(S("sa_pv"), 1)

            for g, q in CU:
                lo = 64 * g
                for b in range(4):
                    last = pe.matmul(ps_buf[32 * b:32 * b + 32, 6 + g, 32 * q:32 * q + CMP],
                                     qrs[lo:lo + 64, 0, 128 * q + 32 * b:128 * q + 32 * b + 32],
                                     ckT[lo:lo + 64, CMP * (4 * q + b):CMP * (4 * q + b) + CMP], start=True, stop=True)
            last.then_inc(S("sa_c_scores"), 1)
            scores(0)
            pe.wait_ge(S("sa_c_p"), 1)
            for m in range(4):
                last = pe.transpose(ps_buf[0:CMP, 6, P * m:P * m + P], Cb[:, m, 0:CMP], ident)
            last.then_inc(S("sa_c_T"), 1)
            scores(1)
            pe.wait_ge(S("sa_c_PT"), 1)
            for m, (g, q) in enumerate(CU):
                for b in range(4):
                    pe.matmul(ps_buf[32 * b:32 * b + 32, 7, 64 * m:64 * m + 64], PTc[0:CMP, m, 32 * b:32 * b + 32],
                              cvt[0:CMP, 4 * q + b, g, :], start=True, stop=True)
                last = pe.matmul(ps_buf[:, 6, 16 * m:16 * m + 9], PTc[0:CMP, m, :], tb("ov"), start=True, stop=True)
            last.then_inc(S("sa_c_pv"), 1)
            turn(0)
            pe.wait_ge(S("sa_c_imp"), 1)
            pe.matmul(ps_buf[:, 6, 64:100], tb("same"), impz.rearrange("p m k -> p (m k)"), start=True, stop=True)\
                .then_inc(S("sa_c_same"), 1)
            for s_ in range(2, NSU + 2):
                if s_ < NSU:
                    scores(s_)
                if s_ < NSU + 1:
                    turn(s_ - 1)
                if s_ == 2:
                    pe.wait_ge(S("sa_c_done"), 1)
                weigh(s_ - 2)
            pe.wait_ge(S("sa_acc"), NSU)
            for q in range(2):
                last = pe.transpose(ps_buf[:, 6, P * q:P * q + P], osamp[:, q, :], ident)
            last.then_inc(S("sa_oT"), 1)

        def sa_act(a):
            ac = nc.scalar

            def turned(u):
                ac.wait_ge(S("sa_T"), u + 1)
                if u >= 3:
                    ac.wait_ge(S("sa_pv"), u - 2)
                a(ac.copy(PTb[:, u % 3, 0:4, :], bank(4).rearrange("p (c t) -> p c t", t=P)))
                a(ac.copy(PTb[0:64, u % 3, 4, :], ps_buf[0:64, 5, 0:P]), S("sa_PT"))

            def exponentials(u):
                ac.wait_ge(S("sa_max"), u + 1)
                a(ac.activation(Sb[:, u % 3, :], Sb[:, u % 3, :], ACT.Exp, bias=stat[:, u % 4, 1:2],
                                accum_out=stat[:, u % 4, 2:3]), S("sa_exp"))

            ac.wait_ge(S("sa_c_max"), 1)
            a(ac.activation(Cb[:, :, 0:CMP], Cb[:, :, 0:CMP], ACT.Exp), S("sa_c_exp"))
            exponentials(0)
            ac.wait_ge(S("sa_c_T"), 1)
            a(ac.copy(PTc[0:CMP, :, :], ps_buf[0:CMP, 6, :].rearrange("p (m t) -> p m t", m=4)), S("sa_c_PT"))
            for s_ in range(1, NSU + 1):
                if s_ < NSU:
                    exponentials(s_)
                turned(s_ - 1)

        def sa_dve(v):
            ve = nc.vector

            def masked(u):
                br, q, g = SU[u]
                w, k = Sb[:, u % 3, :], 2 * (u % 2)
                ve.wait_ge(S("sa_scores"), u + 1)
                if u >= 3:
                    ve.wait_ge(S("sa_T"), u - 2)
                if br == 1:
                    v(ve.tensor_tensor(w[:, 0:512].rearrange("p (s k) -> p s k", s=8),
                                       bank(k).rearrange("p (s k) -> p s k", s=8),
                                       kbias[:, 2 * g + q, :].unsqueeze(2).to_broadcast([P, 8, HD]), ALU.add))
                else:
                    v(ve.tensor_copy(w[:, 0:512], bank(k)))
                    v(ve.tensor_tensor(w[:, 0:8], w[:, 0:8], tb("winm"), ALU.add))
                v(ve.tensor_tensor(w[:, SEQ:T], bank(k + 1, 64), tb("newm")[:, 64 * q:64 * q + 64], ALU.add))
                v(ve.tensor_reduce(stat[:, u % 4, 1:2], w, AX.X, ALU.max, negate=True), S("sa_max"))

            def add(u):
                br, q, g = SU[u]
                st = stat[:, u % 4, :]
                ve.wait_ge(S("sa_exp"), u + 1)
                v(ve.reciprocal(st[:, 3:4], st[:, 2:3]))
                v(ve.tensor_tensor(st[:, 3:4], st[:, 3:4], sgate[:, q, g, br:br + 1], ALU.mult))
                ve.wait_ge(S("sa_pv"), u + 1)
                o = osamp[:, q, 64 * g:64 * g + 64]
                v(ve.scalar_tensor_tensor(o, bank(6 + u % 2, 64), st[:, 3:4], o, ALU.mult, ALU.add), S("sa_acc"))

            def rows4(w, n):
                return w.unsqueeze(2).to_broadcast([P, 4, n])

            rank = tb("rank")[:, 0:6].unsqueeze(1).to_broadcast([P, 4, 6])
            v(ve.memset(kbias, 0.0))
            ve.wait_ge(S("sa_c_scores"), 1)
            raw_c = [ps_buf[:, 6 + g, 0:64].rearrange("p (q k) -> p q k", q=2)[:, :, 0:CMP] for g in range(2)]
            for g in range(2):
                v(ve.tensor_reduce(cmax[:, 2 * g:2 * g + 2], raw_c[g], AX.X, ALU.max))
            for g in range(2):
                v(ve.tensor_tensor(Cb[:, 2 * g:2 * g + 2, 0:CMP], raw_c[g],
                                   cmax[:, 2 * g:2 * g + 2].unsqueeze(2).to_broadcast([P, 2, CMP]), ALU.subtract),
                  *([S("sa_c_max")] if g else []))
            masked(0)
            ve.wait_ge(S("sa_c_exp"), 1)
            v(ve.tensor_reduce(csum, Cb[:, :, 0:CMP], AX.X, ALU.add))
            v(ve.reciprocal(csum, csum))
            v(ve.tensor_tensor(Cb[:, :, 0:CMP], Cb[:, :, 0:CMP], rows4(csum, CMP), ALU.mult), S("sa_c_p"))
            masked(1)
            ve.wait_ge(S("sa_c_pv"), 1)
            v(ve.tensor_copy(impz, ps_buf[:, 6, 0:64].rearrange("p (m k) -> p m k", m=4)[:, :, 0:9]), S("sa_c_imp"))
            for g in range(2):
                v(ve.tensor_tensor(osamp[:, :, 64 * g:64 * g + 64],
                                   ps_buf[:, 7, 128 * g:128 * g + 128].rearrange("p (q d) -> p q d", q=2),
                                   sgate[:, :, g, 0].unsqueeze(2).to_broadcast([P, 2, HD]), ALU.mult))
            ve.wait_ge(S("sa_c_same"), 1)
            v(ve.tensor_copy(imps, ps_buf[:, 6, 64:100].rearrange("p (m k) -> p m k", m=4)), S("sa_c_done"))
            v(ve.tensor_reduce(ifew, imps[:, :, 1:7], AX.X, ALU.min))
            v(ve.tensor_tensor(iw, imps[:, :, 1:7], rows4(ifew, 6), ALU.is_equal))
            v(ve.tensor_tensor(iw, iw, rank, ALU.mult))
            v(ve.tensor_reduce(ifew, iw, AX.X, ALU.max))
            v(ve.tensor_tensor(iw, rank, rows4(ifew, 6), ALU.is_equal))
            v(ve.tensor_scalar(kbias[:, :, 1:7], iw, NEG, None, ALU.mult))
            for s_ in range(2, NSU + 2):
                if s_ < NSU:
                    masked(s_)
                add(s_ - 2)
            ve.wait_ge(S("sa_oT"), 1)
            for q in range(2):
                for h in range(4):
                    v(ve.tensor_copy(hmix[:, 4 + h, SEQ + 32 * q:SEQ + 32 * q + 32].rearrange("p (b t) -> p b t", t=TS),
                                     ps_buf[:, 6, P * q:P * q + P].rearrange("p (b i t) -> p b i t", i=4, t=TS)[:, :, h, :]))

        def wo_raw(slot):
            return cols_buf[:, slot * KD * P:(slot + 1) * KD * P]

        def wo_sp(l):
            for c in range(KD):
                if c >= 2:
                    sync.wait_ge(S("wo_split"), c - 1)
                sync.dma_start(wo_raw(c % 2), A["w_out"][l * KD + c].rearrange("p k c -> p (k c)"))\
                    .then_inc(S(f"w_out_{c % 2}"), 16)

        def wo_act(a):
            for k in range(KD):
                if k >= 2:
                    nc.scalar.wait_ge(S("wo_x"), k - 1)
                a(nc.scalar.copy(split_v[:, k % 2, :], hmix[:, k, :]), S("wo_x_hi"))
                if k < 3:
                    wo_hi(a, k)
            for c in range(3, KD):
                wo_hi(a, c)

        def wo_hi(a, c):
            nc.scalar.wait_ge(S(f"w_out_{c % 2}"), 16 * (c // 2 + 1))
            if c >= 3:
                nc.scalar.wait_ge(S("wo_done"), c - 2)
            split_hi(a, c % 3, wo_raw(c % 2), KD, UNIT, S("wo_hi"))

        def wo_pool(g):
            for c in range(KD):
                nc.gpsimd.wait_ge(S("wo_hi"), c + 1)
                split_lo(g, c % 3, wo_raw(c % 2), KD, UNIT, S("wo_split"))

        def wo_pe():
            for c in range(KD):
                nc.tensor.wait_ge(S("wo_split"), c + 1)
                if c >= 3:
                    nc.tensor.wait_ge(S("wo_out"), c - 2)
                b = 2 * (c % 3)
                unit_products(c % 3, KD, UNIT, XH, XL, b,
                              (lambda k: nc.tensor.wait_ge(S("wo_x"), k + 1)) if c == 0 else None)\
                    .then_inc(S("wo_done"), 1)

        def wo_dve(v):
            ve = nc.vector
            for k in range(KD):
                ve.wait_ge(S("wo_x_hi"), k + 1)
                v(ve.tensor_tensor(XL[:, k, :], hmix[:, k, :], split_v[:, k % 2, :].bitcast(F32), ALU.subtract))
                v(ve.tensor_copy(XH[:, k, :], split_v[:, k % 2, :].bitcast(F32)), S("wo_x"))
            for c in range(KD):
                ve.wait_ge(S("wo_done"), c + 1)
                b = 2 * (c % 3)
                v(ve.tensor_tensor(halves(x[:, c, :]), halves(x[:, c, :]), two(b), ALU.add), S("wo_out"))

        def rt_pe():
            pe = nc.tensor
            for k in range(KD):
                pe.wait_ge(S("ffn_norm_scaled"), k + 1)
                wide(0, router[:, k, :], ntmp[:, k % 3, :], k == 0, k == KD - 1, rows=8).then_inc(S("rt_rows"), 1)
            pe.wait_ge(S("rt_rows_out"), 1)
            for i, (t0, n) in enumerate(TILES):
                last = pe.transpose(ps_buf[0:n, 2, 8 * i:8 * i + 8], lgT[0:8, t0:t0 + n], ident[0:8, 0:8])
            last.then_inc(S("rt_logits"), 1)
            pe.wait_ge(S("rt_comb"), 1)
            for i, (t0, n) in enumerate(TILES):
                o = ps_buf[0:8, 3, t0:t0 + n] if i < 4 else ps_buf[0:8, 4, 0:n]
                last = pe.transpose(o, lw[0:n, 0, 8 * i:8 * i + 8], ident[0:n, 0:n])
            last.then_inc(S("rt_T"), 1)

        def rt_act(a):
            ac = nc.scalar
            ac.wait_ge(S("rt_diff"), 1)
            a(ac.activation(lw[:, 7, 0:5], lw[:, 7, 0:5], ACT.Exp), S("rt_exp"))

        def rt_dve(v):
            ve = nc.vector

            def g5(k):
                return lw[:, k, :].rearrange("p (i e) -> p i e", i=5)

            def spread5(ap):
                return ap.unsqueeze(2).to_broadcast([P, 5, 8])

            v(ve.memset(lg, 0.0))
            ve.wait_ge(S("rt_rows"), KD)
            v(ve.tensor_copy(halves(lgT[0:8, :]), two(0, 8)), S("rt_rows_out"))
            ve.wait_ge(S("rt_logits"), 1)
            v(ve.tensor_copy(lg[:, 0:4, :], ps_buf[:, 2, 0:32].rearrange("p (i e) -> p i e", i=4)))
            v(ve.tensor_copy(lg[0:64, 4, :], ps_buf[0:64, 2, 32:40]))
            m = [lw[:, 5, 0:5], lw[:, 6, 0:5]]
            rank = tb("rrank").rearrange("p (i e) -> p i e", i=5)
            for k in range(2):
                v(ve.tensor_reduce(m[k], lg, AX.X, ALU.max))
                v(ve.tensor_tensor(g5(4), lg, spread5(m[k]), ALU.is_equal))
                v(ve.tensor_tensor(g5(4), g5(4), rank, ALU.mult))
                v(ve.tensor_reduce(lw[:, 7, 8:13], g5(4), AX.X, ALU.max))
                v(ve.tensor_tensor(g5(1 + k), rank, spread5(lw[:, 7, 8:13]), ALU.is_equal))
                if k == 0:
                    v(ve.scalar_tensor_tensor(lg, g5(1), NEG, lg, ALU.mult, ALU.add))
            v(ve.tensor_tensor(lw[:, 7, 0:5], m[1], m[0], ALU.subtract), S("rt_diff"))
            ve.wait_ge(S("rt_exp"), 1)
            v(ve.tensor_scalar(lw[:, 5, 0:5], lw[:, 7, 0:5], 1.0, None, ALU.add))
            v(ve.reciprocal(lw[:, 5, 0:5], lw[:, 5, 0:5]))
            v(ve.tensor_tensor(lw[:, 6, 0:5], lw[:, 7, 0:5], lw[:, 5, 0:5], ALU.mult))
            v(ve.tensor_tensor(g5(1), g5(1), spread5(lw[:, 5, 0:5]), ALU.mult))
            v(ve.tensor_tensor(g5(2), g5(2), spread5(lw[:, 6, 0:5]), ALU.mult))
            v(ve.tensor_tensor(lw[:, 0, :], lw[:, 1, :], lw[:, 2, :], ALU.add))
            v(ve.tensor_scalar(lw[:, 0, :], lw[:, 0, :], -1.0, V("flag"), ALU.add, ALU.mult))
            v(ve.tensor_scalar(lw[:, 0, :], lw[:, 0, :], 1.0, None, ALU.add), S("rt_comb"))
            ve.wait_ge(S("rt_T"), 1)
            v(ve.tensor_copy(cT[0:8, 0:SEQ], ps_buf[0:8, 3, :]))
            v(ve.tensor_copy(cT[0:8, SEQ:T], ps_buf[0:8, 4, 0:64]), S("rt_cT"))

        NUN = 2 * FC + KD
        FREE_RAW, FREE_PARTS, FREE_OUT = 3, 3, 2

        def nk_of(u):
            return KD if u < 2 * FC else FC

        def ex_sp(e):
            for u in range(NUN):
                sync.wait_ge(S("g_raw_free"), e * NUN + (u + 1))
                src = A["w13"][e * 2 * FC + u] if u < 2 * FC else A["w2"][e * KD + (u - 2 * FC)]
                sync.dma_start(raw(u % 3, nk_of(u)), src).then_inc(S(f"g_raw_in_{u % 3}"), 16)

        def ex_act(a, e):
            ac = nc.scalar
            for u in range(NUN):
                ac.wait_ge(S(f"g_raw_in_{u % 3}"), e * (16 * NUN // 3) + 16 * (u // 3 + 1))
                ac.wait_ge(S("g_unit_done"), e * NUN + (u + 1))
                split_hi(a, u % 3, raw(u % 3, nk_of(u)), nk_of(u), UNIT, S("g_w_hi"))
                if u >= 3 and u % 2 == 1 and (u - 3) // 2 < FC:
                    f = (u - 3) // 2
                    ac.wait_ge(S("g_unit_done"), e * NUN + (2 * f + 1 + FREE_PARTS))
                    ac.wait_ge(S("g_h"), e * FC + (f + 1))
                    a(ac.activation(halves(sg[:, f % 2, :]), two(0), ACT.Silu), S("g_silu"))

        def ex_pool(g, e):
            for u in range(NUN):
                nc.gpsimd.wait_ge(S("g_w_hi"), e * NUN + (u + 1))
                split_lo(g, u % 3, raw(u % 3, nk_of(u)), nk_of(u), UNIT, S("g_w_ready"), S("g_raw_free"))

        def ex_pe(e):
            pe = nc.tensor
            for u in range(NUN):
                pe.wait_ge(S("g_w_ready"), e * NUN + (u + 1))
                if u < 2 * FC:
                    f, w = u // 2, u % 2
                    if f and w == 0:
                        pe.wait_ge(S("g_silu"), e * FC + f)
                    if f and w == 1:
                        pe.wait_ge(S("g_h"), e * FC + (f + 2))
                    unit_products(u % 3, KD, UNIT, XH, XL, 2 * w)\
                        .then_inc(S("g_unit_done"), 1)
                    if u == 1:
                        pe.wait_ge(S("g_gate_row"), e + 1)
                        wide(6, tb("ones")[0:8, :], cTe[0:8, :]).then_inc(S("g_gate"), 1)
                else:
                    c = u - 2 * FC
                    pe.wait_ge(S("g_out_free"), e * KD + (c + 1))
                    before = None
                    if c == 0:
                        def before(k):
                            if k in (0, FC - 1):
                                pe.wait_ge(S("g_h"), e * FC + ((FC - 1 if k == 0 else FC) + 2))
                    unit_products(u % 3, FC, UNIT, HH, HL, 4 + 2 * (c % 2),
                                  before).then_inc(S("g_unit_done"), 1)

        def ex_dve(v, e, le):
            ve = nc.vector
            v(ve.tensor_scalar(cTe[0:8, :], cT[0:8, :], ident[0:8, bass.ds(le, 1)], None, ALU.mult), S("g_gate_row"))
            ve.wait_ge(S("g_gate"), e + 1)
            v(ve.tensor_copy(halves(combE), two(6)))
            for f in range(FC):
                ve.wait_ge(S("g_silu"), e * FC + (f + 1))
                ve.wait_ge(S("g_unit_done"), e * NUN + (2 * f + 2 + FREE_PARTS))
                h = htmp[:, f % 2, :]
                v(ve.tensor_tensor(halves(h), halves(sg[:, f % 2, :]), two(2), ALU.mult))
                v(ve.tensor_tensor(h, h, combE, ALU.mult))
                v(ve.tensor_copy(HH[:, f, :], h))
                v(ve.tensor_tensor(HL[:, f, :], h, HH[:, f, :].bitcast(F32), ALU.subtract), S("g_h"))
            for c in range(KD):
                ve.wait_ge(S("g_unit_done"), e * NUN + (2 * FC + c + 1 + FREE_PARTS))
                v(ve.tensor_tensor(halves(x[:, c, :]), halves(x[:, c, :]), two(4 + 2 * (c % 2)), ALU.add),
                  S("g_out_free"))

        def iteration_ends(eng, tag):
            eng.drain().then_inc(S(tag + "_arrived"), 1)
            eng.wait_ge(S(tag + "_go"), 1)
            eng.sem_inc(S(tag + "_left"), 1)

        def clear(tag):
            sync.wait_ge(S(tag + "_arrived"), 4)
            S(tag + "_go"), S(tag + "_left")
            if tag == "half":
                own = {s.num for s in shared}
            else:
                own = {s.num for n, s in sems.items() if not n.startswith(("g_", "layer_", "half_"))}
            own = sorted(own | {S(tag + "_arrived").num})
            k = 0
            while k < len(own):
                m = k
                while m + 1 < len(own) and own[m + 1] == own[m] + 1:
                    m += 1
                sync.sem_clear(range(own[k], own[m] + 1))
                k = m + 1
            sync.sem_inc(S(tag + "_go"), 1)
            sync.wait_ge(S(tag + "_left"), 4)
            for n in ("_go", "_left"):
                sync.sem_clear(S(tag + n))

        POOL = 40

        def load_pages(eng, l, samples):
            eng.wait_ge(S("g_in"), 80)
            for b in samples:
                for c in range(PAGES):
                    k = b * PAGES + c
                    pg = eng.value_load(page_buf[0:1, k:k + 1], min_val=0, max_val=POOL - 1)
                    eng.dma_start(ckb[:, k].rearrange("p j g t -> p (j g t)"), A["pages_c"][l * POOL + pg])\
                        .then_inc(S("kpages_in"), 16)

        def experts(l):
            return 2 + 6 * l

        with nc.Block() as block:
            @block.vector
            def _(eng):
                v = Chain(eng, S("dve_chain"))
                eng.wait_ge(S("g_in"), 80)
                v0 = Chain(eng, S("g_chain_dve"))
                v0(nc.vector.memset(gates, 0.0))
                eng.sem_inc(S("g_out_free"), FREE_OUT)
                eng.sem_inc(S("g_h"), 2)
                with eng.Fori(0, DEPTH) as l:
                    eng.wait_ge(S("small_in"), 48)
                    norm_dve(v, "mix_norm", rstd, lambda k: V("nmix", k))
                    proj_dve(v)
                    meet(eng, "dve")
                    rows_dve(v)
                    ml_dve(v)
                    meet(eng, "dve")
                    rwprep_dve(v)
                    rw_dve(v)
                    hn_dve(v)
                    eng.wait_ge(S("rw_outs"), 32)
                    iteration_ends(eng, "half")
                    cmp_dve(v)
                    meet(eng, "dve")
                    at_dve(v)
                    meet(eng, "dve")
                    sa_dve(v)
                    meet(eng, "dve")
                    wo_dve(v)
                    norm_dve(v, "ffn_norm", rstd, lambda k: V("nffn", k))
                    rt_dve(v)
                    eng.wait_ge(S("kv_outs"), 32)
                    meet(eng, "dve")
                    with eng.Fori(0, experts(l)) as e:
                        ex_dve(Chain(eng, S("g_chain_ex_dve")), e + 2 * l, e)
                        eng.sem_clear(S("g_chain_ex_dve"))
                    iteration_ends(eng, "layer")
                norm_dve(v0, "g_fin", rstd, lambda k: nfin[:, k:k + 1], final=True)

            @block.scalar
            def _(eng):
                a = Chain(eng, S("act_chain"))
                eng.wait_ge(S("g_in"), 80)
                with eng.Fori(0, DEPTH) as l:
                    eng.wait_ge(S("small_in"), 48)
                    norm_act(a, "mix_norm", rstd)
                    proj_act(a)
                    meet(eng, "act")
                    rows_act(a)
                    ml_act(a)
                    meet(eng, "act")
                    rwprep_act(a)
                    rw_act(a)
                    hn_act(a, 1)
                    iteration_ends(eng, "half")
                    cmp_act(a)
                    meet(eng, "act")
                    at_act(a)
                    meet(eng, "act")
                    sa_act(a)
                    meet(eng, "act")
                    wo_act(a)
                    norm_act(a, "ffn_norm", rstd)
                    rt_act(a)
                    eng.drain().then_inc(S("phase_ended"), 1)
                    with eng.Fori(0, experts(l)) as e:
                        ex_act(Chain(eng, S("g_chain_ex_act")), e + 2 * l)
                        eng.sem_clear(S("g_chain_ex_act"))
                    iteration_ends(eng, "layer")
                norm_act(Chain(eng, S("g_chain_act")), "g_fin", rstd, final=True)

            @block.gpsimd
            def _(eng):
                g = Chain(eng, S("pool_chain"))
                with eng.Fori(0, DEPTH) as l:
                    proj_pool(g)
                    ml_pool(g)
                    iteration_ends(eng, "half")
                    wo_pool(g)
                    with eng.Fori(0, experts(l)) as e:
                        ex_pool(Chain(eng, S("g_chain_ex_pool")), e + 2 * l)
                        eng.sem_clear(S("g_chain_ex_pool"))
                    iteration_ends(eng, "layer")

            @block.tensor
            def _(eng):
                eng.wait_ge(S("g_in"), 80)
                eng.sem_inc(S("g_unit_done"), FREE_PARTS)
                with eng.Fori(0, DEPTH) as l:
                    norm_pe("mix_norm")
                    proj_pe()
                    meet(eng, "pe")
                    ml_pe()
                    meet(eng, "pe")
                    rwprep_pe()
                    rw_pe()
                    hn_pe()
                    iteration_ends(eng, "half")
                    cmp_pe()
                    meet(eng, "pe")
                    at_pe()
                    meet(eng, "pe")
                    sa_pe()
                    meet(eng, "pe")
                    wo_pe()
                    norm_pe("ffn_norm")
                    rt_pe()
                    meet(eng, "pe")
                    with eng.Fori(0, experts(l)) as e:
                        ex_pe(e + 2 * l)
                    iteration_ends(eng, "layer")
                norm_pe("g_fin")

            @block.sync
            def _(eng):
                eng.dma_start(tab[:, :], A["tab"]).then_inc(S("g_in"), 16)
                eng.dma_start(x, A["x"]).then_inc(S("g_in"), 16)
                eng.dma_start(router, A["router"]).then_inc(S("g_in"), 16)
                eng.dma_start(nfin, A["nfin"]).then_inc(S("g_in"), 16)
                eng.dma_start(page_buf[:, :], A["pages"]).then_inc(S("g_in"), 16)
                eng.sem_inc(S("g_raw_free"), FREE_RAW)
                with eng.Fori(0, DEPTH) as l:
                    one = lambda name, k: A[name][bass.ds(k, 1)]

                    def ld(dst, name, k, sem):
                        eng.dma_start(dst, A[name][k]).then_inc(S(sem), 16)

                    ld(vec, "vec", l, "small_in")
                    ld(state_in, "state", l, "small_in")
                    ld(m0_in[0:4, :], "m0", l, "small_in")
                    proj_sp(l)
                    eng.wait_ge(S("conv_done"), 4)
                    eng.wait_ge(S("shift_done"), 8)
                    eng.dma_start(A["o_state"][l], state_out).then_inc(S("state_outs"), 16)
                    eng.wait_ge(S("phase_ended"), 3)
                    for j in range(2):
                        ld(Cs[:, j].rearrange("p b c -> p (b c)"), "C0", 2 * l + j, "ml_state_in")
                    eng.wait_ge(S("m_out"), 1)
                    eng.dma_start(A["o_m"][l], seg12[0:4, 2, :]).then_inc(S("ml_outs"), 16)
                    eng.wait_ge(S("ml_final"), 1)
                    eng.dma_start(A["o_Cp"][l], Cp).then_inc(S("ml_outs"), 16)
                    eng.dma_start(A["o_Cs"][l], Cs.rearrange("p j b c -> p (j b c)")).then_inc(S("ml_outs"), 16)
                    eng.wait_ge(S("phase_ended"), 6)
                    ld(rw_w[:, 0, :], "lora", 2 * l, "rw_w_in")
                    ld(rw_w[:, 1, :], "lora", 2 * l + 1, "rw_w_in")
                    ld(S0s.rearrange("p j b c -> p (j b c)"), "S0", l, "rw_state_in")
                    eng.wait_ge(S("rw_ready"), 1)
                    load_pages(eng, l, range(EARLY_B))
                    for b in range(NB):
                        eng.dma_start(A["o_win"][l * NB + b, 0:PAST - TS], A["win"][l * NB + b, TS:PAST])\
                            .then_inc(S("g_win"), 16)
                    eng.wait_ge(S("rw_final"), 1)
                    eng.dma_start(A["o_Sp"][l], S0).then_inc(S("rw_outs"), 16)
                    eng.dma_start(A["o_Ss"][l], S0s.rearrange("p j b c -> p (j b c)")).then_inc(S("rw_outs"), 16)
                    clear("half")
                    ld(cw1.rearrange("p j a b -> p (j a b)"), "cw1", l, "cw1_in")
                    ld(cw2.rearrange("p a b -> p (a b)"), "cw2", l, "cw2_in")
                    load_pages(eng, l, range(EARLY_B, NB))
                    eng.wait_ge(S("rope_out"), 6)
                    eng.dma_start(A["o_kv"][l], cols[:, CCK:CCK + 4, :]).then_inc(S("kv_outs"), 16)
                    eng.dma_start(A["o_wkv"][l], cols[:, CWK:CWK + 2, :]).then_inc(S("kv_outs"), 16)
                    eng.wait_ge(S("phase_ended"), 9)
                    for q in range(2):
                        for b in range(4):
                            w = l * NB + 4 * q + b
                            eng.dma_start(wkq[q][:, b, :], A["win_k"][w]).then_inc(S(f"qwin_{q}"), 16)
                            eng.dma_start(wvq[q][:, b, :, :], A["win_v"][w].rearrange("(c p) d -> p c d", p=P))\
                                .then_inc(S(f"qwin_{q}"), 16)
                    for b in range(NB):
                        for c in range(PAGES):
                            k = b * PAGES + c
                            pg = eng.value_load(page_buf[0:1, k:k + 1], min_val=0, max_val=POOL - 1)
                            eng.dma_start(skq[b // 4][:, b % 4, P * c:P * c + P],
                                          A["pages_k"][l * POOL + pg]).then_inc(S(f"qpages_{b}"), 16)
                            eng.dma_start(svq[b // 4][:, b % 4, c, :],
                                          A["pages_v"][l * POOL + pg]).then_inc(S(f"qpages_{b}"), 16)
                    eng.wait_ge(S("phase_ended"), 12)
                    wo_sp(l)
                    eng.wait_ge(S("state_outs"), 16)
                    eng.wait_ge(S("wo_split"), KD)
                    with eng.Fori(0, experts(l)) as e:
                        ex_sp(e + 2 * l)
                    clear("layer")
                for k in range(KD):
                    eng.wait_ge(S("g_fin_done"), k + 1)
                    eng.dma_start(A["o_y"][k], hmix[:, k, :]).then_inc(S("g_y"), 16)
                eng.wait_ge(S("g_y"), 16 * KD)
                eng.wait_ge(S("g_win"), 16 * DEPTH * NB)

            return len(sems)


ML_W, RW0, NS0 = 1032, 1032, 2056


def in_columns():
    r = lambda a, n: list(range(a, a + n))
    out = r(0, 1024)
    out += r(RW0, 256) + r(RW0 + 256, 64) + r(RW0 + 832, 64) + r(RW0 + 320, 256) + r(RW0 + 576, 256) + r(RW0 + 896, 128)
    for i in range(4):
        out += r(NS0 + 64 * i, 64) + r(NS0 + 64 * (4 + i), 64)
    out += r(NS0 + 512, 768)
    gate = [-1] * P
    gate[0:4], gate[32:36], gate[64:88] = r(1024, 4), r(1028, 4), r(NS0 + 1280, 24)
    return out + gate


def rw_columns():
    r = lambda a, n: list(range(a, a + n))
    return r(0, 256) + r(256, 64) + r(832, 64) + r(320, 256) + r(576, 256) + r(896, 128)


def pack(inp):
    n = {k: np.asarray(v) for k, v in inp.items()}
    f = np.float32
    o = {}
    at, w = table_layout()
    t = np.zeros((P, w), f)
    for k, a in tables().items():
        c, r, m = at[k]
        t[0:r, c:c + m] = a
    o["tab"] = t
    x = np.concatenate([n["x_prompt"].reshape(SEQ, D), n["x_sample"].reshape(NS_TOK, D)], 0)

    def chans(a):
        return np.moveaxis(a.reshape(a.shape[:-1] + (-1, P)), -1, -2)

    o["x"] = x.T.reshape(KD, P, T).transpose(1, 0, 2)
    cols = np.array(in_columns())
    w_in = np.where(cols >= 0, n["w_in"][:, :, np.maximum(cols, 0)], f(0))
    o["w_in"] = w_in.reshape(DEPTH, KD, P, NCH, P).transpose(0, 3, 2, 1, 4).reshape(DEPTH * NCH, P, KD, P)
    mix = list(range(512))
    for i in range(4):
        mix += list(range(512 + 64 * i, 576 + 64 * i)) + list(range(512 + 64 * (4 + i), 576 + 64 * (4 + i)))
    o["w_out"] = n["w_out"][:, mix].reshape(DEPTH, KD, P, KD, P).transpose(0, 3, 2, 1, 4).reshape(DEPTH * KD, P, KD, P)
    E1 = FC * P

    def up(dense, moe):
        d = dense[0].reshape(D, 2, E1).transpose(1, 0, 2)
        a = np.concatenate([d, moe[0]], 0)
        return a.reshape(10, KD, P, FC, P).transpose(0, 3, 2, 1, 4)

    o["w13"] = np.stack([up(n["ffn_w1"], n["moe_w1"]), up(n["ffn_w3"], n["moe_w3"])], 2).reshape(20 * FC, P, KD * P)
    w2 = np.concatenate([n["ffn_w2"][0].reshape(2, E1, D), n["moe_w2"][0]], 0)
    o["w2"] = w2.reshape(10, FC, P, KD, P).transpose(0, 3, 2, 1, 4).reshape(10 * KD, P, FC * P)
    o["router"] = n["moe_router"][0].reshape(KD, P, 8).transpose(1, 0, 2)
    o["nfin"] = chans(n["norm_final_w"])
    v = np.zeros((DEPTH, P, NV), f)

    def put(name, a):
        v[:, :, VEC[name]:VEC[name] + a.shape[-1]] = a

    rwc = rw_columns()
    put("nmix", chans(n["norm_mix_w"]))
    put("nffn", chans(n["norm_ffn_w"]))
    put("convw", chans(n["ml_conv_w"]).transpose(0, 2, 1, 3).reshape(DEPTH, P, 16))
    put("convb", chans(n["ml_conv_b"]))
    put("mu", chans(n["rw_mu"][:, rwc]))
    for name, key in (("w0", "rw_w0"), ("a0", "rw_a0"), ("kk", "rw_k_k"), ("ka", "rw_k_a"), ("lnw", "rw_ln_w"),
                      ("lnb", "rw_ln_b"), ("mlw", "ml_norm_w")):
        put(name, chans(n[key]))
    put("rk", chans(n["rw_r_k"].reshape(DEPTH, 256)))
    v[:, 0:4, VEC["gb"]] = n["ml_b_i"]
    v[:, 32:36, VEC["gb"]] = n["ml_b_f"]
    v[1, :, VEC["flag"]] = 1.0
    pos = n["nsa_cmp_pos"].reshape(DEPTH, 2, CLEN // 2, 2, HD).transpose(0, 3, 4, 1, 2)
    put("cpos", pos.reshape(DEPTH, P, CLEN))
    o["vec"] = v
    conv = n["state_mlstm_conv"].transpose(0, 3, 1, 2).reshape(DEPTH, 4, P, NB * 3).transpose(0, 2, 1, 3)
    shift = n["state_rwkv_shift"][:, :, rwc].transpose(0, 2, 1).reshape(DEPTH, 8, P, NB).transpose(0, 2, 1, 3)
    o["state"] = np.concatenate([conv.reshape(DEPTH, P, -1), shift.reshape(DEPTH, P, -1)], 2)
    o["m0"] = n["state_mlstm_m"].transpose(0, 2, 1)
    C = np.zeros((DEPTH, 2, P, NB, 130), f)
    S_ = np.zeros((DEPTH, P, 2, NB, P), f)
    for h in range(4):
        j, q = h // 2, h % 2
        C[:, j, 64 * q:64 * q + 64, :, 65 * q:65 * q + 64] = n["state_mlstm_C"][:, :, h].transpose(0, 3, 1, 2)
        C[:, j, 64 * q:64 * q + 64, :, 65 * q + 64] = n["state_mlstm_n"][:, :, h].transpose(0, 2, 1)
        S_[:, 64 * q:64 * q + 64, j, :, 64 * q:64 * q + 64] = n["state_rwkv_S"][:, :, h].transpose(0, 3, 1, 2)
    o["C0"] = C.reshape(DEPTH * 2, P, NB * 130)
    o["S0"] = S_.reshape(DEPTH, P, 2 * NB * P)
    lora = np.zeros((DEPTH, 2, P, 256), f)
    lora[:, 0, 0:64], lora[:, 0, 64:128], lora[:, 1] = n["rw_w2"], n["rw_a2"], n["rw_g2"]
    o["lora"] = lora.reshape(DEPTH * 2, P, 256)
    cw1 = n["nsa_cmp_w1"].reshape(DEPTH, 2, CLEN // 2, 2, HD, P).transpose(0, 3, 4, 1, 2, 5)
    o["cw1"] = cw1.reshape(DEPTH, P, CLEN * P)
    o["cw2"] = n["nsa_cmp_w2"].transpose(0, 2, 1, 3).reshape(DEPTH, P, P)
    kv = n["cache_nsa_kv"].reshape(DEPTH * 40, P, 4, P)
    c = kv[:, :, 0:2].reshape(DEPTH * 40, P // 2, 2, 2, 2, HD)
    o["pages_c"] = c.transpose(0, 2, 5, 3, 4, 1).reshape(DEPTH * 40, P, 4 * HD)
    o["pages_k"] = kv[:, :, 2].transpose(0, 2, 1)
    o["pages_v"] = kv[:, :, 3]
    win = n["cache_win_kv"].reshape(DEPTH, NB, PAST, 2, P)
    o["win"] = win.reshape(DEPTH * NB, PAST, 256)
    o["win_k"] = win[:, :, :, 0].transpose(0, 1, 3, 2).reshape(DEPTH * NB, P, PAST)
    o["win_v"] = win[:, :, :, 1].reshape(DEPTH * NB, PAST, P)
    o["pages"] = n["page_table"].reshape(1, NB * PAGES).astype(np.int32)
    return {k: np.ascontiguousarray(a) for k, a in o.items()}


OUTS = {
    "o_y": (KD, P, T), "o_kv": (DEPTH, P, 4, T), "o_wkv": (DEPTH, P, 2, T), "o_win": (DEPTH * NB, PAST, 256),
    "o_state": (DEPTH, P, OUT_W), "o_m": (DEPTH, 4, 12), "o_Cp": (DEPTH, P, 260), "o_Cs": (DEPTH, P, 2 * NB * 130),
    "o_Sp": (DEPTH, P, 256), "o_Ss": (DEPTH, P, 2 * NB * P),
}


def unpack(r):
    y = r["o_y"].transpose(2, 0, 1).reshape(T, D)
    out = [y[None, 0:SEQ], y[SEQ:].reshape(NB, TS, D)]
    kv = r["o_kv"].transpose(0, 3, 2, 1)
    out += [kv[:, None, 0:SEQ].reshape(DEPTH, 1, SEQ, 4, 2, HD), kv[:, SEQ:].reshape(DEPTH, NB, TS, 4, 2, HD)]
    wkv = r["o_wkv"].transpose(0, 3, 2, 1)
    win = r["o_win"].reshape(DEPTH, NB, PAST, 256).copy()
    win[:, :, PAST - TS:] = wkv[:, SEQ:].reshape(DEPTH, NB, TS, 256)
    out += [wkv[:, None, 0:SEQ].reshape(DEPTH, 1, SEQ, 2, 2, HD), win.reshape(DEPTH, NB, PAST, 2, 2, HD)]
    Cp = r["o_Cp"].reshape(DEPTH, P, 2, 1, 130)
    Cs = r["o_Cs"].reshape(DEPTH, P, 2, NB, 130)
    Sp = r["o_Sp"].reshape(DEPTH, P, 2, 1, P)
    Ss = r["o_Ss"].reshape(DEPTH, P, 2, NB, P)

    def by_head(a, w, n):
        return np.stack([a[:, 64 * (h % 2):64 * (h % 2) + 64, h // 2, :, w * (h % 2):w * (h % 2) + n] for h in range(4)], 1)

    for a in (Cp, Cs):
        c = by_head(a, 65, 65)
        out.append(c[..., 0:64].transpose(0, 3, 1, 4, 2))
    for a in (Cp, Cs):
        out.append(by_head(a, 65, 65)[..., 64].transpose(0, 3, 1, 2))
    m = r["o_m"]
    out += [m[:, :, 3][:, None], m[:, :, 4:12].transpose(0, 2, 1)]
    st = r["o_state"]

    def conv(a, nb):
        return a.reshape(DEPTH, P, 4, nb, 3).transpose(0, 3, 4, 2, 1).reshape(DEPTH, nb, 3, 512)

    out += [conv(st[:, :, OUT_CP:OUT_CS], 1), conv(st[:, :, OUT_CS:OUT_SP], NB)]
    for a in (Sp, Ss):
        out.append(by_head(a, 64, 64).transpose(0, 3, 1, 4, 2))
    back = np.argsort(np.array(rw_columns()))

    def shift(a, nb):
        return a.reshape(DEPTH, P, 8, nb).transpose(0, 3, 2, 1).reshape(DEPTH, nb, D)[:, :, back]

    out += [shift(st[:, :, OUT_SP:OUT_SS], 1), shift(st[:, :, OUT_SS:], NB)]
    return tuple(np.ascontiguousarray(a) for a in out)


def kernel(**inputs):
    import concourse.bacc as _bacc
    from concourse.bass_utils import run_bass_kernel_spmd as _run

    nc = _bacc.Bacc("TRN2", target_bir_lowering=False, num_devices=1, dynamic_dma_scratch_size=2048)
    arrays = pack(inputs)
    A = {}
    for name, a in arrays.items():
        A[name] = nc.dram_tensor("d_" + name, a.shape, mybir.dt.from_np(a.dtype), kind="ExternalInput").ap()
    for name, shape in OUTS.items():
        A[name] = nc.dram_tensor("d_" + name, shape, F32, kind="ExternalOutput").ap()
    build(nc, A)
    r = _run(nc, [{"d_" + k: a for k, a in arrays.items()}], core_ids=[0]).results[0]
    return unpack({k: np.asarray(r["d_" + k]) for k in OUTS})
```
